# Optimizing a Trainium2 kernel written in Bass

```python
import math
import jax, jax.numpy as jnp
from jax import lax
import numpy as np

D_MODEL = 1024
BATCH = 1
SEQ = 512
DEPTH = 2

N_MIX_HEADS = 16
HEAD_DIM = D_MODEL // N_MIX_HEADS
N_HEADS_DIL = 6
DILATED_PAIRS = ((128, 1), (512, 4), (2048, 16))
N_HEADS_DIFF = 4
DIFF_QK_DIM = HEAD_DIM // 2
N_HEADS_SB = 6
D_MIX = (N_HEADS_DIL + N_HEADS_DIFF + N_HEADS_SB) * HEAD_DIM
IN_SIZES = (N_HEADS_DIL * HEAD_DIM,) * 3 + (N_HEADS_DIFF * 2 * DIFF_QK_DIM,) * 2 + (N_HEADS_DIFF * HEAD_DIM,) + (N_HEADS_SB * HEAD_DIM,) * 3
D_IN = sum(IN_SIZES)
D_FF = 2816
Q_BLOCK = 128
NORM_EPS = 1e-6
N_NORMS = 6


def rmsnorm(x, g):
    xf = x.astype(jnp.float32)
    y = xf * lax.rsqrt(jnp.mean(xf * xf, axis=-1, keepdims=True) + NORM_EPS)
    return (y * g.astype(jnp.float32)).astype(x.dtype)

def swiglu(h, w_gate, w_up, w_down):
    return (jax.nn.silu(h @ w_gate) * (h @ w_up)) @ w_down

def alibi_slopes(n):
    return 2.0 ** (-8.0 * jnp.arange(1, n + 1, dtype=jnp.float32) / n)

def to_heads(t, n_heads):
    b, s, _ = t.shape
    return t.reshape(b, s, n_heads, -1).transpose(0, 2, 1, 3)

def from_heads(t):
    b, h, s, dh = t.shape
    return t.transpose(0, 2, 1, 3).reshape(b, s, h * dh)

def query_blocks(t):
    b, h, s, dh = t.shape
    return t.reshape(b, h, s // Q_BLOCK, Q_BLOCK, dh).transpose(2, 0, 1, 3, 4)

def merge_blocks(t):
    nq, b, h, q, dh = t.shape
    return t.transpose(1, 2, 0, 3, 4).reshape(b, h, nq * q, dh)

def dilated_branch(q, k, v, slopes, window, dilation):
    b, h, s, dh = q.shape
    n_back = window // dilation
    chunk = dilation * n_back
    sp = -(-s // chunk) * chunk
    seg = sp // dilation
    nb = seg // n_back

    def split(t):
        t = jnp.pad(t, ((0, 0), (0, 0), (0, sp - s), (0, 0)))
        t = t.reshape(b, h, seg, dilation, dh).transpose(0, 1, 3, 2, 4)
        return t.reshape(b, h, dilation, nb, n_back, dh)

    def with_prev(t):
        prev = jnp.concatenate([jnp.zeros_like(t[:, :, :, :1]), t[:, :, :, :-1]], axis=3)
        return jnp.concatenate([prev, t], axis=4)

    qb = split(q)
    kk = with_prev(split(k))
    vv = with_prev(split(v))
    sc = jnp.einsum('bhrnqd,bhrnkd->bhrnqk', qb, kk, preferred_element_type=jnp.float32)
    qi = jnp.arange(n_back)[:, None]
    ki = jnp.arange(2 * n_back)[None, :]
    dist = n_back + qi - ki
    band = (dist >= 0) & (dist <= n_back)
    first = (jnp.arange(nb) == 0)[:, None, None] & (ki < n_back)[None]
    valid = band[None] & ~first
    sc = sc - slopes[None, :, None, None, None, None] * (dilation * dist).astype(jnp.float32)
    sc = jnp.where(valid, sc, -jnp.inf)
    m = jnp.max(sc, axis=-1, keepdims=True)
    p = jnp.exp(sc - m)
    den = jnp.sum(p, axis=-1)
    o = jnp.einsum('bhrnqk,bhrnkd->bhrnqd', p, vv, preferred_element_type=jnp.float32) / den[..., None]
    lse = m[..., 0] + jnp.log(den)
    o = o.reshape(b, h, dilation, seg, dh).transpose(0, 1, 3, 2, 4).reshape(b, h, sp, dh)[:, :, :s]
    lse = lse.reshape(b, h, dilation, seg).transpose(0, 1, 3, 2).reshape(b, h, sp)[:, :, :s]
    return o, lse

def dilated_attention(q, k, v):
    slopes = alibi_slopes(q.shape[1])
    outs, lses = zip(*[dilated_branch(q, k, v, slopes, w, d) for (w, d) in DILATED_PAIRS])
    wts = jax.nn.softmax(jnp.stack(lses), axis=0)
    return jnp.sum(wts[..., None] * jnp.stack(outs), axis=0)

def differential_attention(q1, q2, k1, k2, v, lam):
    s = q1.shape[2]
    slopes = alibi_slopes(q1.shape[1])
    kpos = jnp.arange(s)
    starts = jnp.arange(s // Q_BLOCK) * Q_BLOCK

    def block(args):
        start, a, c = args
        rel = (start + jnp.arange(Q_BLOCK))[:, None] - kpos[None, :]
        bias = jnp.where(rel >= 0, -slopes[:, None, None] * rel.astype(jnp.float32), -jnp.inf)
        a1 = jax.nn.softmax(jnp.einsum('bhqd,bhkd->bhqk', a, k1, preferred_element_type=jnp.float32) + bias, axis=-1)
        a2 = jax.nn.softmax(jnp.einsum('bhqd,bhkd->bhqk', c, k2, preferred_element_type=jnp.float32) + bias, axis=-1)
        return jnp.einsum('bhqk,bhkd->bhqd', a1 - lam * a2, v, preferred_element_type=jnp.float32)

    return merge_blocks(lax.map(block, (starts, query_blocks(q1), query_blocks(q2))))

def stick_breaking_attention(q, k, v):
    s = q.shape[2]
    kpos = jnp.arange(s)
    starts = jnp.arange(s // Q_BLOCK) * Q_BLOCK

    def block(args):
        start, a = args
        valid = kpos[None, :] < (start + jnp.arange(Q_BLOCK))[:, None]
        z = jnp.einsum('bhqd,bhkd->bhqk', a, k, preferred_element_type=jnp.float32)
        log_fail = jnp.where(valid, jax.nn.log_sigmoid(-z), 0.0)
        after = lax.cumsum(log_fail, axis=3, reverse=True) - log_fail
        wts = jnp.where(valid, jnp.exp(jax.nn.log_sigmoid(z) + after), 0.0)
        return jnp.einsum('bhqk,bhkd->bhqd', wts, v, preferred_element_type=jnp.float32)

    return merge_blocks(lax.map(block, (starts, query_blocks(q))))

def token_mixer(h, w_in, w_out, lam_params, subln_gain, layer):
    proj = h @ w_in
    idx = [int(i) for i in np.cumsum(IN_SIZES)[:-1]]
    qa, ka, va, qb, kb, vb, qc, kc, vc = jnp.split(proj, idx, axis=-1)
    b, s, _ = h.shape
    o_a = dilated_attention(to_heads(qa, N_HEADS_DIL) * (HEAD_DIM ** -0.5), to_heads(ka, N_HEADS_DIL), to_heads(va, N_HEADS_DIL))
    qb = qb.reshape(b, s, N_HEADS_DIFF, 2, DIFF_QK_DIM).transpose(0, 2, 3, 1, 4) * (DIFF_QK_DIM ** -0.5)
    kb = kb.reshape(b, s, N_HEADS_DIFF, 2, DIFF_QK_DIM).transpose(0, 2, 3, 1, 4)
    lam_init = 0.8 - 0.6 * math.exp(-0.3 * layer)
    lam = jnp.exp(jnp.sum(lam_params[0] * lam_params[1])) - jnp.exp(jnp.sum(lam_params[2] * lam_params[3])) + lam_init
    o_b = differential_attention(qb[:, :, 0], qb[:, :, 1], kb[:, :, 0], kb[:, :, 1], to_heads(vb, N_HEADS_DIFF), lam.astype(jnp.float32))
    o_b = rmsnorm(o_b, subln_gain) * (1.0 - lam_init)
    o_c = stick_breaking_attention(to_heads(qc, N_HEADS_SB) * (HEAD_DIM ** -0.5), to_heads(kc, N_HEADS_SB), to_heads(vc, N_HEADS_SB))
    mixed = jnp.concatenate([from_heads(o_a), from_heads(o_b), from_heads(o_c)], axis=-1).astype(h.dtype)
    return mixed @ w_out

def first_inputs(seed: int = 0) -> dict:
    key = jax.random.key(seed)
    ks = jax.random.split(key, 10)
    f32 = jnp.float32
    x = jax.random.normal(ks[0], (BATCH, SEQ, D_MODEL), f32)
    norm_gains = 1.0 + 0.02 * jax.random.normal(ks[1], (DEPTH, N_NORMS, D_MODEL), f32)
    w_ffn_gate = jax.random.normal(ks[2], (DEPTH, 2, D_MODEL, D_FF), f32) * D_MODEL ** -0.5
    w_ffn_up = jax.random.normal(ks[3], (DEPTH, 2, D_MODEL, D_FF), f32) * D_MODEL ** -0.5
    w_ffn_down = jax.random.normal(ks[4], (DEPTH, 2, D_FF, D_MODEL), f32) * D_FF ** -0.5
    w_in = jax.random.normal(ks[5], (DEPTH, D_MODEL, D_IN), f32) * D_MODEL ** -0.5
    w_out = jax.random.normal(ks[6], (DEPTH, D_MIX, D_MODEL), f32) * D_MIX ** -0.5
    diff_lambda = 0.1 * jax.random.normal(ks[7], (DEPTH, 4, DIFF_QK_DIM), f32)
    diff_subln_gain = 1.0 + 0.02 * jax.random.normal(ks[8], (DEPTH, HEAD_DIM), f32)
    return {"x": x, "norm_gains": norm_gains, "w_ffn_gate": w_ffn_gate, "w_ffn_up": w_ffn_up,
            "w_ffn_down": w_ffn_down, "w_in": w_in, "w_out": w_out,
            "diff_lambda": diff_lambda, "diff_subln_gain": diff_subln_gain}

def first_block(x, norm_gains, w_ffn_gate, w_ffn_up, w_ffn_down, w_in, w_out, diff_lambda, diff_subln_gain):
    for layer in range(DEPTH):
        g = norm_gains[layer]
        h = rmsnorm(x, g[0])
        x = x + 0.5 * rmsnorm(swiglu(h, w_ffn_gate[layer, 0], w_ffn_up[layer, 0], w_ffn_down[layer, 0]), g[1])
        h = rmsnorm(x, g[2])
        x = x + rmsnorm(token_mixer(h, w_in[layer], w_out[layer], diff_lambda[layer], diff_subln_gain[layer], layer), g[3])
        h = rmsnorm(x, g[4])
        x = x + 0.5 * rmsnorm(swiglu(h, w_ffn_gate[layer, 1], w_ffn_up[layer, 1], w_ffn_down[layer, 1]), g[5])
    return x


D_MIX_2 = D_MODEL
HG_WIDTH = D_MIX_2 // 2
HG_HEAD_DIM = 128
HG_HEADS = HG_WIDTH // HG_HEAD_DIM
HG_CHUNK = 64
NSA_WIDTH = D_MIX_2 - HG_WIDTH
NSA_HEAD_DIM = 64
NSA_HEADS = NSA_WIDTH // NSA_HEAD_DIM
NSA_KV_GROUPS = 2
NSA_HPG = NSA_HEADS // NSA_KV_GROUPS
CMP_BLOCK = 32
CMP_STRIDE = 16
CMP_HIDDEN = 128
SLC_BLOCK = 64
SLC_TOPK = 16
SLC_LOCAL = 2
WINDOW = 512
Q_BLOCK_2 = 64
N_BUCKETS = 32
MAX_DISTANCE = 128
D_FF_2 = ((8 * D_MODEL // 3 + 255) // 256) * 256
ALPHA = (2.0 * DEPTH) ** 0.25
BETA = (8.0 * DEPTH) ** -0.25
KV_W = NSA_KV_GROUPS * NSA_HEAD_DIM
SPLIT_SIZES = (HG_WIDTH, HG_WIDTH, HG_WIDTH, HG_WIDTH, NSA_WIDTH, KV_W, KV_W, KV_W, KV_W, KV_W, KV_W, 3 * NSA_HEADS)
D_IN_2 = sum(SPLIT_SIZES)
NEG = -1e30
BIG = 1e9


def _split_points():
    pts, acc = [], 0
    for s in SPLIT_SIZES[:-1]:
        acc += s
        pts.append(acc)
    return pts

def layer_norm(x, g, b, eps=1e-5):
    xf = x.astype(jnp.float32)
    mu = jnp.mean(xf, -1, keepdims=True)
    var = jnp.mean(jnp.square(xf - mu), -1, keepdims=True)
    return ((xf - mu) * lax.rsqrt(var + eps) * g + b).astype(x.dtype)

def hgrn2_lower_bounds(lb_param):
    p = jax.nn.softmax(lb_param.astype(jnp.float32), axis=0)
    c = jnp.cumsum(p, axis=0)
    return c - c[0:1]

def hgrn2_mixer(q, f_logit, i, g, lb, gnorm_w):
    B, S, _ = q.shape
    H, Dk, C = HG_HEADS, HG_HEAD_DIM, HG_CHUNK
    N = S // C
    f32 = jnp.float32
    logf = jnp.logaddexp(jnp.log(lb), jnp.log1p(-lb) + jax.nn.log_sigmoid(f_logit.astype(f32)))
    k = -jnp.expm1(logf)

    def to_chunks(t):
        return t.astype(f32).reshape(B, N, C, H, -1).transpose(1, 0, 3, 2, 4)

    qc, kc, vc = to_chunks(q), to_chunks(k), to_chunks(i)
    bc = jnp.cumsum(to_chunks(logf), axis=3)
    causal = jnp.tril(jnp.ones((C, C), bool))

    def step(state, xs):
        qb, kb, vb, bb = xs
        rel = bb[:, :, :, None, :] - bb[:, :, None, :, :]
        decay = jnp.exp(jnp.where(causal[:, :, None], rel, -jnp.inf))
        scores = jnp.einsum('bhtd,bhsd,bhtsd->bhts', qb, kb, decay)
        o_intra = jnp.einsum('bhts,bhsv->bhtv', scores, vb)
        o_inter = jnp.einsum('bhtd,bhdv->bhtv', qb * jnp.exp(bb), state)
        b_last = bb[:, :, -1:, :]
        k_dec = kb * jnp.exp(b_last - bb)
        new_state = state * jnp.exp(b_last[:, :, 0, :, None]) + jnp.einsum('bhsd,bhsv->bhdv', k_dec, vb)
        return new_state, o_intra + o_inter

    s0 = jnp.zeros((B, H, Dk, Dk), f32)
    _, o = lax.scan(step, s0, (qc, kc, vc, bc))
    o = o.transpose(1, 0, 3, 2, 4).reshape(B, S, H, Dk)
    o = o * lax.rsqrt(jnp.mean(o * o, -1, keepdims=True) + 1e-6) * gnorm_w
    o = o.reshape(B, S, HG_WIDTH) * jax.nn.silu(g.astype(f32))
    return o.astype(q.dtype)

def t5_bucket(n):
    n = jnp.maximum(n, 0)
    max_exact = N_BUCKETS // 2
    nf = jnp.maximum(n, 1).astype(jnp.float32)
    large = max_exact + (jnp.log(nf / max_exact) / math.log(MAX_DISTANCE / max_exact)
                         * (N_BUCKETS - max_exact)).astype(jnp.int32)
    large = jnp.minimum(large, N_BUCKETS - 1)
    return jnp.where(n < max_exact, n, large)

def masked_softmax(s, valid):
    s = jnp.where(valid, s, NEG)
    p = jax.nn.softmax(s, axis=-1)
    return jnp.where(valid, p, 0.0)

def nsa_mixer(q, k_cmp, v_cmp, k_slc, v_slc, k_win, v_win, gates,
              cmp_pos_k, cmp_w1_k, cmp_w2_k, cmp_pos_v, cmp_w1_v, cmp_w2_v, rel_bias):
    B, S, _ = q.shape
    G, HPG, Dh = NSA_KV_GROUPS, NSA_HPG, NSA_HEAD_DIM
    f32 = jnp.float32
    scale = Dh ** -0.5
    rb = rel_bias.astype(f32)
    qh = q.astype(f32).reshape(B, S, G, HPG, Dh).transpose(0, 2, 3, 1, 4)
    gh = jax.nn.sigmoid(gates.astype(f32)).reshape(B, S, 3, G, HPG).transpose(0, 3, 4, 1, 2)

    def kv(t):
        return t.astype(f32).reshape(B, S, G, Dh).transpose(0, 2, 1, 3)

    n_cmp = (S - CMP_BLOCK) // CMP_STRIDE + 1

    def compress(t, pos, w1, w2):
        c = kv(t).reshape(B, G, S // CMP_STRIDE, CMP_STRIDE, Dh)
        blocks = jnp.concatenate([c[:, :, :-1], c[:, :, 1:]], axis=3)
        blocks = (blocks + pos).reshape(B, G, n_cmp, CMP_BLOCK * Dh)
        return jax.nn.gelu(blocks @ w1) @ w2

    kc = compress(k_cmp, cmp_pos_k, cmp_w1_k, cmp_w2_k)
    vc = compress(v_cmp, cmp_pos_v, cmp_w1_v, cmp_w2_v)
    cmp_start = jnp.arange(n_cmp) * CMP_STRIDE
    cmp_end = cmp_start + CMP_BLOCK - 1

    n_slc = S // SLC_BLOCK
    n_sel = min(SLC_TOPK, n_slc)
    ks_blocks = kv(k_slc).reshape(B, G, n_slc, SLC_BLOCK, Dh)
    vs_blocks = kv(v_slc).reshape(B, G, n_slc, SLC_BLOCK, Dh)
    slc_start = jnp.arange(n_slc) * SLC_BLOCK
    overlap = jnp.clip(jnp.minimum(cmp_start[:, None] + CMP_BLOCK, slc_start[None, :] + SLC_BLOCK)
                       - jnp.maximum(cmp_start[:, None], slc_start[None, :]), 0, None)
    agg = overlap.astype(f32) / CMP_STRIDE

    kw_pad = jnp.pad(kv(k_win), ((0, 0), (0, 0), (WINDOW, 0), (0, 0)))
    vw_pad = jnp.pad(kv(v_win), ((0, 0), (0, 0), (WINDOW, 0), (0, 0)))
    tab_g = rb.reshape(N_BUCKETS, G, HPG)
    bi = jnp.arange(B)[:, None, None, None]
    gi = jnp.arange(G)[None, :, None, None]

    def head_bias(dist):
        bsh = rb[t5_bucket(dist)]
        return bsh.reshape(dist.shape + (G, HPG)).transpose(2, 3, 0, 1)

    def block_fn(qb_idx):
        t0 = qb_idx * Q_BLOCK_2
        t_pos = t0 + jnp.arange(Q_BLOCK_2)
        qblk = lax.dynamic_slice_in_dim(qh, t0, Q_BLOCK_2, axis=3)
        gblk = lax.dynamic_slice_in_dim(gh, t0, Q_BLOCK_2, axis=3)
        s_c = jnp.einsum('bghtd,bgnd->bghtn', qblk, kc) * scale + head_bias(t_pos[:, None] - cmp_end[None, :])
        valid_c = cmp_end[None, :] <= t_pos[:, None]
        p_c = masked_softmax(s_c, valid_c)
        o_c = jnp.einsum('bghtn,bgnd->bghtd', p_c, vc)
        imp = jnp.einsum('bghtn,nj->bgtj', p_c, agg)
        cur = t_pos // SLC_BLOCK
        j = jnp.arange(n_slc)
        diff = cur[:, None] - j[None, :]
        forced = (j[None, :] == 0) | ((diff >= 0) & (diff < SLC_LOCAL))
        causal_blk = slc_start[None, :] <= t_pos[:, None]
        score = jnp.where(forced, BIG, jnp.where(causal_blk, imp, -BIG))
        _, idx = lax.top_k(score, n_sel)
        L = n_sel * SLC_BLOCK
        ks_g = ks_blocks[bi, gi, idx].reshape(B, G, Q_BLOCK_2, L, Dh)
        vs_g = vs_blocks[bi, gi, idx].reshape(B, G, Q_BLOCK_2, L, Dh)
        key_pos = (idx[..., None] * SLC_BLOCK + jnp.arange(SLC_BLOCK)).reshape(B, G, Q_BLOCK_2, L)
        dist_s = t_pos[None, None, :, None] - key_pos
        bias_s = jax.vmap(lambda tb, bk: tb[bk], in_axes=(1, 1), out_axes=1)(tab_g, t5_bucket(dist_s))
        bias_s = bias_s.transpose(0, 1, 4, 2, 3)
        s_s = jnp.einsum('bghtd,bgtld->bghtl', qblk, ks_g) * scale + bias_s
        p_s = masked_softmax(s_s, (dist_s >= 0)[:, :, None])
        o_s = jnp.einsum('bghtl,bgtld->bghtd', p_s, vs_g)
        kw = lax.dynamic_slice_in_dim(kw_pad, t0, WINDOW + Q_BLOCK_2, axis=2)
        vw = lax.dynamic_slice_in_dim(vw_pad, t0, WINDOW + Q_BLOCK_2, axis=2)
        kpos = t0 - WINDOW + jnp.arange(WINDOW + Q_BLOCK_2)
        dist_w = t_pos[:, None] - kpos[None, :]
        valid_w = (dist_w >= 0) & (dist_w < WINDOW) & (kpos[None, :] >= 0)
        s_w = jnp.einsum('bghtd,bgkd->bghtk', qblk, kw) * scale + head_bias(dist_w)
        p_w = masked_softmax(s_w, valid_w)
        o_w = jnp.einsum('bghtk,bgkd->bghtd', p_w, vw)
        return gblk[..., 0:1] * o_c + gblk[..., 1:2] * o_s + gblk[..., 2:3] * o_w

    o = lax.map(block_fn, jnp.arange(S // Q_BLOCK_2))
    o = o.transpose(1, 0, 4, 2, 3, 5).reshape(B, S, NSA_WIDTH)
    return o.astype(q.dtype)

def second_inputs(seed: int = 0) -> dict:
    key = jax.random.key(seed)
    ks = jax.random.split(key, 20)
    f32 = jnp.float32

    def nrm(k, shape, fan_in, scale=1.0):
        return jax.random.normal(k, shape, f32) * (scale * fan_in ** -0.5)

    def small(k, shape, s):
        return jax.random.normal(k, shape, f32) * s

    return {
        "x": jax.random.normal(ks[0], (BATCH, SEQ, D_MODEL), f32),
        "w_in": nrm(ks[1], (DEPTH, D_MODEL, D_IN_2), D_MODEL),
        "hg_lb_param": small(ks[2], (DEPTH, HG_WIDTH), 0.1),
        "hg_norm_w": 1.0 + small(ks[3], (DEPTH, HG_HEAD_DIM), 0.02),
        "cmp_pos_k": small(ks[4], (DEPTH, CMP_BLOCK, NSA_HEAD_DIM), 0.02),
        "cmp_w1_k": nrm(ks[5], (DEPTH, CMP_BLOCK * NSA_HEAD_DIM, CMP_HIDDEN), CMP_BLOCK * NSA_HEAD_DIM),
        "cmp_w2_k": nrm(ks[6], (DEPTH, CMP_HIDDEN, NSA_HEAD_DIM), CMP_HIDDEN),
        "cmp_pos_v": small(ks[7], (DEPTH, CMP_BLOCK, NSA_HEAD_DIM), 0.02),
        "cmp_w1_v": nrm(ks[8], (DEPTH, CMP_BLOCK * NSA_HEAD_DIM, CMP_HIDDEN), CMP_BLOCK * NSA_HEAD_DIM),
        "cmp_w2_v": nrm(ks[9], (DEPTH, CMP_HIDDEN, NSA_HEAD_DIM), CMP_HIDDEN),
        "rel_bias": small(ks[10], (N_BUCKETS, NSA_HEADS), 0.1),
        "w_out": nrm(ks[11], (DEPTH, D_MIX_2, D_MODEL), D_MIX_2, BETA),
        "ln1_g": 1.0 + small(ks[12], (DEPTH, D_MODEL), 0.02),
        "ln1_b": small(ks[13], (DEPTH, D_MODEL), 0.02),
        "w_ffn_gate": nrm(ks[14], (DEPTH, D_MODEL, D_FF_2), D_MODEL),
        "w_ffn_up": nrm(ks[15], (DEPTH, D_MODEL, D_FF_2), D_MODEL),
        "w_ffn_down": nrm(ks[16], (DEPTH, D_FF_2, D_MODEL), D_FF_2, BETA),
        "ln2_g": 1.0 + small(ks[17], (DEPTH, D_MODEL), 0.02),
        "ln2_b": small(ks[18], (DEPTH, D_MODEL), 0.02),
    }

def second_block(x, w_in, hg_lb_param, hg_norm_w, cmp_pos_k, cmp_w1_k, cmp_w2_k,
              cmp_pos_v, cmp_w1_v, cmp_w2_v, rel_bias, w_out, ln1_g, ln1_b,
              w_ffn_gate, w_ffn_up, w_ffn_down, ln2_g, ln2_b):
    lbs = hgrn2_lower_bounds(hg_lb_param)
    pts = _split_points()
    for l in range(DEPTH):
        proj = x @ w_in[l]
        hq, hf, hi, hg, nq, kc, vc, ks, vs, kw, vw, gt = jnp.split(proj, pts, axis=-1)
        o_a = hgrn2_mixer(hq, hf, hi, hg, lbs[l], hg_norm_w[l])
        o_b = nsa_mixer(nq, kc, vc, ks, vs, kw, vw, gt,
                        cmp_pos_k[l], cmp_w1_k[l], cmp_w2_k[l],
                        cmp_pos_v[l], cmp_w1_v[l], cmp_w2_v[l], rel_bias)
        mix = jnp.concatenate([o_a, o_b], axis=-1) @ w_out[l]
        x = layer_norm(ALPHA * x + mix, ln1_g[l], ln1_b[l])
        ffn = (jax.nn.silu(x @ w_ffn_gate[l]) * (x @ w_ffn_up[l])) @ w_ffn_down[l]
        x = layer_norm(ALPHA * x + ffn, ln2_g[l], ln2_b[l])
    return x


def setup_inputs(seed=0):
    out = dict(first_inputs(seed))
    for name, value in second_inputs(seed + 1).items():
        if name != "x":
            out[name + "_2"] = value
    return out


def reference(
    x, norm_gains, w_ffn_gate, w_ffn_up, w_ffn_down, w_in, w_out, diff_lambda, diff_subln_gain,
    w_in_2, hg_lb_param_2, hg_norm_w_2, cmp_pos_k_2, cmp_w1_k_2, cmp_w2_k_2, cmp_pos_v_2,
    cmp_w1_v_2, cmp_w2_v_2, rel_bias_2, w_out_2, ln1_g_2, ln1_b_2, w_ffn_gate_2, w_ffn_up_2,
    w_ffn_down_2, ln2_g_2, ln2_b_2,
):
    x = first_block(
        x, norm_gains, w_ffn_gate, w_ffn_up, w_ffn_down, w_in, w_out, diff_lambda,
        diff_subln_gain,
    )
    return second_block(
        x, w_in_2, hg_lb_param_2, hg_norm_w_2, cmp_pos_k_2, cmp_w1_k_2, cmp_w2_k_2, cmp_pos_v_2,
        cmp_w1_v_2, cmp_w2_v_2, rel_bias_2, w_out_2, ln1_g_2, ln1_b_2, w_ffn_gate_2, w_ffn_up_2,
        w_ffn_down_2, ln2_g_2, ln2_b_2,
    )


_drawn_inputs = setup_inputs


def setup_inputs(seed=0):
    import zlib

    import numpy as np

    out = dict(_drawn_inputs(seed))
    spreads = {}
    factors = {'diff_subln_gain': 3.321,
     'hg_lb_param_2': 4.544,
     'hg_norm_w_2': 8.0,
     'cmp_pos_k_2': 64.0,
     'cmp_pos_v_2': 47.011,
     'rel_bias_2': 8.0}
    for name, (base, spread) in spreads.items():
        noise = np.random.default_rng([zlib.crc32(name.encode()), seed]).standard_normal(out[name].shape)
        drawn = base * np.exp(spread * noise) if base else spread * noise
        out[name] = __import__('jax').numpy.asarray(drawn.astype(out[name].dtype))
    for name, factor in factors.items():
        out[name] = (out[name] * factor).astype(out[name].dtype)
    return out
```

```python
from contextlib import ExitStack
import math

import numpy as np

import concourse.bass as bass
from concourse import mybir

F32 = mybir.dt.float32
BF16 = mybir.dt.bfloat16
ALU = mybir.AluOpType
ACT = mybir.ActivationFunctionType
AX_X = mybir.AxisListType.X

P = 128
S = 512
NT = S // P
D = 1024
KD = D // P
FF = 2816
KF = FF // P
DEPTH = 2
NSLOT = 4
WIDE = KF // 2 * P
NARROW = KD * P
BIG = 1e30
EPS_RMS = 1e-6
EPS_LN = 1e-5
ALPHA = (2.0 * DEPTH) ** 0.25

DIL, DIFF, SB = 6, 4, 6
DH = 64
QA, KA, QB, KB, QC, KC = 0, 3, 6, 8, 10, 13
HG = 4
NSA = 8
LEVELS = 7
CMP_END = 31
NCMP = 31
SCR = 15200
VG = 280


class Layout:

    def __init__(self, tensor, width):
        self.tensor, self.width, self.at = tensor, width, 0

    def take(self, n):
        a = self.at
        self.at += n
        assert self.at <= self.width, (self.at, self.width)
        return self.tensor[:, a:self.at]


def triangle(a):
    return [0, 512, 896, 1152][a]


def build(nc, t):
    ctx = ExitStack()
    with ctx:
        def sb(name, shape, dt=F32):
            return ctx.enter_context(nc.sbuf_tensor(name, shape, dt))

        bank = [ctx.enter_context(nc.psum_tensor(f"bank{i}", [P, 512], F32)) for i in range(8)]
        xT = sb("xT", [P, KD, S])
        hT = sb("hT", [P, KD, S])
        yT = sb("yT", [P, KD, S])
        ring = sb("ring", [P, NSLOT, WIDE])
        big = sb("big", [P, 12288])
        guT = big[:, 0:KF * S].rearrange("p (c s) -> p c s", c=KF)
        projT = big[:, 0:16 * S].rearrange("p (c s) -> p c s", c=16)
        table = sb("table", [P, 6400])
        small = sb("small", [P, 256])
        mats = sb("mats", [P, 7, P])
        matsb = sb("matsb", [P, 2, P], BF16)
        scr = sb("scr", [P, SCR])

        nsem = {}

        def sem(name):
            nsem[name] = ctx.enter_context(nc.semaphore(name))
            return nsem[name]

        slot_in = [sem(f"slot_in{i}") for i in range(NSLOT)]
        slots_done = sem("slots_done")
        g_free = sem("g_free")
        silu_ready = sem("silu_ready")
        sq_ready = sem("sq_ready")
        sq_used = sem("sq_used")
        ln_ready = sem("ln_ready")
        rs_ready = sem("rs_ready")
        t_ready = sem("t_ready")
        x_ready = sem("x_ready")
        h_ready = sem("h_ready")
        par_in = sem("par_in")
        par_ready = sem("par_ready")
        seq = sem("seq")
        io = sem("io")
        const_in = sem("const_in")
        tp_free = sem("tp_free")
        vp_free = sem("vp_free")
        s_ready = sem("s_ready")
        p_max = sem("p_max")
        p_exp = sem("p_exp")
        p_rec = sem("p_rec")
        p_norm = sem("p_norm")
        p_turn = sem("p_turn")
        p_back = sem("p_back")
        o_ready = sem("o_ready")
        o_taken = sem("o_taken")
        z_ready = sem("z_ready")
        z_abs = sem("z_abs")
        z_exp = sem("z_exp")
        z_ln = sem("z_ln")
        z_sp = sem("z_sp")
        z_cum = sem("z_cum")
        z_w = sem("z_w")
        z_pv = sem("z_pv")
        d_sq = sem("d_sq")
        d_sum = sem("d_sum")
        d_rs = sem("d_rs")
        d_out = sem("d_out")
        y_done = sem("y_done")
        y_summed = sem("y_summed")
        c_ready = sem("c_ready")
        w_in1 = sem("w_in1")
        win = sem("win")
        c_hid = sem("c_hid")
        c_act = sem("c_act")
        c_out = sem("c_out")
        c_done = sem("c_done")
        f_act = sem("f_act")
        f_dve = sem("f_dve")
        k_turn = sem("k_turn")
        k_back = sem("k_back")
        suf_ready = sem("suf_ready")
        suf_exp = sem("suf_exp")
        kd_ready = sem("kd_ready")
        dec_ready = sem("dec_ready")
        dec_exp = sem("dec_exp")
        q_dec = sem("q_dec")
        k_dec = sem("k_dec")
        a_ready = sem("a_ready")
        a_mask = sem("a_mask")
        a_sum = sem("a_sum")
        u_ready = sem("u_ready")
        st_ready = sem("st_ready")
        ho_ready = sem("ho_ready")
        hsq = sem("hsq")
        hsum = sem("hsum")
        hrs = sem("hrs")
        hout = sem("hout")
        hmix = sem("hmix")
        silu_g = sem("silu_g")
        gate_ready = sem("gate_ready")

        sc = Layout(scr, SCR)
        sq = sc.take(2 * S).rearrange("p (b s) -> p b s", b=2)
        lnv = sc.take(S)
        rs = sc.take(S)
        tmp = sc.take(2 * S).rearrange("p (b s) -> p b s", b=2)
        mixer_at = sc.at

        OFF, ONES, BLK, NEGL, IDENT, SUF, MASK = 0, 1, 2, 3, 4, 5, 6
        onesD, blk64, negL, ident, negones = (mats[:, i, :] for i in (ONES, BLK, NEGL, IDENT, OFF))

        pos = [0]

        def landed(eng, n, i=0, per=0):
            eng.wait_ge(slot_in[n % NSLOT], 16 * (n // NSLOT + 1) + (16 * per // NSLOT) * i)

        def slot(n):
            return ring[:, n % NSLOT, :]

        def load(eng, n, src, width, i=None, per=0):
            if i is None:
                if n >= NSLOT:
                    eng.wait_ge(slots_done, n - NSLOT + 1)
            else:
                eng.wait_ge(slots_done, i * per + (n - NSLOT + 1))
            eng.dma_start(ring[:, n % NSLOT, 0:width], src).then_inc(slot_in[n % NSLOT], 16)

        def stream(eng, layer, arr, first, count, n0, width):
            def src(k):
                return arr[bass.ds(layer, 1), bass.ds(k, 1), :, :].rearrange("a b p n -> (a b p) n")
            head = max(0, NSLOT - n0)
            for k in range(min(head, count)):
                load(eng, n0 + k, src(first + k), width)
            n, rest = head, count - head
            if rest >= NSLOT:
                with eng.Fori(0, rest // NSLOT) as i:
                    for k in range(NSLOT):
                        load(eng, n0 + n + k, src(i * NSLOT + (first + n + k)), width, i, NSLOT)
                n += rest // NSLOT * NSLOT
            for k in range(n, count):
                load(eng, n0 + k, src(first + k), width)

        def sum_square(eng, q, m, i=0, per=0, on=6):
            eng.wait_ge(sq_ready, i * per + (8 * q + m + 1))
            eng.matmul(bank[on][:, :], onesD, sq[:, m % 2, :], start=(m == 0 and per == 0),
                       stop=(m == KD - 1), skip_group_check=True).then_inc(sq_used, 1)

        def act_root(eng, q, eps, on=6):
            eng.wait_ge(sq_used, 8 * q + 8 + 2)
            eng.activation(lnv, bank[on][:, :], ACT.Ln, bias=eps).then_inc(ln_ready, 1)
            eng.wait_ge(ln_ready, q + 1)
            eng.activation(rs, lnv, ACT.Exp, scale=-0.5).then_inc(rs_ready, 1)

        def act_square_x(eng, q, xr):
            for m in range(KD):
                if xr is not None:
                    eng.wait_ge(x_ready, xr + m + 1)
                eng.wait_ge(sq_used, 8 * q + m + 1)
                eng.activation(sq[:, m % 2, :], xT[:, m, :], ACT.Square).then_inc(sq_ready, 1)

        def pe_ffn(eng, c, n0, src, free, add):
            with eng.Fori(0, KF // 2) as i:
                for k in range(2):
                    eng.wait_ge(g_free, i * 2 + (KF * c + k + 1))
                    for u in range(2):
                        n = n0 + 2 * k + u
                        landed(eng, n, i, 4)
                        for kc in range(KD):
                            mm = eng.matmul(bank[k + 2 * u][:, :], slot(n)[:, kc * P:(kc + 1) * P],
                                            src[:, kc, :], start=(kc == 0), stop=(kc == KD - 1))
                        mm.then_inc(slots_done, 1)
            eng.wait_ge(g_free, KF * (c + 1) + 2)
            n1 = n0 + 2 * KF

            def down(m, i=0, per=0):
                free(eng, m, i, per)
                for half in range(2):
                    n = n1 + 2 * m + half
                    landed(eng, n, i, 2 * per)
                    for b in range(KF // 2):
                        kc = half * (KF // 2) + b
                        mm = eng.matmul(bank[4 + m % 2][:, :], slot(n)[:, b * P:(b + 1) * P],
                                        guT[:, kc, :], start=(kc == 0), stop=(kc == KF - 1))
                    mm.then_inc(slots_done, 1)

            down(0)
            down(1)
            add(eng, 0)
            down(2)
            with eng.Fori(0, 2) as i:
                add(eng, 1, i, 2)
                down(3, i, 2)
                add(eng, 2, i, 2)
                down(4, i, 2)
            add(eng, 5)
            down(7)
            add(eng, 6)
            add(eng, 7)

        def rms_free(q):
            def wait(eng, m, i=0, per=0):
                eng.wait_ge(sq_ready, i * per + (8 * q + m - 1))
            return wait

        def rms_add(q):
            return lambda eng, m, i=0, per=0: sum_square(eng, q, m, i, per)

        def ln_free(q):
            def wait(eng, m, i=0, per=0):
                eng.wait_ge(y_done, i * per + (8 * q + m + 1))
            return wait

        def ln_add(q):
            def add(eng, m, i=0, per=0):
                eng.wait_ge(y_done, i * per + (8 * q + m + 1 + 2))
                src = yT[:, m, :] if per == 0 else yT[:, bass.ds(i * per + m, 1), :].rearrange("p a s -> p (a s)")
                eng.matmul(bank[6][:, :], onesD, src, start=(m == 0), stop=(m == KD - 1),
                           skip_group_check=True).then_inc(y_summed, 1)
            return add

        def act_y(eng, q, n1, per_tile, m, i=0, per=0):
            eng.wait_ge(slots_done, i * (per * per_tile) + (n1 + per_tile * (m + 1)))
            dst = yT[:, m, :] if per == 0 else yT[:, bass.ds(i * per + m, 1), :].rearrange("p a s -> p (a s)")
            eng.activation(dst, bank[4 + m % 2][:, :], ACT.Copy)
            eng.wait_ge(sq_used, i * per + (8 * q + m + 1))
            eng.activation(sq[:, m % 2, :], bank[4 + m % 2][:, :], ACT.Square).then_inc(sq_ready, 1)

        def act_silu(eng, c, n0):
            with eng.Fori(0, KF // 2) as i:
                for k in range(2):
                    eng.wait_ge(g_free, i * 2 + (KF * c + k + 1))
                    eng.wait_ge(slots_done, i * 4 + (n0 + 2 * k + 1))
                    eng.activation(tmp[:, k, :], bank[k][:, :], ACT.Silu).then_inc(silu_ready, 1)

        def act_ffn(eng, c, q, n0):
            act_silu(eng, c, n0)
            with eng.Fori(0, KD // 2) as i:
                for m in range(2):
                    act_y(eng, q, n0 + 2 * KF, 2, m, i, 2)
            act_root(eng, q, EPS_RMS)

        def dve_ffn(eng, c, n0):
            with eng.Fori(0, KF // 2) as i:
                for k in range(2):
                    eng.wait_ge(slots_done, i * 4 + (n0 + 2 * k + 2))
                    eng.wait_ge(silu_ready, i * 2 + (KF * c + k + 1))
                    dst = guT[:, bass.ds(i * 2 + k, 1), :].rearrange("p a s -> p (a s)")
                    eng.tensor_tensor(dst, tmp[:, k, :], bank[2 + k][:, :], ALU.mult).then_inc(g_free, 1)

        gcol = small[:, 0:48]
        ghalf = small[:, 48:96]

        def dve_post(eng, q, xr, gains):
            eng.wait_ge(rs_ready, q + 1)
            for m in range(KD):
                if xr + m >= 2:
                    eng.wait_ge(x_ready, xr + m - 1)
                eng.scalar_tensor_tensor(tmp[:, m % 2, :], yT[:, m, :], gains[:, m:m + 1], rs,
                                         ALU.mult, ALU.mult).then_inc(t_ready, 1)

        def pool_post(eng, xr):
            for m in range(KD):
                eng.wait_ge(t_ready, xr + m + 1)
                eng.tensor_tensor(xT[:, m, :], xT[:, m, :], tmp[:, m % 2, :], ALU.add).then_inc(x_ready, 1)

        def dve_pre(eng, q, gains):
            eng.wait_ge(rs_ready, q + 1)
            for m in range(KD):
                eng.scalar_tensor_tensor(hT[:, m, :], xT[:, m, :], gains[:, m:m + 1], rs,
                                         ALU.mult, ALU.mult).then_inc(h_ready, 1)

        N_IN = 24

        def pe_proj_T(eng, n0, tiles, src):
            for j in range(tiles):
                if j >= 2:
                    eng.wait_ge(tp_free, j - 1)
                landed(eng, n0 + j)
                for kc in range(KD):
                    mm = eng.matmul(bank[j % 2][:, :], slot(n0 + j)[:, kc * P:(kc + 1) * P],
                                    src[:, kc, :], start=(kc == 0), stop=(kc == KD - 1))
                mm.then_inc(slots_done, 1)

        def act_proj_T(eng, n0, scales):
            for j, s in enumerate(scales):
                eng.wait_ge(slots_done, n0 + j + 1)
                eng.activation(projT[:, j, :], bank[j % 2][:, :], ACT.Copy, scale=s).then_inc(tp_free, 1)

        def pe_proj_N(eng, n0, half, src, width=512, per=2, slots=4):
            if half:
                eng.wait_ge(vp_free, NT * half)
            for s in range(slots):
                landed(eng, n0 + s)
                for k in range(per):
                    kc = s * per + k
                    for b in range(NT):
                        mm = eng.matmul(bank[2 + b][:, 0:width], src[:, kc, b * P:(b + 1) * P],
                                        slot(n0 + s)[:, k * width:(k + 1) * width],
                                        start=(kc == 0), stop=(kc == KD - 1))
                mm.then_inc(slots_done, 1)

        def dve_proj_N(eng, n0, half, dst, width=512, slots=4):
            eng.wait_ge(slots_done, n0 + slots)
            for b in range(NT):
                eng.tensor_copy(dst[:, b, :], bank[2 + b][:, 0:width]).then_inc(vp_free, 1)

        V1 = big[:, 8192:12288].rearrange("p (b n) -> p b n", b=NT)
        sc.at = mixer_at
        PR = 4
        prob = sc.take(PR * S).rearrange("p (b s) -> p b s", b=PR)
        probT = sc.take(4 * S * 2).rearrange("p (b j s) -> p b j s", b=2, j=NT)
        stat = sc.take(64)
        absz = sc.take(1280)
        softp = sc.take(1280)
        wts = probT.rearrange("p b j s -> p b (j s)")
        dsq = sc.take(S)
        tab1 = table[:, 0:10 * S].rearrange("p (h s) -> p h s", h=10)
        lamcol, negcol = small[:, 96:97], small[:, 97:98]
        lamtmp = small[:, 100:140]
        subg = small[:, 98:99]
        lam_in = sc.take(132)
        lamprod = sc.take(64).rearrange("p (a n) -> p a n", a=2)

        units = [(h, i) for h in range(DIL + DIFF) for i in range(NT)]
        maps = []
        for u, (h, i) in enumerate(units):
            maps += [(u, 0)] + ([(u, 1)] if h >= DIL else [])
        first_map = [next(k for k, (v, _) in enumerate(maps) if v == u) for u in range(len(units))]

        def operands(h, w):
            if h < DIL:
                lo = (h % 2) * DH
                return QA + h // 2, KA + h // 2, lo, lo + DH
            g = h - DIL
            lo = (g % 2) * DH + w * 32
            return QB + g // 2, KB + g // 2, lo, lo + 32

        def pe_soft(eng):
            eng.wait_ge(tp_free, 16)
            eng.wait_ge(vp_free, 8)

            def scores(k):
                u, w = maps[k]
                h, i = units[u]
                q, kk, lo, hi = operands(h, w)
                if k >= 3:
                    eng.wait_ge(p_max, k - 2)
                eng.matmul(bank[k % 3][:, 0:(i + 1) * P], projT[lo:hi, q, i * P:(i + 1) * P],
                           projT[lo:hi, kk, 0:(i + 1) * P], start=True, stop=True).then_inc(s_ready, 1)

            def turn(u):
                h, i = units[u]
                eng.wait_ge(p_norm, u + 1)
                if u >= 2:
                    eng.wait_ge(p_back, u - 1)
                for j in range(i + 1):
                    mm = eng.transpose(bank[3 + u % 2][:, j * P:(j + 1) * P],
                                       prob[:, first_map[u] % PR, j * P:(j + 1) * P], ident)
                mm.then_inc(p_turn, 1)

            def pv(h):
                pair = h // 2
                eng.wait_ge(p_back, NT * (h + 1))
                if h % 2 == 0 and pair >= 2:
                    eng.wait_ge(o_taken, pair - 1)
                lo = (h % 2) * DH
                for j in range(NT):
                    mm = eng.matmul(bank[5 + 2 * (pair % 2)][lo:lo + DH, j * P:S],
                                    V1[:, j, h * DH:(h + 1) * DH], probT[:, h % 2, j, j * P:S],
                                    start=(j == 0), stop=(j == NT - 1), skip_group_check=True)
                mm.then_inc(o_ready, 1)

            k = 0
            LAG = 2
            for u in range(len(units) + LAG + 1):
                if u < len(units):
                    while k < len(maps) and maps[k][0] == u:
                        scores(k)
                        k += 1
                if 0 <= u - LAG < len(units):
                    turn(u - LAG)
                v = u - LAG - 1
                if v >= 0 and v % NT == NT - 1:
                    pv(v // NT)
                    if v // NT == DIL + 1 or v // NT == DIL + 3:
                        pair = v // NT // 2
                        eng.wait_ge(d_sq, pair - 2)
                        eng.matmul(bank[6][:, :], blk64, dsq, start=True, stop=True).then_inc(d_sum, 1)

        def dve_soft(eng):
            def post(u):
                h, i = units[u]
                w = (i + 1) * P
                k = first_map[u]
                if h < DIL:
                    eng.wait_ge(p_exp, k + 1)
                    eng.reciprocal(stat[:, 32 + k % PR:33 + k % PR], stat[:, 16 + k % PR:17 + k % PR]).then_inc(p_rec, 1)
                    rec[0] += 1
                    eng.wait_ge(p_rec, rec[0])
                    a = prob[:, k % PR, 0:w]
                    eng.tensor_scalar(a, a, stat[:, 32 + k % PR:33 + k % PR], None, ALU.mult).then_inc(p_norm, 1)
                    return
                a, b = k % PR, (k + 1) % PR
                eng.wait_ge(p_exp, k + 2)
                eng.reciprocal(stat[:, 32 + a:33 + a], stat[:, 16 + a:17 + a]).then_inc(p_rec, 1)
                eng.reciprocal(stat[:, 32 + b:33 + b], stat[:, 16 + b:17 + b]).then_inc(p_rec, 1)
                rec[0] += 2
                eng.wait_ge(p_rec, rec[0])
                eng.tensor_scalar(prob[:, a, 0:w], prob[:, a, 0:w], stat[:, 32 + a:33 + a], None, ALU.mult).then_inc(p_rec, 1)
                eng.tensor_scalar(stat[:, 48 + b:49 + b], stat[:, 32 + b:33 + b], negcol, None, ALU.mult).then_inc(p_rec, 1)
                rec[0] += 2
                eng.wait_ge(p_rec, rec[0])
                eng.scalar_tensor_tensor(prob[:, a, 0:w], prob[:, b, 0:w], stat[:, 48 + b:49 + b],
                                         prob[:, a, 0:w], ALU.mult, ALU.add).then_inc(p_norm, 1)

            def freed(k):
                if k >= PR:
                    v = maps[k - PR][0]
                    eng.wait_ge(p_turn, v + 1)

            rec = [0]
            k = 0
            for u in range(len(units) + 1):
                if u < len(units):
                    while k < len(maps) and maps[k][0] == u:
                        h, i = units[u]
                        w = (i + 1) * P
                        eng.wait_ge(s_ready, k + 1)
                        freed(k)
                        eng.tensor_tensor_reduce(prob[:, k % PR, 0:w], bank[k % 3][:, 0:w],
                                                 tab1[:, h, S - w:S], 1.0, 3.0e38, ALU.add, ALU.min,
                                                 stat[:, k % PR:k % PR + 1]).then_inc(p_max, 1)
                        k += 1
                if u >= 1:
                    post(u - 1)

        def act_soft(eng):
            def back(u):
                h, i = units[u]
                eng.wait_ge(p_turn, u + 1)
                if h >= 2 and i == 0:
                    eng.wait_ge(o_ready, h - 1)
                eng.activation(probT[:, h % 2, 0:i + 1, i * P:(i + 1) * P],
                               bank[3 + u % 2][:, 0:(i + 1) * P].rearrange("p (j s) -> p j s", j=i + 1),
                               ACT.Copy).then_inc(p_back, 1)

            def take(pair):
                eng.wait_ge(o_ready, 2 * pair + 2)
                b = bank[5 + 2 * (pair % 2)][:, :]
                if pair < DIL // 2:
                    eng.activation(hT[:, pair, :], b, ACT.Copy).then_inc(o_taken, 1)
                    return
                n = pair - DIL // 2
                eng.activation(dsq, b, ACT.Square).then_inc(d_sq, 1)
                eng.activation(hT[:, pair, :], b, ACT.Copy).then_inc(o_taken, 1)
                eng.wait_ge(d_sum, n + 1)
                if n:
                    eng.wait_ge(d_out, n)
                eng.activation(lnv, bank[6][:, :], ACT.Ln, bias=EPS_RMS).then_inc(d_rs, 1)
                eng.wait_ge(d_rs, 2 * n + 1)
                eng.activation(rs, lnv, ACT.Exp, scale=-0.5).then_inc(d_rs, 1)

            k = 0
            for u in range(len(units) + 3):
                if u < len(units):
                    while k < len(maps) and maps[k][0] == u:
                        h, i = units[u]
                        w = (i + 1) * P
                        eng.wait_ge(p_max, k + 1)
                        eng.activation(prob[:, k % PR, 0:w], prob[:, k % PR, 0:w], ACT.Exp, scale=-1.0,
                                       bias=stat[:, k % PR:k % PR + 1],
                                       accum_out=stat[:, 16 + k % PR:17 + k % PR]).then_inc(p_exp, 1)
                        k += 1
                if 0 <= u - 2 < len(units):
                    back(u - 2)
                if u >= 3 and (u - 3) % (2 * NT) == 2 * NT - 1:
                    take((u - 3) // (2 * NT))

        def pool_diff(eng):
            for n in range(2):
                m = DIL // 2 + n
                eng.wait_ge(d_rs, 2 * n + 2)
                eng.tensor_tensor(hT[:, m, :], hT[:, m, :], rs, ALU.mult).then_inc(seq, 1)
                eng.wait_ge(seq, SEQ1 + n + 1)
                eng.tensor_scalar(hT[:, m, :], hT[:, m, :], subg, None, ALU.mult).then_inc(d_out, 1)

        SEQ1 = 6

        def zcols(a, c0, c1):
            return (c0 - 384, c1 - 384) if a == 3 else (c0, c1)

        def zb(h, a):
            return bank[3 * (h % 2) + [0, 1, 2, 1][a]]

        def pe_stick(eng):
            eng.wait_ge(p_back, len(units))
            eng.wait_ge(o_taken, 5)

            def z(h):
                q, kk, lo = QC + h // 2, KC + h // 2, (h % 2) * DH
                if h >= 2:
                    eng.wait_ge(z_w, 4 * (h - 1))
                for a in (0, 1, 3, 2):
                    c0, c1 = zcols(a, a * P, S)
                    eng.matmul(zb(h, a)[:, c0:c1], projT[lo:lo + DH, kk, a * P:(a + 1) * P],
                               projT[lo:lo + DH, q, a * P:S], start=(a != 3), stop=False,
                               skip_group_check=True)
                    mm = eng.matmul(zb(h, a)[:, c0:c0 + P], matsb[:, 0, :], matsb[:, 1, :],
                                    start=False, stop=True, skip_group_check=True)
                mm.then_inc(z_ready, 1)

            def cum(h):
                eng.wait_ge(z_sp, 4 * (h + 1))
                for a in (0, 1, 3, 2):
                    for b in range(a, NT):
                        c0, c1 = zcols(a, b * P, S)
                        mm = eng.matmul(zb(h, a)[:, c0:c1], negL if a == b else negones,
                                        softp[:, triangle(b):triangle(b) + (NT - b) * P],
                                        start=False, stop=True, skip_group_check=True)
                mm.then_inc(z_cum, 1)

            def pv(h):
                eng.wait_ge(z_w, 4 * (h + 1))
                pair, lo = h // 2, (h % 2) * DH
                if h % 2 == 0 and pair >= 1:
                    eng.wait_ge(o_taken, 5 + pair)
                for a in range(NT):
                    mm = eng.matmul(bank[7][lo:lo + DH, a * P:S], V1[:, a, 640 + h * DH:640 + (h + 1) * DH],
                                    wts[:, h % 2, triangle(a):triangle(a) + (NT - a) * P],
                                    start=(a == 0), stop=(a == NT - 1), skip_group_check=True)
                mm.then_inc(z_pv, 1)

            z(0)
            for h in range(SB):
                if h + 1 < SB:
                    z(h + 1)
                cum(h)
                if h >= 1:
                    pv(h - 1)
            pv(SB - 1)

        def dve_stick(eng):
            for h in range(SB):
                eng.wait_ge(z_ready, h + 1)
                eng.wait_ge(z_ln, h + 1)
                for a in range(NT):
                    c0, c1 = zcols(a, a * P, S)
                    t0 = triangle(a)
                    sp = softp[:, t0:t0 + c1 - c0]
                    eng.scalar_tensor_tensor(sp, zb(h, a)[:, c0:c1], 0.0, sp, ALU.max, ALU.add).then_inc(z_sp, 1)

        def act_stick(eng):
            def first(h):
                eng.wait_ge(z_ready, h + 1)
                for a in range(NT):
                    c0, c1 = zcols(a, a * P, S)
                    t0 = triangle(a)
                    eng.activation(absz[:, t0:t0 + c1 - c0], zb(h, a)[:, c0:c1], ACT.Abs).then_inc(z_abs, 1)
                eng.wait_ge(z_abs, 4 * (h + 1))
                eng.activation(absz, absz, ACT.Exp, scale=-1.0).then_inc(z_exp, 1)
                eng.wait_ge(z_exp, h + 1)
                if h:
                    eng.wait_ge(z_cum, h)
                eng.activation(softp, absz, ACT.Ln, bias=1.0).then_inc(z_ln, 1)

            def weights(h):
                eng.wait_ge(z_cum, h + 1)
                if h >= 2:
                    eng.wait_ge(z_pv, h - 1)
                for a in range(NT):
                    c0, c1 = zcols(a, a * P, S)
                    t0 = triangle(a)
                    eng.activation(wts[:, h % 2, t0:t0 + c1 - c0], zb(h, a)[:, c0:c1], ACT.Exp).then_inc(z_w, 1)

            def take(pair):
                eng.wait_ge(z_pv, 2 * pair + 2)
                eng.activation(hT[:, 5 + pair, :], bank[7][:, :], ACT.Copy).then_inc(o_taken, 1)

            for h in range(SB):
                first(h)
                weights(h)
                if h >= 2 and h % 2 == 0:
                    take(h // 2 - 1)
            take(2)

        def pe_out(eng, n0, free, add):
            def col(m):
                free(eng, m)
                landed(eng, n0 + m)
                for kc in range(KD):
                    mm = eng.matmul(bank[4 + m % 2][:, :], slot(n0 + m)[:, kc * P:(kc + 1) * P],
                                    hT[:, kc, :], start=(kc == 0), stop=(kc == KD - 1))
                mm.then_inc(slots_done, 1)
            for m in range(KD):
                col(m)
                if m:
                    add(eng, m - 1)
            add(eng, KD - 1)

        with nc.Block() as block:
            @block.sync
            def _(sp):
                sp.dma_start(xT[:, :, :], t["xT"]).then_inc(io, 16)
                sp.dma_start(mats[:, :, :], t["mats"]).then_inc(io, 16)
                sp.dma_start(table[:, 0:10 * S], t["table1"]).then_inc(io, 16)
                sp.wait_ge(io, 48)

            @block.vector
            def _(dve):
                dve.wait_ge(io, 48)
                dve.tensor_copy(matsb[:, 0, :], ident)
                dve.tensor_copy(matsb[:, 1, :], mats[:, MASK, :])

        FFN_SLOTS = 2 * KF + 2 * KD
        n_ffn0, n_in = 0, FFN_SLOTS
        n_out = n_in + N_IN
        n_ffn1 = n_out + KD
        A = 2 * KF

        with nc.Fori(0, DEPTH) as layer:
            with nc.Block() as block:
                @block.sync
                def _(sp):
                    sp.dma_start(small[:, 0:48], t["gains1"][bass.ds(layer, 1), :, :].rearrange("a p n -> (a p) n")).then_inc(par_in, 16)
                    sp.dma_start(small[:, 98:100], t["subg"][bass.ds(layer, 1), :, :].rearrange("a p n -> (a p) n")).then_inc(par_in, 16)
                    sp.dma_start(lam_in[:, 0:129], t["lam"][bass.ds(layer, 1), :, :].rearrange("a p n -> (a p) n")).then_inc(par_in, 16)
                    stream(sp, layer, t["w8_1"], 0, A, n_ffn0, NARROW)
                    stream(sp, layer, t["w11_1"], 0, 2 * KD, n_ffn0 + A, WIDE)
                    stream(sp, layer, t["w8_1"], A, N_IN + KD, n_in, NARROW)
                    stream(sp, layer, t["w8_1"], A + N_IN + KD, A, n_ffn1, NARROW)
                    stream(sp, layer, t["w11_1"], 2 * KD, 2 * KD, n_ffn1 + A, WIDE)

                @block.tensor
                def _(pe):
                    for m in range(KD):
                        sum_square(pe, 0, m)
                    pe.wait_ge(h_ready, 8)
                    pe_ffn(pe, 0, n_ffn0, hT, rms_free(1), rms_add(1))
                    for m in range(KD):
                        sum_square(pe, 2, m)
                    pe.wait_ge(h_ready, 16)
                    pe_proj_T(pe, n_in, 16, hT)
                    pe_proj_N(pe, n_in + 16, 0, hT)
                    pe_proj_N(pe, n_in + 20, 1, hT)
                    pe_soft(pe)
                    pe_stick(pe)
                    pe.wait_ge(o_taken, 8)
                    pe.wait_ge(d_out, 2)
                    pe_out(pe, n_out, rms_free(3), rms_add(3))
                    for m in range(KD):
                        sum_square(pe, 4, m)
                    pe.wait_ge(h_ready, 24)
                    pe_ffn(pe, 1, n_ffn1, hT, rms_free(5), rms_add(5))

                @block.scalar
                def _(act):
                    act_square_x(act, 0, None)
                    act_root(act, 0, EPS_RMS)
                    act_ffn(act, 0, 1, n_ffn0)
                    act_square_x(act, 2, 0)
                    act_root(act, 2, EPS_RMS)
                    act_proj_T(act, n_in, [-DH ** -0.5] * 3 + [1.0] * 3 + [-32 ** -0.5] * 2 + [1.0] * 2
                               + [DH ** -0.5] * 3 + [1.0] * 3)
                    act.wait_ge(seq, 4)
                    act.activation(lamtmp[:, 2:4], lamtmp[:, 0:2], ACT.Exp).then_inc(par_ready, 1)
                    act_soft(act)
                    act_stick(act)
                    for m in range(KD):
                        act_y(act, 3, n_out, 1, m)
                    act_root(act, 3, EPS_RMS)
                    act_square_x(act, 4, 8)
                    act_root(act, 4, EPS_RMS)
                    act_ffn(act, 1, 5, n_ffn1)

                @block.vector
                def _(dve):
                    dve.sem_inc(g_free, 2)
                    dve.sem_inc(sq_used, 2)
                    dve.wait_ge(par_in, 48)
                    dve.tensor_scalar(ghalf, gcol, 0.5, None, ALU.mult).then_inc(seq, 1)
                    dve.tensor_tensor(lamprod, lam_in[:, 0:64].rearrange("p (a n) -> p a n", a=2),
                                      lam_in[:, 64:128].rearrange("p (a n) -> p a n", a=2), ALU.mult).then_inc(seq, 1)
                    dve.wait_ge(seq, 2)
                    dve.tensor_reduce(lamtmp[:, 0:2], lamprod, AX_X, ALU.add).then_inc(seq, 1)
                    dve.tensor_scalar(subg, subg, small[:, 99:100], None, ALU.mult).then_inc(seq, 1)
                    dve.wait_ge(seq, 4)
                    dve_pre(dve, 0, gcol[:, 0:8])
                    dve_ffn(dve, 0, n_ffn0)
                    dve_post(dve, 1, 0, ghalf[:, 8:16])
                    dve_pre(dve, 2, gcol[:, 16:24])
                    dve_proj_N(dve, n_in + 16, 0, V1[:, :, 0:512])
                    dve_proj_N(dve, n_in + 20, 1, V1[:, :, 512:1024])
                    dve.wait_ge(par_ready, 1)
                    dve.tensor_tensor(lamtmp[:, 4:5], lamtmp[:, 3:4], lamtmp[:, 2:3], ALU.subtract).then_inc(seq, 1)
                    dve.wait_ge(seq, 5)
                    dve.tensor_scalar(negcol, lamtmp[:, 4:5], lam_in[:, 128:129], None, ALU.subtract).then_inc(seq, 1)
                    dve.wait_ge(seq, 6)
                    dve_soft(dve)
                    dve_stick(dve)
                    dve_post(dve, 3, 8, gcol[:, 24:32])
                    dve_pre(dve, 4, gcol[:, 32:40])
                    dve_ffn(dve, 1, n_ffn1)
                    dve_post(dve, 5, 16, ghalf[:, 40:48])

                @block.gpsimd
                def _(pool):
                    pool_post(pool, 0)
                    pool_diff(pool)
                    pool_post(pool, 8)
                    pool_post(pool, 16)

            with nc.Block() as block:
                @block.sync
                def _(sp):
                    for s in nsem.values():
                        sp.sem_clear(s)

        HQ, HGT, NQ, KCM, VCM, KSL, KWI = 0, 4, 8, 12, 13, 14, 15
        LF = big[:, 8192:10240].rearrange("p (b n) -> p b n", b=NT)
        HV = big[:, 10240:12288].rearrange("p (b n) -> p b n", b=NT)
        sc.at = mixer_at
        par = sc.take(64 + 128 + 1 + 32)
        posk, posv, w2k, w2v = par[:, 0:32], par[:, 32:64], par[:, 64:128], par[:, 128:192]
        gwcol = par[:, 192:193]
        g1, b1, g2, b2 = (par[:, 193 + 8 * n:201 + 8 * n] for n in range(4))
        flags = sc.take(4)
        vg = sc.take(NT * VG).rearrange("p (b n) -> p b n", b=NT)
        gate = sc.take(NT * 24).rearrange("p (b n) -> p b n", b=NT)
        chid = sc.take(128).rearrange("p (g k n) -> p g k n", g=2, k=2)
        kcmp = sc.take(32)
        vcmp = sc.take(128)
        valid = sc.take(1)
        both_at = sc.at
        winK = sc.take(32 * NCMP).rearrange("p (i n) -> p i n", i=32)
        winV = sc.take(32 * NCMP).rearrange("p (i n) -> p i n", i=32)
        w1k = hT[:, :, :].rearrange("p c s -> p (c s)").rearrange("p (i n) -> p i n", i=32)
        w1v = yT[:, :, :].rearrange("p c s -> p (c s)").rearrange("p (i n) -> p i n", i=32)
        tab2 = table[:, 0:NSA * S].rearrange("p (h s) -> p h s", h=NSA)
        span = table[:, 4096:5120]
        lmask = table[:, 5120:6144]

        sc.at = both_at
        kN = sc.take(2048).rearrange("p (b n) -> p b n", b=NT)
        kT = sc.take(2048).rearrange("p (h s) -> p h s", h=HG)
        t_at = sc.at
        QR = sc.take(2048).rearrange("p (r l s) -> p r l s", r=2, l=8)
        KL = sc.take(1792).rearrange("p (r l s) -> p r l s", r=2, l=LEVELS)
        AM = sc.take(1024)
        scs = sc.take(256).rearrange("p (r s) -> p r s", r=2)
        ST = sc.take(256).rearrange("p (r s) -> p r s", r=2)
        T1 = scr[:, t_at:t_at + 2048].rearrange("p (b n) -> p b n", b=NT)
        T2 = scr[:, t_at + 2048:t_at + 4096].rearrange("p (b n) -> p b n", b=NT)
        logA, logB = kT[:, 0, :], kT[:, 1, :]
        lbp0, lbp1 = kT[:, 2, :], kT[:, 3, :]
        yflat = yT[:, :, :].rearrange("p c s -> p (c s)")
        E = yflat[:, 0:2048].rearrange("p (r n) -> p r n", r=2)
        KDE = yflat[:, 2048:3584].rearrange("p (b n) -> p b n", b=3)

        def wide(v):
            return v.unsqueeze(1).broadcast_to([P, NT, 512])

        def dve_forget(eng):
            def step(ins):
                ins.then_inc(f_dve, 1)
                fd[0] += 1
            fd = [0]
            eng.wait_ge(par_in, 48)
            step(eng.tensor_tensor(T1[:, 0, :], lbp1, lbp0, ALU.subtract))
            eng.wait_ge(f_act, 3)
            step(eng.scalar_tensor_tensor(T1[:, 1, :], T1[:, 0, :], 0.0, T1[:, 1, :], ALU.max, ALU.add))
            eng.wait_ge(f_dve, 2)
            step(eng.tensor_scalar(logB, T1[:, 1, :], flags[:, 1:2], None, ALU.mult))
            step(eng.tensor_tensor(T1[:, 2, :], T1[:, 0, :], T1[:, 1, :], ALU.subtract))
            eng.wait_ge(f_dve, 4)
            step(eng.tensor_scalar(logA, T1[:, 2, :], flags[:, 0:1], flags[:, 2:3], ALU.mult, ALU.add))
            eng.wait_ge(f_dve, 5)
            eng.wait_ge(f_act, 6)
            step(eng.scalar_tensor_tensor(T2, LF, 0.0, T1, ALU.min, ALU.subtract))
            eng.wait_ge(f_dve, 6)
            step(eng.tensor_tensor(T2, T2, wide(logB), ALU.add))
            eng.wait_ge(f_dve, 7)
            step(eng.tensor_tensor(kN, T2, LF, ALU.subtract))
            step(eng.tensor_tensor(T1, wide(logA), T2, ALU.subtract))
            eng.wait_ge(f_dve, 9)
            step(eng.tensor_tensor(LF, wide(logA), T2, ALU.max))
            eng.wait_ge(f_act, 10)
            eng.wait_ge(f_dve, 10)
            step(eng.tensor_tensor(LF, LF, T1, ALU.add))

        def act_forget(eng):
            def step(ins):
                ins.then_inc(f_act, 1)
                fa[0] += 1
                eng.wait_ge(f_act, fa[0])
            fa = [0]
            eng.wait_ge(f_dve, 1)
            step(eng.activation(T1[:, 1, :], T1[:, 0, :], ACT.Abs))
            step(eng.activation(T1[:, 1, :], T1[:, 1, :], ACT.Exp, scale=-1.0))
            step(eng.activation(T1[:, 1, :], T1[:, 1, :], ACT.Ln, bias=1.0))
            eng.wait_ge(f_dve, 5)
            eng.wait_ge(vp_free, 4)
            step(eng.activation(T1, LF, ACT.Abs))
            step(eng.activation(T1, T1, ACT.Exp, scale=-1.0))
            step(eng.activation(T1, T1, ACT.Ln, bias=1.0))
            eng.wait_ge(f_dve, 9)
            step(eng.activation(T1, T1, ACT.Abs))
            step(eng.activation(kN, kN, ACT.Exp))
            step(eng.activation(T1, T1, ACT.Exp, scale=-1.0))
            step(eng.activation(T1, T1, ACT.Ln, bias=1.0))

        def dve_windows(eng):
            eng.wait_ge(tp_free, 14)
            for dst, j, pos_ in ((winK, KCM, posk), (winV, VCM, posv)):
                src = projT[:, j, :].rearrange("p (n i) -> p i n", i=16)
                for half in range(2):
                    eng.tensor_tensor(dst[:, 16 * half:16 * half + 16, :], src[:, :, half:half + NCMP],
                                      pos_[:, 16 * half:16 * half + 16].unsqueeze(2).broadcast_to([P, 16, NCMP]),
                                      ALU.add).then_inc(win, 1)

        def pe_compress(eng):
            eng.wait_ge(w_in1, 32)
            eng.wait_ge(win, 4)
            eng.wait_ge(tp_free, 16)
            for kind, (w1, src) in enumerate(((w1k, winK), (w1v, winV))):
                for g in range(2):
                    lo = g * DH
                    for i in range(32):
                        mm = eng.matmul(bank[g][:, kind * 32:kind * 32 + NCMP], w1[lo:lo + DH, i, :],
                                        src[lo:lo + DH, i, :], start=(i == 0), stop=(i == 31),
                                        skip_group_check=True)
            mm.then_inc(c_hid, 1)
            eng.wait_ge(c_act, 2)
            for g in range(2):
                eng.matmul(bank[6][g * DH:(g + 1) * DH, 0:NCMP], w2k, chid[:, g, 0, 0:NCMP],
                           start=True, stop=True, skip_group_check=True)
            for g in range(2):
                mm = eng.matmul(bank[7][0:NCMP, g * DH:(g + 1) * DH], chid[:, g, 1, 0:NCMP], w2v,
                                start=True, stop=True, skip_group_check=True)
            mm.then_inc(c_out, 1)

        def act_compress(eng):
            eng.wait_ge(c_hid, 1)
            for g in range(2):
                eng.activation(chid[:, g, :, 0:NCMP],
                               bank[g][:, 0:64].rearrange("p (k n) -> p k n", k=2)[:, :, 0:NCMP],
                               ACT.Gelu_apprx_tanh).then_inc(c_act, 1)

        def dve_compress(eng):
            eng.wait_ge(c_out, 1)
            eng.tensor_copy(kcmp[:, 0:NCMP], bank[6][:, 0:NCMP]).then_inc(c_done, 1)
            eng.tensor_copy(vcmp[0:NCMP, :], bank[7][0:NCMP, 0:128]).then_inc(c_done, 1)

        def pe_hgrn_keys(eng):
            eng.wait_ge(f_act, 8)
            for h in range(HG):
                for b in range(NT):
                    mm = eng.transpose(bank[2 + h][:, b * P:(b + 1) * P], kN[:, b, h * P:(h + 1) * P], ident)
                mm.then_inc(k_turn, 1)
            eng.wait_ge(f_dve, 11)
            for b in range(3):
                eng.matmul(bank[[6, 7, 0][b]][:, :], mats[:, SUF, :], LF[:, b, :],
                           start=True, stop=True).then_inc(suf_ready, 1)

        def act_hgrn_keys(eng):
            for h in range(HG):
                eng.wait_ge(k_turn, h + 1)
                if h == 0:
                    eng.wait_ge(f_dve, 10)
                eng.activation(kT[:, h, :], bank[2 + h][:, :], ACT.Copy).then_inc(k_back, 1)
            for b in range(3):
                eng.wait_ge(suf_ready, b + 1)
                eng.activation(KDE[:, b, :], bank[[6, 7, 0][b]][:, :], ACT.Exp).then_inc(suf_exp, 1)

        def dve_hgrn_keys(eng):
            for b in range(3):
                eng.wait_ge(suf_exp, b + 1)
                eng.tensor_tensor(KDE[:, b, :], KDE[:, b, :], kN[:, b, :], ALU.mult).then_inc(kd_ready, 1)

        HU = HG * NT

        def pe_hgrn(eng):
            eng.wait_ge(suf_exp, 3)
            eng.wait_ge(kd_ready, 3)
            eng.wait_ge(vp_free, 8)

            def decays(u):
                h, b = divmod(u, NT)
                if u:
                    eng.wait_ge(dec_exp, 2 * u)
                for half in range(2):
                    mm = eng.matmul(bank[half][:, :], LF[:, b, h * P:(h + 1) * P],
                                    span[:, half * 512:half * 512 + 512], start=True, stop=True)
                mm.then_inc(dec_ready, 1)

            def scores(u):
                h, b = divmod(u, NT)
                eng.wait_ge(q_dec, u + 1)
                eng.wait_ge(k_dec, u + 1)
                if u:
                    eng.wait_ge(a_mask, 2 * u)
                for l in range(LEVELS):
                    eng.matmul(bank[2 + l // 4][:, (l % 4) * P:(l % 4 + 1) * P], KL[:, u % 2, l, :],
                               QR[:, u % 2, l, :], start=True, stop=True, skip_group_check=True)
                eng.matmul(bank[3][:, 3 * P:4 * P], kT[:, h, b * P:(b + 1) * P],
                           projT[:, HQ + h, b * P:(b + 1) * P], start=True, stop=True,
                           skip_group_check=True).then_inc(a_ready, 1)

            def output(u):
                h, b = divmod(u, NT)
                eng.wait_ge(a_sum, u + 1)
                if b == 0 and h >= 2:
                    eng.wait_ge(hout, h - 1)
                o = bank[4 + h % 2][:, b * P:(b + 1) * P]
                mm = eng.matmul(o, HV[:, b, h * P:(h + 1) * P], scs[:, u % 2, :], start=True,
                                stop=(b == 0), skip_group_check=True)
                if b:
                    eng.wait_ge(st_ready, 3 * h + b)
                    mm = eng.matmul(o, ST[:, (b - 1) % 2, :], QR[:, u % 2, 7, :], start=False, stop=True,
                                    skip_group_check=True)
                mm.then_inc(ho_ready, 1)
                if b < NT - 1:
                    if 3 * h + b >= 1:
                        eng.wait_ge(st_ready, 3 * h + b)
                    eng.matmul(bank[7][:, 0:P], KDE[:, b, h * P:(h + 1) * P], HV[:, b, h * P:(h + 1) * P],
                               start=True, stop=True).then_inc(u_ready, 1)

            decays(0)
            for u in range(HU + 1):
                if u < HU:
                    if u + 1 < HU:
                        decays(u + 1)
                    scores(u)
                if u >= 1:
                    output(u - 1)
                    if (u - 1) % NT == NT - 1:
                        h = (u - 1) // NT
                        eng.wait_ge(hsq, h + 1)
                        eng.matmul(bank[6][:, :], onesD, sq[:, h % 2, :], start=True, stop=True).then_inc(hsum, 1)

        def act_hgrn(eng):
            for u in range(HU + 2):
                if u < HU:
                    eng.wait_ge(dec_ready, u + 1)
                    if u >= 2:
                        eng.wait_ge(q_dec, u - 1)
                        eng.wait_ge(k_dec, u - 1)
                        eng.wait_ge(st_ready, (u - 1) // NT * 3 + min((u - 1) % NT, 3))
                    for half in range(2):
                        eng.activation(E[:, u % 2, half * 512:half * 512 + 512], bank[half][:, :],
                                       ACT.Exp).then_inc(dec_exp, 1)
                if u >= 2 and (u - 2) % NT == NT - 1:
                    h = (u - 2) // NT
                    eng.wait_ge(ho_ready, 4 * (h + 1))
                    eng.activation(sq[:, h % 2, :], bank[4 + h % 2][:, :], ACT.Square).then_inc(hsq, 1)
                    eng.wait_ge(hsum, h + 1)
                    eng.activation(lnv, bank[6][:, :], ACT.Ln, bias=EPS_RMS, scale=D / P).then_inc(hrs, 1)
                    eng.wait_ge(hrs, 2 * h + 1)
                    if h:
                        eng.wait_ge(hout, h)
                    eng.activation(rs, lnv, ACT.Exp, scale=-0.5).then_inc(hrs, 1)

        def dve_hgrn(eng):
            eng.wait_ge(k_back, 4)

            def queries(u):
                h, b = divmod(u, NT)
                eng.wait_ge(dec_exp, 2 * u + 2)
                if u >= 2:
                    eng.wait_ge(ho_ready, u - 1)
                eng.tensor_tensor(QR[:, u % 2, :, :], E[:, u % 2, :].rearrange("p (l s) -> p l s", l=8),
                                  projT[:, HQ + h, b * P:(b + 1) * P].unsqueeze(1).broadcast_to([P, 8, P]),
                                  ALU.mult).then_inc(q_dec, 1)

            queries(0)
            for u in range(HU):
                h, b = divmod(u, NT)
                eng.wait_ge(a_ready, u + 1)
                if u:
                    eng.wait_ge(a_sum, u)
                for half in range(2):
                    eng.tensor_tensor(AM[:, half * 512:half * 512 + 512], bank[2 + half][:, :],
                                      lmask[:, half * 512:half * 512 + 512], ALU.mult).then_inc(a_mask, 1)
                if u + 1 < HU:
                    queries(u + 1)
                eng.wait_ge(a_mask, 2 * u + 2)
                if u >= 2:
                    eng.wait_ge(ho_ready, u - 1)
                eng.tensor_reduce(scs[:, u % 2, :], AM.rearrange("p (l s) -> p s l", l=8), AX_X,
                                  ALU.add).then_inc(a_sum, 1)
                if b < NT - 1:
                    eng.wait_ge(u_ready, 3 * h + b + 1)
                    if b == 0:
                        if h:
                            eng.wait_ge(ho_ready, 4 * h)
                        eng.tensor_copy(ST[:, 0, :], bank[7][:, 0:P]).then_inc(st_ready, 1)
                    else:
                        if b == 2:
                            eng.wait_ge(ho_ready, 4 * h + 2)
                        eng.wait_ge(st_ready, 3 * h + b)
                        eng.scalar_tensor_tensor(ST[:, b % 2, :], ST[:, (b - 1) % 2, :],
                                                 E[:, u % 2, 1023:1024], bank[7][:, 0:P],
                                                 ALU.mult, ALU.add).then_inc(st_ready, 1)
                if b == NT - 1:
                    eng.wait_ge(hrs, 2 * h + 2)
                    if h >= 2:
                        eng.wait_ge(hmix, h - 1)
                    eng.scalar_tensor_tensor(tmp[:, h % 2, :], bank[4 + h % 2][:, :], gwcol, rs,
                                             ALU.mult, ALU.mult).then_inc(hout, 1)

        def pool_hgrn(eng):
            def keys(u):
                h, b = divmod(u, NT)
                eng.wait_ge(dec_exp, 2 * u + 2)
                if u >= 2:
                    eng.wait_ge(a_ready, u - 1)
                eng.tensor_tensor(KL[:, u % 2, :, :], E[:, u % 2, 0:LEVELS * P].rearrange("p (l s) -> p l s", l=LEVELS),
                                  kT[:, h, b * P:(b + 1) * P].unsqueeze(1).broadcast_to([P, LEVELS, P]),
                                  ALU.mult).then_inc(k_dec, 1)

            def mix(h):
                eng.wait_ge(hout, h + 1)
                eng.wait_ge(silu_g, 4)
                eng.tensor_tensor(hT[:, h, :], tmp[:, h % 2, :], projT[:, HGT + h, :], ALU.mult).then_inc(hmix, 1)

            eng.wait_ge(k_back, 4)
            for u in range(HU):
                keys(u)
                if u >= NT and u % NT == 1:
                    mix(u // NT - 1)
            mix(HG - 1)

        sc.at = both_at
        p3 = sc.take(2 * 3 * S).rearrange("p (r w s) -> p r w s", r=2, w=3)
        probS = sc.take(4096)
        probC = sc.take(1024).rearrange("p (r s) -> p r s", r=2)
        st3 = sc.take(32)
        pT = [probS.rearrange("p (w j s) -> p w j s", w=2, j=NT), yflat.rearrange("p (w j s) -> p w j s", w=2, j=NT)]
        NU = NSA * NT

        def cw(i):
            return 8 * i + 7

        def pe_nsa(eng):
            eng.wait_ge(hout, 4)
            eng.wait_ge(c_done, 2)

            def scores(u):
                h, i = divmod(u, NT)
                g, hp = divmod(h, 4)
                lo = g * DH
                q = projT[lo:lo + DH, NQ + hp, i * P:(i + 1) * P]
                for w, (keys, n) in enumerate(((kcmp[lo:lo + DH, 0:cw(i)], cw(i)),
                                               (projT[lo:lo + DH, KSL, 0:(i + 1) * P], (i + 1) * P),
                                               (projT[lo:lo + DH, KWI, 0:(i + 1) * P], (i + 1) * P))):
                    if u:
                        eng.wait_ge(p_max, 3 * u + w - 2)
                    eng.matmul(bank[w][:, 0:n], q, keys, start=True, stop=True).then_inc(s_ready, 1)

            def turn(u):
                h, i = divmod(u, NT)
                for w in range(3):
                    eng.wait_ge(p_norm, 3 * u + w + 1)
                    if u:
                        eng.wait_ge(p_back, 3 * u + w - 2)
                    if w == 0:
                        mm = eng.transpose(bank[6][0:cw(i), 0:P], p3[:, u % 2, 0, 0:cw(i)], ident)
                    else:
                        for j in range(i + 1):
                            mm = eng.transpose(bank[2 + w][:, j * P:(j + 1) * P],
                                               p3[:, u % 2, w, j * P:(j + 1) * P], ident)
                    mm.then_inc(p_turn, 1)

            def pv(h):
                g, pair, lo = h // 4, h // 2, (h % 2) * DH
                eng.wait_ge(p_back, 12 * (h + 1))
                if h % 2 == 0 and pair >= 2:
                    eng.wait_ge(o_taken, pair - 1)
                o = bank[5 + 2 * (pair % 2)]
                for w in range(2):
                    for j in range(NT):
                        eng.matmul(o[lo:lo + DH, j * P:S], vg[:, j, w * P + g * DH:w * P + (g + 1) * DH],
                                   pT[h % 2][:, w, j, j * P:S], start=(w == 0 and j == 0), stop=False,
                                   skip_group_check=True)
                for i in range(NT):
                    mm = eng.matmul(o[lo:lo + DH, i * P:(i + 1) * P], vcmp[0:cw(i), g * DH:(g + 1) * DH],
                                    probC[0:cw(i), h % 2, i * P:(i + 1) * P], start=False, stop=(i == NT - 1),
                                    skip_group_check=True)
                mm.then_inc(o_ready, 1)

            scores(0)
            for u in range(NU + 1):
                if u + 1 < NU:
                    scores(u + 1)
                if u < NU:
                    turn(u)
                if u >= 1 and (u - 1) % NT == NT - 1:
                    pv((u - 1) // NT)

        def dve_gates(eng):
            eng.wait_ge(gate_ready, 1)
            g2d = gate.rearrange("p b n -> p (b n)")
            eng.tensor_scalar(g2d, g2d, 1.0, None, ALU.add).then_inc(p_rec, 1)
            eng.wait_ge(p_rec, 1)
            eng.reciprocal(g2d, g2d).then_inc(p_rec, 1)
            eng.wait_ge(p_rec, 2)
            eng.tensor_scalar(gate[:, 0, 0:8], gate[:, 0, 0:8], valid, None, ALU.mult).then_inc(p_rec, 1)
            eng.wait_ge(p_rec, 3)

        def dve_nsa(eng):
            rec = [3]
            for u in range(NU + 1):
                if u < NU:
                    h, i = divmod(u, NT)
                    n = (i + 1) * P
                    c0 = S - P - i * P + CMP_END
                    for w in range(3):
                        m = cw(i) if w == 0 else n
                        bias = tab2[:, h, c0:c0 + 16 * (m - 1) + 1:16] if w == 0 else tab2[:, h, S - n:S]
                        eng.wait_ge(s_ready, 3 * u + w + 1)
                        if u >= 2:
                            eng.wait_ge(p_turn, 3 * (u - 2) + w + 1)
                        a = (u % 2) * 3 + w
                        eng.tensor_tensor_reduce(p3[:, u % 2, w, 0:m], bank[w][:, 0:m], bias, 1.0, 3.0e38,
                                                 ALU.add, ALU.min, st3[:, a:a + 1]).then_inc(p_max, 1)
                if u >= 1:
                    v = u - 1
                    h, i = divmod(v, NT)
                    a = (v % 2) * 3
                    eng.wait_ge(p_exp, 3 * v + 3)
                    eng.reciprocal(st3[:, 16 + a:19 + a], st3[:, 8 + a:11 + a]).then_inc(p_rec, 1)
                    eng.wait_ge(p_rec, rec[0] + 1)
                    eng.tensor_tensor(st3[:, 24 + a:27 + a], st3[:, 16 + a:19 + a],
                                      gate[:, i, h:h + 17:8], ALU.mult).then_inc(p_rec, 1)
                    eng.wait_ge(p_rec, rec[0] + 2)
                    rec[0] += 2
                    for w in range(3):
                        m = cw(i) if w == 0 else (i + 1) * P
                        x = p3[:, v % 2, w, 0:m]
                        eng.tensor_scalar(x, x, st3[:, 24 + a + w:25 + a + w], None, ALU.mult).then_inc(p_norm, 1)

        def act_nsa(eng):
            def back(u):
                h, i = divmod(u, NT)
                if i == 0 and h >= 2:
                    eng.wait_ge(o_ready, h - 1)
                for w in range(3):
                    eng.wait_ge(p_turn, 3 * u + w + 1)
                    if w == 0:
                        eng.activation(probC[0:cw(i), h % 2, i * P:(i + 1) * P], bank[6][0:cw(i), 0:P],
                                       ACT.Copy).then_inc(p_back, 1)
                    else:
                        eng.activation(pT[h % 2][:, w - 1, 0:i + 1, i * P:(i + 1) * P],
                                       bank[2 + w][:, 0:(i + 1) * P].rearrange("p (j s) -> p j s", j=i + 1),
                                       ACT.Copy).then_inc(p_back, 1)

            for u in range(NU + 2):
                if u < NU:
                    i = u % NT
                    for w in range(3):
                        m = cw(i) if w == 0 else (i + 1) * P
                        a = (u % 2) * 3 + w
                        eng.wait_ge(p_max, 3 * u + w + 1)
                        eng.activation(p3[:, u % 2, w, 0:m], p3[:, u % 2, w, 0:m], ACT.Exp, scale=-1.0,
                                       bias=st3[:, a:a + 1], accum_out=st3[:, 8 + a:9 + a]).then_inc(p_exp, 1)
                if 1 <= u <= NU:
                    back(u - 1)
                if u >= 2 and (u - 2) % (2 * NT) == 2 * NT - 1:
                    pair = (u - 2) // (2 * NT)
                    eng.wait_ge(o_ready, 2 * pair + 2)
                    eng.activation(hT[:, HG + pair, :], bank[5 + 2 * (pair % 2)][:, :], ACT.Copy).then_inc(o_taken, 1)

        def dve_sum(eng, q, n1, per_tile, m, i=0, per=0):
            eng.wait_ge(slots_done, i * (per * per_tile) + (n1 + per_tile * (m + 1)))
            if per == 0:
                x, y = xT[:, m, :], yT[:, m, :]
            else:
                x, y = (v[:, bass.ds(i * per + m, 1), :].rearrange("p a s -> p (a s)") for v in (xT, yT))
            eng.scalar_tensor_tensor(y, x, ALPHA, bank[4 + m % 2][:, :], ALU.mult, ALU.add).then_inc(y_done, 1)

        def dve_ln(eng, q, g, b):
            eng.wait_ge(y_summed, 8 * q + 8)
            for m in range(KD):
                eng.tensor_tensor(yT[:, m, :], yT[:, m, :], bank[6][:, :], ALU.subtract).then_inc(c_ready, 1)
            eng.wait_ge(rs_ready, q + 1)
            for m in range(KD):
                if 8 * q + m >= 2:
                    eng.wait_ge(x_ready, 8 * q + m - 1)
                eng.scalar_tensor_tensor(tmp[:, m % 2, :], yT[:, m, :], g[:, m:m + 1], rs,
                                         ALU.mult, ALU.mult).then_inc(t_ready, 1)

        def pool_ln(eng, q, b):
            for m in range(KD):
                eng.wait_ge(t_ready, 8 * q + m + 1)
                eng.tensor_scalar(xT[:, m, :], tmp[:, m % 2, :], b[:, m:m + 1], None, ALU.add).then_inc(x_ready, 1)

        def act_ln(eng, q):
            for m in range(KD):
                eng.wait_ge(c_ready, 8 * q + m + 1)
                eng.wait_ge(sq_used, 8 * q + m + 1)
                eng.activation(sq[:, m % 2, :], yT[:, m, :], ACT.Square).then_inc(sq_ready, 1)
            act_root(eng, q, EPS_LN, 7)

        with nc.Block() as block:
            @block.sync
            def _(sp):
                sp.sem_clear(io)
        with nc.Block() as block:
            onehot = scr[0:33, mixer_at:mixer_at + 640]
            rb = scr[0:33, mixer_at + 640:mixer_at + 648]
            rows8 = scr[0:8, mixer_at + 648:mixer_at + 1288]
            flip = scr[:, mixer_at + 1288:mixer_at + 1288 + P]
            turned = scr[:, mixer_at + 2000:mixer_at + 2000 + NSA * S].rearrange("p (h s) -> p h s", h=NSA)

            @block.sync
            def _(sp):
                sp.dma_start(onehot, t["onehot"]).then_inc(io, 16)
                sp.dma_start(rb[0:32, :], t["rel_bias"]).then_inc(io, 16)
                sp.dma_start(rb[32:33, :], t["one8"]).then_inc(io, 16)
                sp.dma_start(table[:, 4096:6144], t["table2"]).then_inc(io, 16)
                sp.dma_start(valid, t["valid"]).then_inc(io, 16)
                sp.dma_start(flip, t["flip"]).then_inc(io, 16)
                sp.wait_ge(c_done, 2)
                sp.dma_start(t["spread"], rows8).then_inc(w_in1, 16)
                sp.wait_ge(w_in1, 16)
                sp.dma_start(turned, bass.AP(tensor=t["spread"].tensor, offset=0,
                                             ap=[[1, P], [640, NSA], [1, S]])).then_inc(par_in, 16)
                sp.wait_ge(par_in, 16)

            @block.tensor
            def _(pe):
                pe.wait_ge(io, 96)
                for n, c in enumerate((0, 320)):
                    pe.matmul(bank[n][0:8, 0:320], rb, onehot[:, c:c + 320], start=True, stop=True).then_inc(c_out, 1)
                pe.wait_ge(par_in, 16)
                for h in range(NSA):
                    if h == 0:
                        pe.wait_ge(c_done, 2)
                    if h >= 2:
                        pe.wait_ge(c_done, 2 + h - 1)
                    pe.matmul(bank[h % 2][:, :], flip, turned[:, h, :], start=True, stop=True).then_inc(c_out, 1)

            @block.vector
            def _(dve):
                for n, c in enumerate((0, 320)):
                    dve.wait_ge(c_out, n + 1)
                    dve.tensor_copy(rows8[:, c:c + 320], bank[n][0:8, 0:320]).then_inc(c_done, 1)
                for h in range(NSA):
                    dve.wait_ge(c_out, 2 + h + 1)
                    dve.tensor_copy(tab2[:, h, :], bank[h % 2][:, :]).then_inc(c_done, 1)

        with nc.Block() as block:
            @block.sync
            def _(sp):
                for s in nsem.values():
                    sp.sem_clear(s)

        n_in2, n_vg, n_out2, n_ffn2 = 0, 24, 26, 34
        with nc.Fori(0, DEPTH) as layer:
            def of_layer(name):
                return t[name][bass.ds(layer, 1), :, :].rearrange("a p n -> (a p) n")

            with nc.Block() as block:
                @block.sync
                def _(sp):
                    sp.dma_start(par, of_layer("par2")).then_inc(par_in, 16)
                    sp.dma_start(flags, of_layer("flags")).then_inc(par_in, 16)
                    sp.dma_start(kT[:, 2:4, :], of_layer("lbp")).then_inc(par_in, 16)
                    stream(sp, layer, t["w8_2"], 0, 24, n_in2, NARROW)
                    sp.dma_start(w1k, of_layer("w1k")).then_inc(w_in1, 16)
                    sp.dma_start(w1v, of_layer("w1v")).then_inc(w_in1, 16)
                    stream(sp, layer, t["vg_2"], 0, 2, n_vg, 4 * VG)
                    stream(sp, layer, t["w8_2"], 24, KD, n_out2, NARROW)
                    stream(sp, layer, t["w8_2"], 24 + KD, A, n_ffn2, NARROW)
                    stream(sp, layer, t["w11_2"], 0, 2 * KD, n_ffn2 + A, WIDE)

                @block.tensor
                def _(pe):
                    pe_proj_T(pe, n_in2, 16, xT)
                    pe_proj_N(pe, n_in2 + 16, 0, xT)
                    pe_proj_N(pe, n_in2 + 20, 1, xT)
                    pe_proj_N(pe, n_vg, 2, xT, VG, 4, 2)
                    pe_compress(pe)
                    pe.wait_ge(vp_free, 12)
                    pe.wait_ge(c_done, 2)
                    pe_hgrn_keys(pe)
                    pe_hgrn(pe)
                    pe_nsa(pe)
                    pe.wait_ge(o_taken, 4)
                    pe.wait_ge(hmix, 4)
                    pe_out(pe, n_out2, ln_free(0), ln_add(0))
                    for m in range(KD):
                        sum_square(pe, 0, m, on=7)
                    pe.wait_ge(x_ready, 8)
                    pe_ffn(pe, 0, n_ffn2, xT, ln_free(1), ln_add(1))
                    for m in range(KD):
                        sum_square(pe, 1, m, on=7)

                @block.scalar
                def _(act):
                    act_proj_T(act, n_in2, [1.0] * 8 + [-DH ** -0.5] * 4 + [1.0] * 4)
                    act.wait_ge(vp_free, 12)
                    act.activation(gate, vg[:, :, 256:280], ACT.Exp, scale=-1.0).then_inc(gate_ready, 1)
                    act_compress(act)
                    act_forget(act)
                    for h in range(HG):
                        act.activation(projT[:, HGT + h, :], projT[:, HGT + h, :], ACT.Silu).then_inc(silu_g, 1)
                    act_hgrn_keys(act)
                    act_hgrn(act)
                    act_nsa(act)
                    act_ln(act, 0)
                    act_silu(act, 0, n_ffn2)
                    act_ln(act, 1)

                @block.vector
                def _(dve):
                    dve.sem_inc(g_free, 2)
                    dve.sem_inc(sq_used, 2)
                    dve.sem_inc(y_done, 2)
                    dve.wait_ge(par_in, 48)
                    dve_windows(dve)
                    dve_proj_N(dve, n_in2 + 16, 0, LF)
                    dve_proj_N(dve, n_in2 + 20, 1, HV)
                    dve_proj_N(dve, n_vg, 2, vg, VG, 2)
                    dve_compress(dve)
                    dve_forget(dve)
                    dve_gates(dve)
                    dve_hgrn_keys(dve)
                    dve_hgrn(dve)
                    dve_nsa(dve)
                    for m in range(KD):
                        dve_sum(dve, 0, n_out2, 1, m)
                    dve_ln(dve, 0, g1, b1)
                    dve_ffn(dve, 0, n_ffn2)
                    with dve.Fori(0, KD // 2) as i:
                        for m in range(2):
                            dve_sum(dve, 1, n_ffn2 + A, 2, m, i, 2)
                    dve_ln(dve, 1, g2, b2)

                @block.gpsimd
                def _(pool):
                    pool_hgrn(pool)
                    pool_ln(pool, 0, b1)
                    pool_ln(pool, 1, b2)

            with nc.Block() as block:
                @block.sync
                def _(sp):
                    for s in nsem.values():
                        sp.sem_clear(s)

        with nc.Block() as block:
            @block.sync
            def _(sp):
                sp.dma_start(t["out"], xT[:, :, :]).then_inc(io, 16)
                sp.wait_ge(io, 16)


def alibi(n):
    return 2.0 ** (-8.0 * np.arange(1, n + 1, dtype=np.float32) / np.float32(n))


def constants():
    p = np.arange(P)[:, None]
    c = np.arange(S)[None, :]
    dist = p + (S - P) - c
    count = (dist <= 128).astype(np.int64) + (dist % 4 == 0) + (dist % 16 == 0)
    mult = np.where((dist >= 0) & (count > 0), count, 1)
    dil = [np.where((dist >= 0) & (count > 0), sl * dist - np.log(mult), BIG) for sl in alibi(DIL)]
    dif = [np.where(dist >= 0, sl * dist, BIG) for sl in alibi(DIFF)]
    table1 = np.stack(dil + dif, 1).reshape(P, -1).astype(np.float32)
    j, k = np.arange(P)[:, None], np.arange(P)[None, :]
    mats = np.zeros((7, P, P), np.float32)
    mats[0] = -1.0
    mats[1] = 1.0 / D
    mats[2] = (j // DH == k // DH) / DH
    mats[3] = -1.0 * (j >= k)
    mats[4] = np.eye(P)
    mats[5] = j > k
    mats[6] = np.where(j >= k, -BIG, 0.0)
    return table1, np.ascontiguousarray(mats.transpose(1, 0, 2))


def columns(w):
    k, n = w.shape
    return w.reshape(k // P, P, n // P, P).transpose(2, 1, 0, 3).reshape(n // P, P, k)


def rows(w, width, per):
    k, n = w.shape
    return w.reshape(k // P // per, per, P, width).transpose(0, 2, 1, 3).reshape(-1, P, per * width)


def halves(w):
    return w.reshape(2, KF // 2, P, KD, P).transpose(3, 0, 2, 1, 4).reshape(2 * KD, P, WIDE)


def gate_up(g, u):
    return np.stack([columns(g), columns(u)], 1).reshape(2 * KF, P, NARROW)


def by_partition(v):
    return v.reshape(-1, KD, P).transpose(2, 0, 1).reshape(P, -1)


def laid_out(x, norm_gains, w_ffn_gate, w_ffn_up, w_ffn_down, w_in, w_out, diff_lambda, diff_subln_gain, **second):
    a = {}
    a["xT"] = x[0].T.reshape(KD, P, S).transpose(1, 0, 2)
    a["table1"], a["mats"] = constants()
    w8, w11 = [], []
    for l in range(DEPTH):
        c = np.cumsum([0, 384, 384, 384, 256, 256, 256, 384, 384, 384])
        part = [w_in[l][:, c[i]:c[i + 1]] for i in range(9)]
        qk = np.concatenate([part[i] for i in (0, 1, 3, 4, 6, 7)], 1)
        v = np.concatenate([part[i] for i in (2, 5, 8)], 1)
        w8 += [gate_up(w_ffn_gate[l, 0], w_ffn_up[l, 0]), columns(qk), rows(v[:, :512], 512, 2),
               rows(v[:, 512:], 512, 2), columns(w_out[l]), gate_up(w_ffn_gate[l, 1], w_ffn_up[l, 1])]
        w11 += [halves(w_ffn_down[l, 0]), halves(w_ffn_down[l, 1])]
    a["w8_1"] = np.concatenate(w8).reshape(DEPTH, -1, P, NARROW)
    a["w11_1"] = np.concatenate(w11).reshape(DEPTH, -1, P, WIDE)
    a["gains1"] = np.stack([by_partition(norm_gains[l]) for l in range(DEPTH)])
    init = [0.8 - 0.6 * math.exp(-0.3 * l) for l in range(DEPTH)]
    lam = diff_lambda[:, [0, 2, 1, 3], :].reshape(DEPTH, 1, 128)
    tail = np.array(init, np.float32).reshape(DEPTH, 1, 1)
    a["lam"] = np.broadcast_to(np.concatenate([lam, tail], 2), (DEPTH, P, 129))
    gain = np.concatenate([diff_subln_gain] * 2, 1)[:, :, None]
    keep = np.broadcast_to(np.array([1.0 - i for i in init], np.float32).reshape(DEPTH, 1, 1), (DEPTH, P, 1))
    a["subg"] = np.concatenate([gain, keep], 2)
    laid_out_2(a, **second)
    return {k: np.ascontiguousarray(v) for k, v in a.items()}


def bucket(n):
    exact = 16
    nf = np.maximum(n, 1).astype(np.float32)
    large = exact + (np.log(nf / np.float32(exact)) / np.float32(math.log(128 / exact)) * np.float32(16)).astype(np.int32)
    return np.where(n < exact, np.maximum(n, 0), np.minimum(large, 31))


def constants_2():
    x = np.arange(640)
    dist = S - 1 - x
    onehot = np.zeros((33, 640), np.float32)
    seen = dist >= 0
    onehot[bucket(dist)[seen], x[seen]] = -1.0
    onehot[32, ~seen] = BIG
    s, u = np.arange(P)[:, None], np.arange(P)[None, :]
    span, mask = np.zeros((P, 8, P), np.float32), np.zeros((P, 8, P), np.float32)
    for l in range(LEVELS):
        half = (P // 2) >> l
        mid = u // (2 * half) * (2 * half) + half
        right = u >= mid
        span[:, l] = np.where(right, (s >= mid) & (s <= u), (s > u) & (s < mid))
        mask[:, l] = right & (s // (2 * half) == u // (2 * half)) & (s < mid)
    span[:, 7] = s <= u
    mask[:, 7] = s == u
    return onehot, np.concatenate([span.reshape(P, -1), mask.reshape(P, -1)], 1)


def laid_out_2(a, w_in_2, hg_lb_param_2, hg_norm_w_2, cmp_pos_k_2, cmp_w1_k_2, cmp_w2_k_2, cmp_pos_v_2,
               cmp_w1_v_2, cmp_w2_v_2, rel_bias_2, w_out_2, ln1_g_2, ln1_b_2, w_ffn_gate_2,
               w_ffn_up_2, w_ffn_down_2, ln2_g_2, ln2_b_2):
    a["onehot"], a["table2"] = constants_2()
    a["rel_bias"] = rel_bias_2
    a["flip"] = np.eye(P, dtype=np.float32)[::-1]
    a["one8"] = np.ones((1, NSA), np.float32)
    a["valid"] = (np.arange(P) >= CMP_END).astype(np.float32)[:, None]
    w8, w11, vg, w1, par = [], [], [], {"k": [], "v": []}, []
    order = [h * DH + g * 4 * DH + d for h in range(4) for g in range(2) for d in range(DH)]
    for l in range(DEPTH):
        c = np.cumsum([0, 512, 512, 512, 512, 512] + [128] * 6 + [24])
        hq, hf, hi, hg, nq, kc, vc, ks, vs, kw, vw, gt = (w_in_2[l][:, c[i]:c[i + 1]] for i in range(12))
        turned = np.concatenate([hq, hg, nq[:, order], kc, vc, ks, kw], 1)
        w8 += [columns(turned), rows(hf, 512, 2), rows(hi, 512, 2), columns(w_out_2[l]),
               gate_up(w_ffn_gate_2[l], w_ffn_up_2[l])]
        vg.append(rows(np.concatenate([vs, vw, gt], 1), VG, 4))
        w11.append(halves(w_ffn_down_2[l]))
        for kind, w in (("k", cmp_w1_k_2), ("v", cmp_w1_v_2)):
            v = w[l].reshape(32, DH, P).transpose(1, 0, 2).reshape(DH, -1)
            w1[kind].append(np.concatenate([v, v], 0))
        pos = [np.concatenate([p[l].T] * 2, 0) for p in (cmp_pos_k_2, cmp_pos_v_2)]
        par.append(np.concatenate(pos + [cmp_w2_k_2[l], cmp_w2_v_2[l], hg_norm_w_2[l][:, None]]
                                  + [by_partition(v[l]) for v in (ln1_g_2, ln1_b_2, ln2_g_2, ln2_b_2)], 1))
    a["w8_2"] = np.concatenate(w8).reshape(DEPTH, -1, P, NARROW)
    a["w11_2"] = np.concatenate(w11).reshape(DEPTH, -1, P, WIDE)
    a["vg_2"] = np.concatenate(vg).reshape(DEPTH, -1, P, 4 * VG)
    a["w1k"], a["w1v"] = np.stack(w1["k"]), np.stack(w1["v"])
    a["par2"] = np.stack(par)
    a["flags"] = np.broadcast_to(np.array([[[0, 0, -BIG, 0]], [[1, -1, 0, 0]]], np.float32), (DEPTH, P, 4))
    a["lbp"] = np.broadcast_to(hg_lb_param_2.reshape(1, 1, DEPTH * 512), (DEPTH, P, DEPTH * 512))


def kernel(**inputs):
    import concourse.bacc as bacc
    from concourse.bass_utils import run_bass_kernel_spmd

    arrays = laid_out(**{k: np.asarray(v) for k, v in inputs.items()})
    nc = bacc.Bacc("TRN2", target_bir_lowering=False, num_devices=1)
    t = {k: nc.dram_tensor("in_" + k, v.shape, mybir.dt.from_np(v.dtype), kind="ExternalInput").ap()
         for k, v in arrays.items()}
    t["spread"] = nc.dram_tensor("spread", (NSA, 640), F32).ap()
    t["out"] = nc.dram_tensor("out", (P, KD, S), F32, kind="ExternalOutput").ap()
    build(nc, t)
    r = run_bass_kernel_spmd(nc, [{"in_" + k: v for k, v in arrays.items()}], core_ids=[0])
    out = r.results[0]["out"]
    return np.ascontiguousarray(out.transpose(1, 0, 2).reshape(D, S).T)[None]
```

```python
from contextlib import ExitStack
import math

import numpy as np

import concourse.bass as bass
from concourse import mybir

F32 = mybir.dt.float32
F32R = mybir.dt.float32r
BF16 = mybir.dt.bfloat16
ALU = mybir.AluOpType
ACT = mybir.ActivationFunctionType
AX_X = mybir.AxisListType.X

P = 128
S = 512
NT = S // P
D = 1024
KD = D // P
FF = 2816
KF = FF // P
DEPTH = 2
NSLOT = 2
WIDE = KD * P
DOWN = (8, 7, 7)
assert sum(DOWN) == KF
BIG = 1e30
EPS_RMS = 1e-6
EXP_LN = "natural_log_exp_and_others"
EPS_LN = 1e-5
ALPHA = (2.0 * DEPTH) ** 0.25

DIL, DIFF, SB = 6, 4, 6
DH = 64
QA, KA, QB, KB, QC, KC = 0, 3, 6, 8, 10, 13
HG = 4
NSA = 8
LEVELS = 7
CMP_END = 31
NCMP = 31
VG = 280
VG_ROWS = (3, 3, 2)


class Layout:

    def __init__(self, tensor, width):
        self.tensor, self.width, self.at = tensor, width, 0

    def take(self, n):
        a = self.at
        self.at += n
        assert self.at <= self.width, (self.at, self.width)
        return self.tensor[:, a:self.at]


def triangle(a):
    return [0, 512, 896, 1152][a]


def build(nc, t):
    ctx = ExitStack()
    with ctx:
        def sb(name, shape, dt=F32):
            return ctx.enter_context(nc.sbuf_tensor(name, shape, dt))

        bank = [ctx.enter_context(nc.psum_tensor(f"bank{i}", [P, 512], F32)) for i in range(8)]
        base = -(-nc.sbuf_base // 64) * 64

        def at(name, floats, shape, dt=F32):
            n = int(np.prod(shape[1:])) * (2 if dt == BF16 else 4)
            assert base + 4 * floats + n <= nc.sbuf_usable_end, name
            return nc.alloc_sbuf_tensor_at(name, shape, dt, offset=base + 4 * floats)

        xT = at("xT", 0, [P, KD, S])
        yT = at("yT", 4096, [P, KD, S])
        hH = at("hH", 8192, [P, KD, S], F32R)
        hL = at("hL", 12288, [P, KD, S], F32R)
        ring = at("ring", 16384, [P, NSLOT, WIDE])
        wH = at("wH", 18432, [P, NSLOT, WIDE], F32R)
        wL = at("wL", 20480, [P, NSLOT, WIDE], F32R)
        work = at("work", 22528, [P, 3072])
        small = at("small", 25600, [P, 512])
        mats = at("mats", 26112, [P, 7, P])
        matsb = at("matsb", 27008, [P, 2, P], BF16)
        M = 27136
        guH = at("guH", M, [P, KF, S], F32R)
        guL = at("guL", M + KF * S, [P, KF, S], F32R)
        gfull = at("gfull", M + 2 * KF * S, [P, 2, S])
        MW = (nc.sbuf_usable_end - base) // 4 - M
        mix = at("mix", M, [P, MW])
        projT = mix[:, 0:16 * S].rearrange("p (c s) -> p c s", c=16)

        nsem = {}

        def sem(name):
            nsem[name] = ctx.enter_context(nc.semaphore(name))
            return nsem[name]

        slot_in = [sem(f"slot_in{i}") for i in range(NSLOT)]
        w_hi = sem("w_hi")
        w_lo = sem("w_lo")
        slots_done = sem("slots_done")
        f_ready = sem("f_ready")
        h_hi = sem("h_hi")
        gsteps = sem("gsteps")
        o_hi = sem("o_hi")
        tab_in = sem("tab_in")
        g_free = sem("g_free")
        silu_ready = sem("silu_ready")
        sq_ready = sem("sq_ready")
        sq_used = sem("sq_used")
        ln_ready = sem("ln_ready")
        rs_ready = sem("rs_ready")
        t_ready = sem("t_ready")
        x_ready = sem("x_ready")
        h_ready = sem("h_ready")
        par_in = sem("par_in")
        par_ready = sem("par_ready")
        seq = sem("seq")
        io = sem("io")
        const_in = sem("const_in")
        tp_free = sem("tp_free")
        vp_free = sem("vp_free")
        s_ready = sem("s_ready")
        p_max = sem("p_max")
        p_exp = sem("p_exp")
        p_rec = sem("p_rec")
        p_norm = sem("p_norm")
        p_turn = sem("p_turn")
        p_back = sem("p_back")
        o_ready = sem("o_ready")
        o_taken = sem("o_taken")
        z_ready = sem("z_ready")
        z_abs = sem("z_abs")
        z_exp = sem("z_exp")
        z_ln = sem("z_ln")
        z_sp = sem("z_sp")
        z_cum = sem("z_cum")
        z_w = sem("z_w")
        z_pv = sem("z_pv")
        d_sq = sem("d_sq")
        d_sum = sem("d_sum")
        d_rs = sem("d_rs")
        d_out = sem("d_out")
        y_done = sem("y_done")
        y_summed = sem("y_summed")
        c_ready = sem("c_ready")
        w_in1 = sem("w_in1")
        win = sem("win")
        c_hid = sem("c_hid")
        c_act = sem("c_act")
        c_out = sem("c_out")
        c_done = sem("c_done")
        f_act = sem("f_act")
        f_dve = sem("f_dve")
        k_turn = sem("k_turn")
        k_back = sem("k_back")
        suf_ready = sem("suf_ready")
        suf_exp = sem("suf_exp")
        kd_ready = sem("kd_ready")
        dec_ready = sem("dec_ready")
        dec_exp = sem("dec_exp")
        q_dec = sem("q_dec")
        k_dec = sem("k_dec")
        a_ready = sem("a_ready")
        a_mask = sem("a_mask")
        a_sum = sem("a_sum")
        u_ready = sem("u_ready")
        st_ready = sem("st_ready")
        ho_ready = sem("ho_ready")
        hsq = sem("hsq")
        hsum = sem("hsum")
        hrs = sem("hrs")
        hout = sem("hout")
        hmix = sem("hmix")
        silu_g = sem("silu_g")
        gate_ready = sem("gate_ready")

        sc = Layout(work, 3072)
        sq = sc.take(2 * S).rearrange("p (b s) -> p b s", b=2)
        lnv = sc.take(S)
        rs = sc.take(S)
        tmp = sc.take(2 * S).rearrange("p (b s) -> p b s", b=2)

        OFF, ONES, BLK, NEGL, IDENT, SUF, MASK = 0, 1, 2, 3, 4, 5, 6
        onesD, blk64, negL, ident, negones = (mats[:, i, :] for i in (ONES, BLK, NEGL, IDENT, OFF))

        def slot_sem(eng, n, i=0, per=0):
            eng.wait_ge(slot_in[n % NSLOT], i * (16 * per // NSLOT) + 16 * (n // NSLOT + 1))

        def landed(eng, n, i=0, per=0):
            eng.wait_ge(w_lo, i * per + (n + 1))

        def product(eng, out, n, c0, c1, hi, lo, first, last):
            a, b = wH[:, n % NSLOT, c0:c1], wL[:, n % NSLOT, c0:c1]
            eng.matmul(out, a, hi, start=first, stop=False)
            eng.matmul(out, a, lo, start=False, stop=False)
            return eng.matmul(out, b, hi, start=False, stop=last)

        def load(eng, n, src, width, i=0, per=0):
            if per or n >= NSLOT:
                eng.wait_ge(w_lo, i * per + (n - NSLOT + 1))
            eng.dma_start(ring[:, n % NSLOT, 0:width], src).then_inc(slot_in[n % NSLOT], 16)

        def stream(eng, layer, arr, first, count, n0, width):
            def src(k):
                return arr[bass.ds(layer, 1), bass.ds(k, 1), :, 0:width].rearrange("a b p n -> (a b p) n")
            head = max(0, NSLOT - n0)
            for k in range(head):
                load(eng, n0 + k, src(first + k), width)
            loops = (count - head) // NSLOT
            if loops:
                with eng.Fori(0, loops) as i:
                    for k in range(head, head + NSLOT):
                        load(eng, n0 + k, src(i * NSLOT + (first + k)), width, i, NSLOT)
            for k in range(head + loops * NSLOT, count):
                load(eng, n0 + k, src(first + k), width)

        def stream_down(eng, layer, arr, first, n0):
            with eng.Fori(0, KD // 2) as i:
                for k in range(6):
                    w = DOWN[k % 3] * P
                    load(eng, n0 + k, arr[bass.ds(layer, 1), bass.ds(i * 6 + (first + k), 1), :, 0:w]
                         .rearrange("a b p n -> (a b p) n"), w, i, 6)

        def hi(eng, n, width=WIDE, i=0, per=0):
            if n >= total_slots[0]:
                return
            slot_sem(eng, n, i, per)
            if per or n >= NSLOT:
                eng.wait_ge(slots_done, i * per + (n - NSLOT + 1))
            eng.activation(wH[:, n % NSLOT, 0:width], ring[:, n % NSLOT, 0:width], ACT.Copy).then_inc(w_hi, 1)

        def lo(eng, n, width=WIDE, i=0, per=0):
            if n >= total_slots[0]:
                return
            eng.wait_ge(w_hi, i * per + (n + 1))
            eng.tensor_tensor(wL[:, n % NSLOT, 0:width], ring[:, n % NSLOT, 0:width],
                              wH[:, n % NSLOT, 0:width], ALU.subtract).then_inc(w_lo, 1)

        total_slots = [0]
        widths = []

        def width(n):
            return widths[n] if n < len(widths) else WIDE

        def los(eng, a, b):
            for n in range(a, b):
                lo(eng, n, width(n))

        def sum_square(eng, q, m, i=0, per=0, on=6):
            eng.wait_ge(sq_ready, i * per + (8 * q + m + 1))
            eng.matmul(bank[on][:, :], onesD, sq[:, m % 2, :], start=(m == 0 and per == 0),
                       stop=(m == KD - 1), skip_group_check=True).then_inc(sq_used, 1)

        def act_root(eng, q, eps, on=6):
            eng.wait_ge(sq_used, 8 * q + 8 + 2)
            eng.activation(lnv, bank[on][:, :], ACT.Ln, bias=eps).then_inc(ln_ready, 1)
            eng.wait_ge(ln_ready, q + 1)
            eng.activation(rs, lnv, ACT.Exp, scale=-0.5).then_inc(rs_ready, 1)

        def act_square_x(eng, q, xr):
            for m in range(KD):
                if xr is not None:
                    eng.wait_ge(x_ready, xr + m + 1)
                eng.wait_ge(sq_used, 8 * q + m + 1)
                eng.activation(sq[:, m % 2, :], xT[:, m, :], ACT.Square).then_inc(sq_ready, 1)

        def pe_ffn(eng, c, n0, h0, free, add):
            def tiles(i, dyn):
                for k in range(2):
                    eng.wait_ge(g_free, i * 2 + (KF * c + k + 1))
                    for u in range(2):
                        n = n0 + 2 * k + u
                        landed(eng, n, i, 4)
                        for kc in range(KD):
                            if not dyn and k == u == 0:
                                eng.wait_ge(h_ready, h0 + kc + 1)
                            mm = product(eng, bank[k + 2 * u][:, :], n, kc * P, (kc + 1) * P,
                                         hH[:, kc, :], hL[:, kc, :], kc == 0, kc == KD - 1)
                        mm.then_inc(slots_done, 1)

            tiles(0, False)
            with eng.Fori(1, KF // 2) as i:
                tiles(i, True)
            eng.wait_ge(g_free, KF * (c + 1) + 2)
            n1 = n0 + 2 * KF

            def down(m, i=0, per=0):
                free(eng, m, i, per)
                kc = 0
                for s, tiles_ in enumerate(DOWN):
                    n = n1 + 3 * m + s
                    landed(eng, n, i, 3 * per)
                    for b in range(tiles_):
                        mm = product(eng, bank[4 + m % 2][:, :], n, b * P, (b + 1) * P,
                                     guH[:, kc, :], guL[:, kc, :], kc == 0, kc == KF - 1)
                        kc += 1
                    mm.then_inc(slots_done, 1)

            down(0)
            down(1)
            add(eng, 0)
            down(2)
            with eng.Fori(0, 2) as i:
                add(eng, 1, i, 2)
                down(3, i, 2)
                add(eng, 2, i, 2)
                down(4, i, 2)
            add(eng, 5)
            down(7)
            add(eng, 6)
            add(eng, 7)

        def rms_free(q):
            def wait(eng, m, i=0, per=0):
                eng.wait_ge(sq_ready, i * per + (8 * q + m - 1))
            return wait

        def rms_add(q):
            return lambda eng, m, i=0, per=0: sum_square(eng, q, m, i, per)

        def ln_free(q):
            def wait(eng, m, i=0, per=0):
                eng.wait_ge(y_done, i * per + (8 * q + m + 1))
            return wait

        def ln_add(q):
            def add(eng, m, i=0, per=0):
                eng.wait_ge(y_done, i * per + (8 * q + m + 1 + 2))
                src = yT[:, m, :] if per == 0 else yT[:, bass.ds(i * per + m, 1), :].rearrange("p a s -> p (a s)")
                eng.matmul(bank[6][:, :], onesD, src, start=(m == 0), stop=(m == KD - 1),
                           skip_group_check=True).then_inc(y_summed, 1)
            return add

        def act_y(eng, q, n1, per_tile, m, i=0, per=0):
            eng.wait_ge(slots_done, i * (per * per_tile) + (n1 + per_tile * (m + 1)))
            dst = yT[:, m, :] if per == 0 else yT[:, bass.ds(i * per + m, 1), :].rearrange("p a s -> p (a s)")
            eng.activation(dst, bank[4 + m % 2][:, :], ACT.Copy)
            eng.wait_ge(sq_used, i * per + (8 * q + m + 1))
            eng.activation(sq[:, m % 2, :], bank[4 + m % 2][:, :], ACT.Square).then_inc(sq_ready, 1)

        def act_silu(eng, c, n0):
            eng.preload_act_table(ACT.Silu)
            with eng.Fori(0, KF // 2) as i:
                for k in range(2):
                    eng.wait_ge(g_free, i * 2 + (KF * c + k + 1))
                    eng.wait_ge(slots_done, i * 4 + (n0 + 2 * k + 1))
                    eng.activation(tmp[:, k, :], bank[k][:, :], ACT.Silu).then_inc(silu_ready, 1)
                    hi(eng, n0 + 2 * k + 2, WIDE, i, 4)
                    hi(eng, n0 + 2 * k + 3, WIDE, i, 4)
            eng.preload_act_table_set(EXP_LN)

        def pool_silu(eng, n0):
            with eng.Fori(0, KF // 2) as i:
                for k in range(4):
                    lo(eng, n0 + 2 + k, WIDE, i, 4)

        def act_down(eng, n1, take):
            def pair(i, per):
                for m in range(2):
                    for s in range(3):
                        hi(eng, n1 + 3 * m + s + 2, WIDE, i, 3 * per)
                    take(m, i, per)
            with eng.Fori(0, KD // 2 - 1) as i:
                pair(i, 2)
            for m in (KD - 2, KD - 1):
                for s in range(3):
                    hi(eng, n1 + 3 * m + s + 2, WIDE)
                take(m, 0, 0)

        def pool_down(eng, n1):
            with eng.Fori(0, KD // 2 - 1) as i:
                for s in range(6):
                    lo(eng, n1 + s + 2, WIDE, i, 6)
            for s in range(6):
                lo(eng, n1 + 3 * (KD - 2) + s + 2, WIDE)

        def act_ffn(eng, c, q, n0):
            act_silu(eng, c, n0)
            act_down(eng, n0 + 2 * KF, lambda m, i, per: act_y(eng, q, n0 + 2 * KF, 3, m, i, per))
            act_root(eng, q, EPS_RMS)

        def pool_ffn(eng, n0):
            pool_silu(eng, n0)
            pool_down(eng, n0 + 2 * KF)

        def dve_ffn(eng, c, n0):
            with eng.Fori(0, KF // 2) as i:
                for k in range(2):
                    eng.wait_ge(slots_done, i * 4 + (n0 + 2 * k + 2))
                    eng.wait_ge(silu_ready, i * 2 + (KF * c + k + 1))
                    at_h, at_l = (v[:, bass.ds(i * 2 + k, 1), :].rearrange("p a s -> p (a s)") for v in (guH, guL))
                    eng.tensor_tensor(gfull[:, k, :], tmp[:, k, :], bank[2 + k][:, :], ALU.mult).then_inc(gsteps, 1)
                    eng.wait_ge(gsteps, i * 4 + (2 * KF * c + 2 * k + 1))
                    eng.tensor_copy(at_h, gfull[:, k, :]).then_inc(gsteps, 1)
                    eng.wait_ge(gsteps, i * 4 + (2 * KF * c + 2 * k + 2))
                    eng.tensor_tensor(at_l, gfull[:, k, :], at_h, ALU.subtract).then_inc(g_free, 1)

        gcol = small[:, 0:48]
        ghalf = small[:, 48:96]

        def dve_post(eng, q, xr, gains):
            eng.wait_ge(rs_ready, q + 1)
            for m in range(KD):
                if xr + m >= 2:
                    eng.wait_ge(x_ready, xr + m - 1)
                eng.scalar_tensor_tensor(tmp[:, m % 2, :], yT[:, m, :], gains[:, m:m + 1], rs,
                                         ALU.mult, ALU.mult).then_inc(t_ready, 1)

        def pool_post(eng, xr):
            for m in range(KD):
                eng.wait_ge(t_ready, xr + m + 1)
                eng.tensor_tensor(xT[:, m, :], xT[:, m, :], tmp[:, m % 2, :], ALU.add).then_inc(x_ready, 1)

        def dve_pre(eng, q, h0, gains):
            eng.wait_ge(rs_ready, q + 1)
            for m in range(KD):
                if m >= 2:
                    eng.wait_ge(h_ready, h0 + m - 1)
                eng.scalar_tensor_tensor(tmp[:, m % 2, :], xT[:, m, :], gains[:, m:m + 1], rs,
                                         ALU.mult, ALU.mult).then_inc(f_ready, 1)

        def act_round(eng, h0, src, ready):
            for m in range(KD):
                if ready is not None:
                    eng.wait_ge(ready[0], ready[1] + m + 1)
                eng.activation(hH[:, m, :], src(m), ACT.Copy).then_inc(h_hi, 1)

        def pool_rest(eng, h0, src):
            for m in range(KD):
                eng.wait_ge(h_hi, h0 + m + 1)
                eng.tensor_tensor(hL[:, m, :], src(m), hH[:, m, :], ALU.subtract).then_inc(h_ready, 1)

        def of_tmp(m):
            return tmp[:, m % 2, :]

        def of_x(m):
            return xT[:, m, :]

        N_IN = 24

        def pe_proj_T(eng, n0, tiles, h0):
            for j in range(tiles):
                if j >= 2:
                    eng.wait_ge(tp_free, j - 1)
                landed(eng, n0 + j)
                for kc in range(KD):
                    if j == 0:
                        eng.wait_ge(h_ready, h0 + kc + 1)
                    mm = product(eng, bank[j % 2][:, :], n0 + j, kc * P, (kc + 1) * P,
                                 hH[:, kc, :], hL[:, kc, :], kc == 0, kc == KD - 1)
                mm.then_inc(slots_done, 1)

        def act_proj_T(eng, n0, scales):
            for j, s in enumerate(scales):
                eng.wait_ge(slots_done, n0 + j + 1)
                eng.activation(projT[:, j, :], bank[j % 2][:, :], ACT.Copy, scale=s).then_inc(tp_free, 1)
                hi(eng, n0 + j + 2, width(n0 + j + 2))

        def act_proj_N(eng, n0, slots):
            for n in range(n0 + 2, n0 + 2 + slots):
                hi(eng, n, width(n))

        def pe_proj_N(eng, n0, part, w=512, per=(2, 2, 2, 2)):
            if part:
                eng.wait_ge(vp_free, NT * part)
            kc = 0
            for s, count in enumerate(per):
                n = n0 + s
                landed(eng, n)
                for k in range(count):
                    a, b = (v[:, n % NSLOT, k * w:(k + 1) * w] for v in (wH, wL))
                    for tile in range(NT):
                        out = bank[2 + tile][:, 0:w]
                        x, y = (v[:, kc, tile * P:(tile + 1) * P] for v in (hH, hL))
                        eng.matmul(out, x, a, start=(kc == 0), stop=False)
                        eng.matmul(out, x, b, start=False, stop=False)
                        mm = eng.matmul(out, y, a, start=False, stop=(kc == KD - 1))
                    kc += 1
                mm.then_inc(slots_done, 1)

        def dve_proj_N(eng, n0, dst, w=512, slots=4):
            eng.wait_ge(slots_done, n0 + slots)
            for b in range(NT):
                eng.tensor_copy(dst[:, b, :], bank[2 + b][:, 0:w]).then_inc(vp_free, 1)

        V1 = yT[:, :, :].rearrange("p c s -> p (c s)").rearrange("p (b n) -> p b n", b=NT)
        sc = Layout(mix, MW)
        sc.take(16 * S)
        tab1_at = sc.at
        tab1 = sc.take(10 * S).rearrange("p (h s) -> p h s", h=10)
        PR = 4
        prob = sc.take(PR * S).rearrange("p (b s) -> p b s", b=PR)
        probT = sc.take(4 * S * 2).rearrange("p (b j s) -> p b j s", b=2, j=NT)
        stat = sc.take(64)
        absz = sc.take(1280)
        softp = sc.take(1280)
        wts = probT.rearrange("p b j s -> p b (j s)")
        dsq = sc.take(S)
        dfull = sc.take(2 * S).rearrange("p (n s) -> p n s", n=2)
        lamcol, negcol = small[:, 96:97], small[:, 97:98]
        subg = small[:, 98:99]
        lamtmp = small[:, 100:140]
        lam_in = small[:, 140:272]
        lamprod = small[:, 272:336].rearrange("p (a n) -> p a n", a=2)

        units = [(h, i) for h in range(DIL + DIFF) for i in range(NT)]
        maps = []
        for u, (h, i) in enumerate(units):
            maps += [(u, 0)] + ([(u, 1)] if h >= DIL else [])
        first_map = [next(k for k, (v, _) in enumerate(maps) if v == u) for u in range(len(units))]

        def operands(h, w):
            if h < DIL:
                lo = (h % 2) * DH
                return QA + h // 2, KA + h // 2, lo, lo + DH
            g = h - DIL
            lo = (g % 2) * DH + w * 32
            return QB + g // 2, KB + g // 2, lo, lo + 32

        def pe_soft(eng):
            eng.wait_ge(tp_free, 16)
            eng.wait_ge(vp_free, 8)

            def scores(k):
                u, w = maps[k]
                h, i = units[u]
                q, kk, lo, hi = operands(h, w)
                if k >= 3:
                    eng.wait_ge(p_max, k - 2)
                eng.matmul(bank[k % 3][:, 0:(i + 1) * P], projT[lo:hi, q, i * P:(i + 1) * P],
                           projT[lo:hi, kk, 0:(i + 1) * P], start=True, stop=True).then_inc(s_ready, 1)

            def turn(u):
                h, i = units[u]
                eng.wait_ge(p_norm, u + 1)
                if u >= 2:
                    eng.wait_ge(p_back, u - 1)
                for j in range(i + 1):
                    mm = eng.transpose(bank[3 + u % 2][:, j * P:(j + 1) * P],
                                       prob[:, first_map[u] % PR, j * P:(j + 1) * P], ident)
                mm.then_inc(p_turn, 1)

            def pv(h):
                pair = h // 2
                eng.wait_ge(p_back, NT * (h + 1))
                if h % 2 == 0 and pair >= 2:
                    eng.wait_ge(o_taken, pair - 1)
                lo = (h % 2) * DH
                for j in range(NT):
                    mm = eng.matmul(bank[5 + 2 * (pair % 2)][lo:lo + DH, j * P:S],
                                    V1[:, j, h * DH:(h + 1) * DH], probT[:, h % 2, j, j * P:S],
                                    start=(j == 0), stop=(j == NT - 1), skip_group_check=True)
                mm.then_inc(o_ready, 1)

            k = 0
            LAG = 2
            for u in range(len(units) + LAG + 1):
                if u < len(units):
                    while k < len(maps) and maps[k][0] == u:
                        scores(k)
                        k += 1
                if 0 <= u - LAG < len(units):
                    turn(u - LAG)
                v = u - LAG - 1
                if v >= 0 and v % NT == NT - 1:
                    pv(v // NT)
                    if v // NT == DIL + 1 or v // NT == DIL + 3:
                        pair = v // NT // 2
                        eng.wait_ge(d_sq, pair - 2)
                        eng.matmul(bank[6][:, :], blk64, dsq, start=True, stop=True).then_inc(d_sum, 1)

        def dve_soft(eng):
            def post(u):
                h, i = units[u]
                w = (i + 1) * P
                k = first_map[u]
                if h < DIL:
                    eng.wait_ge(p_exp, k + 1)
                    eng.reciprocal(stat[:, 32 + k % PR:33 + k % PR], stat[:, 16 + k % PR:17 + k % PR]).then_inc(p_rec, 1)
                    rec[0] += 1
                    eng.wait_ge(p_rec, rec[0])
                    a = prob[:, k % PR, 0:w]
                    eng.tensor_scalar(a, a, stat[:, 32 + k % PR:33 + k % PR], None, ALU.mult).then_inc(p_norm, 1)
                    return
                a, b = k % PR, (k + 1) % PR
                eng.wait_ge(p_exp, k + 2)
                eng.reciprocal(stat[:, 32 + a:33 + a], stat[:, 16 + a:17 + a]).then_inc(p_rec, 1)
                eng.reciprocal(stat[:, 32 + b:33 + b], stat[:, 16 + b:17 + b]).then_inc(p_rec, 1)
                rec[0] += 2
                eng.wait_ge(p_rec, rec[0])
                eng.tensor_scalar(prob[:, a, 0:w], prob[:, a, 0:w], stat[:, 32 + a:33 + a], None, ALU.mult).then_inc(p_rec, 1)
                eng.tensor_scalar(stat[:, 48 + b:49 + b], stat[:, 32 + b:33 + b], negcol, None, ALU.mult).then_inc(p_rec, 1)
                rec[0] += 2
                eng.wait_ge(p_rec, rec[0])
                eng.scalar_tensor_tensor(prob[:, a, 0:w], prob[:, b, 0:w], stat[:, 48 + b:49 + b],
                                         prob[:, a, 0:w], ALU.mult, ALU.add).then_inc(p_norm, 1)

            def freed(k):
                if k >= PR:
                    v = maps[k - PR][0]
                    eng.wait_ge(p_turn, v + 1)

            rec = [0]
            k = 0
            def take(pair):
                b = bank[5 + 2 * (pair % 2)][:, :]
                if pair < DIL // 2:
                    eng.wait_ge(o_hi, pair + 1)
                    eng.tensor_tensor(hL[:, pair, :], b, hH[:, pair, :], ALU.subtract).then_inc(o_taken, 1)
                else:
                    n = pair - DIL // 2
                    eng.wait_ge(d_rs, 2 * n + 2)
                    eng.scalar_tensor_tensor(dfull[:, n, :], b, subg, rs, ALU.mult, ALU.mult).then_inc(o_taken, 1)

            for u in range(len(units) + 4):
                if u >= 4 and (u - 4) % (2 * NT) == 2 * NT - 1:
                    take((u - 4) // (2 * NT))
                if u < len(units):
                    while k < len(maps) and maps[k][0] == u:
                        h, i = units[u]
                        w = (i + 1) * P
                        eng.wait_ge(s_ready, k + 1)
                        freed(k)
                        eng.tensor_tensor_reduce(prob[:, k % PR, 0:w], bank[k % 3][:, 0:w],
                                                 tab1[:, h, S - w:S], 1.0, 3.0e38, ALU.add, ALU.min,
                                                 stat[:, k % PR:k % PR + 1]).then_inc(p_max, 1)
                        k += 1
                if 1 <= u <= len(units):
                    post(u - 1)

        def act_soft(eng):
            def back(u):
                h, i = units[u]
                eng.wait_ge(p_turn, u + 1)
                if h >= 2 and i == 0:
                    eng.wait_ge(o_ready, h - 1)
                eng.activation(probT[:, h % 2, 0:i + 1, i * P:(i + 1) * P],
                               bank[3 + u % 2][:, 0:(i + 1) * P].rearrange("p (j s) -> p j s", j=i + 1),
                               ACT.Copy).then_inc(p_back, 1)

            def take(pair):
                eng.wait_ge(o_ready, 2 * pair + 2)
                b = bank[5 + 2 * (pair % 2)][:, :]
                if pair < DIL // 2:
                    eng.activation(hH[:, pair, :], b, ACT.Copy).then_inc(o_hi, 1)
                    return
                n = pair - DIL // 2
                eng.activation(dsq, b, ACT.Square).then_inc(d_sq, 1)
                eng.wait_ge(d_sum, n + 1)
                if n:
                    eng.wait_ge(o_taken, DIL // 2 + n)
                eng.activation(lnv, bank[6][:, :], ACT.Ln, bias=EPS_RMS).then_inc(d_rs, 1)
                eng.wait_ge(d_rs, 2 * n + 1)
                eng.activation(rs, lnv, ACT.Exp, scale=-0.5).then_inc(d_rs, 1)

            k = 0
            for u in range(len(units) + 3):
                if u < len(units):
                    while k < len(maps) and maps[k][0] == u:
                        h, i = units[u]
                        w = (i + 1) * P
                        eng.wait_ge(p_max, k + 1)
                        eng.activation(prob[:, k % PR, 0:w], prob[:, k % PR, 0:w], ACT.Exp, scale=-1.0,
                                       bias=stat[:, k % PR:k % PR + 1],
                                       accum_out=stat[:, 16 + k % PR:17 + k % PR]).then_inc(p_exp, 1)
                        k += 1
                if 0 <= u - 2 < len(units):
                    back(u - 2)
                if u >= 3 and (u - 3) % (2 * NT) == 2 * NT - 1:
                    take((u - 3) // (2 * NT))

        def pool_diff(eng):
            for n in range(2):
                m = DIL // 2 + n
                eng.wait_ge(o_taken, m + 1)
                eng.tensor_copy(hH[:, m, :], dfull[:, n, :]).then_inc(d_out, 1)
                eng.wait_ge(d_out, 2 * n + 1)
                eng.tensor_tensor(hL[:, m, :], dfull[:, n, :], hH[:, m, :], ALU.subtract).then_inc(d_out, 1)

        def zcols(a, c0, c1):
            return (c0 - 384, c1 - 384) if a == 3 else (c0, c1)

        def zb(h, a):
            return bank[3 * (h % 2) + [0, 1, 2, 1][a]]

        def pe_stick(eng):
            eng.wait_ge(p_back, len(units))
            eng.wait_ge(o_taken, 5)

            def z(h):
                q, kk, lo = QC + h // 2, KC + h // 2, (h % 2) * DH
                if h >= 2:
                    eng.wait_ge(z_w, 4 * (h - 1))
                for a in (0, 1, 3, 2):
                    c0, c1 = zcols(a, a * P, S)
                    eng.matmul(zb(h, a)[:, c0:c1], projT[lo:lo + DH, kk, a * P:(a + 1) * P],
                               projT[lo:lo + DH, q, a * P:S], start=(a != 3), stop=False,
                               skip_group_check=True)
                    mm = eng.matmul(zb(h, a)[:, c0:c0 + P], matsb[:, 0, :], matsb[:, 1, :],
                                    start=False, stop=True, skip_group_check=True)
                mm.then_inc(z_ready, 1)

            def cum(h):
                eng.wait_ge(z_sp, 4 * (h + 1))
                for a in (0, 1, 3, 2):
                    for b in range(a, NT):
                        c0, c1 = zcols(a, b * P, S)
                        mm = eng.matmul(zb(h, a)[:, c0:c1], negL if a == b else negones,
                                        softp[:, triangle(b):triangle(b) + (NT - b) * P],
                                        start=False, stop=True, skip_group_check=True)
                mm.then_inc(z_cum, 1)

            def pv(h):
                eng.wait_ge(z_w, 4 * (h + 1))
                pair, lo = h // 2, (h % 2) * DH
                if h % 2 == 0 and pair >= 1:
                    eng.wait_ge(o_taken, 5 + pair)
                for a in range(NT):
                    mm = eng.matmul(bank[7][lo:lo + DH, a * P:S], V1[:, a, 640 + h * DH:640 + (h + 1) * DH],
                                    wts[:, h % 2, triangle(a):triangle(a) + (NT - a) * P],
                                    start=(a == 0), stop=(a == NT - 1), skip_group_check=True)
                mm.then_inc(z_pv, 1)

            z(0)
            for h in range(SB):
                if h + 1 < SB:
                    z(h + 1)
                cum(h)
                if h >= 1:
                    pv(h - 1)
            pv(SB - 1)

        def dve_stick(eng):
            def take(pair):
                eng.wait_ge(o_hi, DIL // 2 + pair + 1)
                eng.tensor_tensor(hL[:, 5 + pair, :], bank[7][:, :], hH[:, 5 + pair, :],
                                  ALU.subtract).then_inc(o_taken, 1)

            for h in range(SB):
                eng.wait_ge(z_ready, h + 1)
                eng.wait_ge(z_ln, h + 1)
                for a in range(NT):
                    c0, c1 = zcols(a, a * P, S)
                    t0 = triangle(a)
                    sp = softp[:, t0:t0 + c1 - c0]
                    eng.scalar_tensor_tensor(sp, zb(h, a)[:, c0:c1], 0.0, sp, ALU.max, ALU.add).then_inc(z_sp, 1)
                if h >= 2 and h % 2 == 0:
                    take(h // 2 - 1)
            take(2)

        def act_stick(eng):
            def first(h):
                eng.wait_ge(z_ready, h + 1)
                for a in range(NT):
                    c0, c1 = zcols(a, a * P, S)
                    t0 = triangle(a)
                    eng.activation(absz[:, t0:t0 + c1 - c0], zb(h, a)[:, c0:c1], ACT.Abs).then_inc(z_abs, 1)
                eng.wait_ge(z_abs, 4 * (h + 1))
                eng.activation(absz, absz, ACT.Exp, scale=-1.0).then_inc(z_exp, 1)
                eng.wait_ge(z_exp, h + 1)
                if h:
                    eng.wait_ge(z_cum, h)
                eng.activation(softp, absz, ACT.Ln, bias=1.0).then_inc(z_ln, 1)

            def weights(h):
                eng.wait_ge(z_cum, h + 1)
                if h >= 2:
                    eng.wait_ge(z_pv, h - 1)
                for a in range(NT):
                    c0, c1 = zcols(a, a * P, S)
                    t0 = triangle(a)
                    eng.activation(wts[:, h % 2, t0:t0 + c1 - c0], zb(h, a)[:, c0:c1], ACT.Exp).then_inc(z_w, 1)

            def take(pair):
                eng.wait_ge(z_pv, 2 * pair + 2)
                eng.activation(hH[:, 5 + pair, :], bank[7][:, :], ACT.Copy).then_inc(o_hi, 1)

            for h in range(SB):
                first(h)
                weights(h)
                if h >= 2 and h % 2 == 0:
                    take(h // 2 - 1)
            take(2)

        def pe_out(eng, n0, free, add):
            def col(m):
                free(eng, m)
                landed(eng, n0 + m)
                for kc in range(KD):
                    mm = product(eng, bank[4 + m % 2][:, :], n0 + m, kc * P, (kc + 1) * P,
                                 hH[:, kc, :], hL[:, kc, :], kc == 0, kc == KD - 1)
                mm.then_inc(slots_done, 1)
            for m in range(KD):
                col(m)
                if m:
                    add(eng, m - 1)
            add(eng, KD - 1)

        with nc.Block() as block:
            @block.sync
            def _(sp):
                sp.dma_start(xT[:, :, :], t["xT"]).then_inc(io, 16)
                sp.dma_start(mats[:, :, :], t["mats"]).then_inc(io, 16)
                sp.wait_ge(io, 32)

            @block.vector
            def _(dve):
                dve.wait_ge(io, 32)
                dve.tensor_copy(matsb[:, 0, :], ident)
                dve.tensor_copy(matsb[:, 1, :], mats[:, MASK, :])

        FFN_SLOTS = 2 * KF + 3 * KD
        A, B = 2 * KF, 3 * KD
        n_ffn0, n_in = 0, FFN_SLOTS
        n_out = n_in + N_IN
        n_ffn1 = n_out + KD
        total_slots[0] = n_ffn1 + FFN_SLOTS

        def of_layer(layer, name):
            return t[name][bass.ds(layer, 1), :, :].rearrange("a p n -> (a p) n")

        with nc.Fori(0, DEPTH) as layer:
            with nc.Block() as block:
                @block.sync
                def _(sp):
                    sp.dma_start(small[:, 0:48], of_layer(layer, "gains1")).then_inc(par_in, 16)
                    sp.dma_start(small[:, 98:100], of_layer(layer, "subg")).then_inc(par_in, 16)
                    sp.dma_start(lam_in[:, 0:129], of_layer(layer, "lam")).then_inc(par_in, 16)
                    stream(sp, layer, t["w8_1"], 0, A, n_ffn0, WIDE)
                    stream_down(sp, layer, t["down_1"], 0, n_ffn0 + A)
                    sp.wait_ge(slots_done, n_in)
                    sp.dma_start(tab1, t["table1"]).then_inc(tab_in, 16)
                    stream(sp, layer, t["w8_1"], A, N_IN + KD, n_in, WIDE)
                    stream(sp, layer, t["w8_1"], A + N_IN + KD, A, n_ffn1, WIDE)
                    stream_down(sp, layer, t["down_1"], B, n_ffn1 + A)

                @block.tensor
                def _(pe):
                    for m in range(KD):
                        sum_square(pe, 0, m)
                    pe_ffn(pe, 0, n_ffn0, 0, rms_free(1), rms_add(1))
                    for m in range(KD):
                        sum_square(pe, 2, m)
                    pe_proj_T(pe, n_in, 16, 8)
                    pe_proj_N(pe, n_in + 16, 0)
                    pe_proj_N(pe, n_in + 20, 1)
                    pe_soft(pe)
                    pe_stick(pe)
                    pe.wait_ge(o_taken, 8)
                    pe.wait_ge(d_out, 4)
                    pe_out(pe, n_out, rms_free(3), rms_add(3))
                    for m in range(KD):
                        sum_square(pe, 4, m)
                    pe_ffn(pe, 1, n_ffn1, 16, rms_free(5), rms_add(5))

                @block.scalar
                def _(act):
                    act.preload_act_table_set(EXP_LN)
                    hi(act, 0)
                    hi(act, 1)
                    act_square_x(act, 0, None)
                    act_root(act, 0, EPS_RMS)
                    act_round(act, 0, of_tmp, (f_ready, 0))
                    act_ffn(act, 0, 1, n_ffn0)
                    act_square_x(act, 2, 0)
                    act_root(act, 2, EPS_RMS)
                    act_round(act, 8, of_tmp, (f_ready, 8))
                    act_proj_T(act, n_in, [-DH ** -0.5] * 3 + [1.0] * 3 + [-32 ** -0.5] * 2 + [1.0] * 2
                               + [DH ** -0.5] * 3 + [1.0] * 3)
                    act_proj_N(act, n_in + 16, 8)
                    act.wait_ge(seq, 4)
                    act.activation(lamtmp[:, 2:4], lamtmp[:, 0:2], ACT.Exp).then_inc(par_ready, 1)
                    act_soft(act)
                    act_stick(act)
                    for m in range(KD):
                        act_y(act, 3, n_out, 1, m)
                        hi(act, n_out + m + 2)
                    act_root(act, 3, EPS_RMS)
                    act_square_x(act, 4, 8)
                    act_root(act, 4, EPS_RMS)
                    act_round(act, 16, of_tmp, (f_ready, 16))
                    act_ffn(act, 1, 5, n_ffn1)

                @block.vector
                def _(dve):
                    dve.sem_inc(g_free, 2)
                    dve.sem_inc(sq_used, 2)
                    dve.wait_ge(par_in, 48)
                    dve.tensor_scalar(ghalf, gcol, 0.5, None, ALU.mult).then_inc(seq, 1)
                    dve.tensor_tensor(lamprod, lam_in[:, 0:64].rearrange("p (a n) -> p a n", a=2),
                                      lam_in[:, 64:128].rearrange("p (a n) -> p a n", a=2), ALU.mult).then_inc(seq, 1)
                    dve.wait_ge(seq, 2)
                    dve.tensor_reduce(lamtmp[:, 0:2], lamprod, AX_X, ALU.add).then_inc(seq, 1)
                    dve.tensor_scalar(subg, subg, small[:, 99:100], None, ALU.mult).then_inc(seq, 1)
                    dve.wait_ge(seq, 4)
                    dve_pre(dve, 0, 0, gcol[:, 0:8])
                    dve_ffn(dve, 0, n_ffn0)
                    dve_post(dve, 1, 0, ghalf[:, 8:16])
                    dve_pre(dve, 2, 8, gcol[:, 16:24])
                    dve_proj_N(dve, n_in + 16, V1[:, :, 0:512])
                    dve_proj_N(dve, n_in + 20, V1[:, :, 512:1024])
                    dve.wait_ge(par_ready, 1)
                    dve.tensor_tensor(lamtmp[:, 4:5], lamtmp[:, 3:4], lamtmp[:, 2:3], ALU.subtract).then_inc(seq, 1)
                    dve.wait_ge(seq, 5)
                    dve.tensor_scalar(negcol, lamtmp[:, 4:5], lam_in[:, 128:129], None, ALU.subtract).then_inc(seq, 1)
                    dve.wait_ge(seq, 6)
                    dve.wait_ge(tab_in, 16)
                    dve_soft(dve)
                    dve_stick(dve)
                    dve_post(dve, 3, 8, gcol[:, 24:32])
                    dve_pre(dve, 4, 16, gcol[:, 32:40])
                    dve_ffn(dve, 1, n_ffn1)
                    dve_post(dve, 5, 16, ghalf[:, 40:48])

                @block.gpsimd
                def _(pool):
                    los(pool, 0, 2)
                    pool_rest(pool, 0, of_tmp)
                    pool_ffn(pool, n_ffn0)
                    pool_post(pool, 0)
                    pool_rest(pool, 8, of_tmp)
                    los(pool, n_in + 2, n_out + 2)
                    pool_diff(pool)
                    los(pool, n_out + 2, n_ffn1 + 2)
                    pool_post(pool, 8)
                    pool_rest(pool, 16, of_tmp)
                    pool_ffn(pool, n_ffn1)
                    pool_post(pool, 16)

            with nc.Block() as block:
                @block.sync
                def _(sp):
                    for s in nsem.values():
                        sp.sem_clear(s)

        HQ, HGT, NQ, KCM, VCM, KSL, KWI = 0, 4, 8, 12, 13, 14, 15
        yflat = yT[:, :, :].rearrange("p c s -> p (c s)")
        sc = Layout(mix, MW)
        sc.take(16 * S)
        forget_at = sc.at
        LF = sc.take(2048).rearrange("p (b n) -> p b n", b=NT)
        HV = sc.take(2048).rearrange("p (b n) -> p b n", b=NT)
        tab2 = mix[:, forget_at:forget_at + NSA * S].rearrange("p (h s) -> p h s", h=NSA)
        span = sc.take(1024)
        lmask = sc.take(1024)
        par = sc.take(64 + 128 + 1)
        posk, posv, w2k, w2v = par[:, 0:32], par[:, 32:64], par[:, 64:128], par[:, 128:192]
        gwcol = par[:, 192:193]
        g1, b1, g2, b2 = (small[:, 8 * n:8 * n + 8] for n in range(4))
        flags = sc.take(4)
        vg = sc.take(NT * VG).rearrange("p (b n) -> p b n", b=NT)
        gate = sc.take(NT * 24).rearrange("p (b n) -> p b n", b=NT)
        chid = sc.take(128).rearrange("p (g k n) -> p g k n", g=2, k=2)
        kcmp = sc.take(32)
        vcmp = sc.take(128)
        valid = sc.take(1)
        both_at = sc.at
        winK = sc.take(32 * NCMP).rearrange("p (i n) -> p i n", i=32)
        winV = sc.take(32 * NCMP).rearrange("p (i n) -> p i n", i=32)
        w1k = yflat.rearrange("p (i n) -> p i n", i=32)
        w1v = mix[:, both_at + 2048:both_at + 6144].rearrange("p (i n) -> p i n", i=32)

        sc.at = both_at
        kN = sc.take(2048).rearrange("p (b n) -> p b n", b=NT)
        kT = sc.take(2048).rearrange("p (h s) -> p h s", h=HG)
        t_at = sc.at
        QR = sc.take(2048).rearrange("p (r l s) -> p r l s", r=2, l=8)
        KL = sc.take(1792).rearrange("p (r l s) -> p r l s", r=2, l=LEVELS)
        AM = sc.take(1024)
        scs = sc.take(256).rearrange("p (r s) -> p r s", r=2)
        ST = sc.take(256).rearrange("p (r s) -> p r s", r=2)
        T1 = mix[:, t_at:t_at + 2048].rearrange("p (b n) -> p b n", b=NT)
        T2 = mix[:, t_at + 2048:t_at + 4096].rearrange("p (b n) -> p b n", b=NT)
        logA, logB = kT[:, 0, :], kT[:, 1, :]
        lbp0, lbp1 = T2[:, 2, :], T2[:, 3, :]
        E = yflat[:, 0:2048].rearrange("p (r n) -> p r n", r=2)
        KDE = yflat[:, 2048:3584].rearrange("p (b n) -> p b n", b=3)

        def wide(v):
            return v.unsqueeze(1).broadcast_to([P, NT, 512])

        def dve_forget(eng):
            def step(ins):
                ins.then_inc(f_dve, 1)
                fd[0] += 1
            fd = [0]
            eng.wait_ge(par_in, 48)
            step(eng.tensor_tensor(T1[:, 0, :], lbp1, lbp0, ALU.subtract))
            eng.wait_ge(f_act, 3)
            step(eng.scalar_tensor_tensor(T1[:, 1, :], T1[:, 0, :], 0.0, T1[:, 1, :], ALU.max, ALU.add))
            eng.wait_ge(f_dve, 2)
            step(eng.tensor_scalar(logB, T1[:, 1, :], flags[:, 1:2], None, ALU.mult))
            step(eng.tensor_tensor(T1[:, 2, :], T1[:, 0, :], T1[:, 1, :], ALU.subtract))
            eng.wait_ge(f_dve, 4)
            step(eng.tensor_scalar(logA, T1[:, 2, :], flags[:, 0:1], flags[:, 2:3], ALU.mult, ALU.add))
            eng.wait_ge(f_dve, 5)
            eng.wait_ge(f_act, 6)
            step(eng.scalar_tensor_tensor(T2, LF, 0.0, T1, ALU.min, ALU.subtract))
            eng.wait_ge(f_dve, 6)
            step(eng.tensor_tensor(T2, T2, wide(logB), ALU.add))
            eng.wait_ge(f_dve, 7)
            step(eng.tensor_tensor(kN, T2, LF, ALU.subtract))
            step(eng.tensor_tensor(T1, wide(logA), T2, ALU.subtract))
            eng.wait_ge(f_dve, 9)
            step(eng.tensor_tensor(LF, wide(logA), T2, ALU.max))
            eng.wait_ge(f_act, 10)
            eng.wait_ge(f_dve, 10)
            step(eng.tensor_tensor(LF, LF, T1, ALU.add))

        def act_forget(eng):
            def step(ins):
                ins.then_inc(f_act, 1)
                fa[0] += 1
                eng.wait_ge(f_act, fa[0])
            fa = [0]
            eng.wait_ge(f_dve, 1)
            step(eng.activation(T1[:, 1, :], T1[:, 0, :], ACT.Abs))
            step(eng.activation(T1[:, 1, :], T1[:, 1, :], ACT.Exp, scale=-1.0))
            step(eng.activation(T1[:, 1, :], T1[:, 1, :], ACT.Ln, bias=1.0))
            eng.wait_ge(f_dve, 5)
            eng.wait_ge(vp_free, 4)
            step(eng.activation(T1, LF, ACT.Abs))
            step(eng.activation(T1, T1, ACT.Exp, scale=-1.0))
            step(eng.activation(T1, T1, ACT.Ln, bias=1.0))
            eng.wait_ge(f_dve, 9)
            step(eng.activation(T1, T1, ACT.Abs))
            step(eng.activation(kN, kN, ACT.Exp))
            step(eng.activation(T1, T1, ACT.Exp, scale=-1.0))
            step(eng.activation(T1, T1, ACT.Ln, bias=1.0))

        def dve_windows(eng):
            eng.wait_ge(tp_free, 14)
            for dst, j, pos_ in ((winK, KCM, posk), (winV, VCM, posv)):
                src = projT[:, j, :].rearrange("p (n i) -> p i n", i=16)
                for half in range(2):
                    eng.tensor_tensor(dst[:, 16 * half:16 * half + 16, :], src[:, :, half:half + NCMP],
                                      pos_[:, 16 * half:16 * half + 16].unsqueeze(2).broadcast_to([P, 16, NCMP]),
                                      ALU.add).then_inc(win, 1)

        def pe_compress(eng):
            eng.wait_ge(w_in1, 32)
            eng.wait_ge(win, 4)
            eng.wait_ge(tp_free, 16)
            for kind, (w1, src) in enumerate(((w1k, winK), (w1v, winV))):
                for g in range(2):
                    lo = g * DH
                    for i in range(32):
                        mm = eng.matmul(bank[g][:, kind * 32:kind * 32 + NCMP], w1[lo:lo + DH, i, :],
                                        src[lo:lo + DH, i, :], start=(i == 0), stop=(i == 31),
                                        skip_group_check=True)
            mm.then_inc(c_hid, 1)
            eng.wait_ge(c_act, 2)
            for g in range(2):
                eng.matmul(bank[6][g * DH:(g + 1) * DH, 0:NCMP], w2k, chid[:, g, 0, 0:NCMP],
                           start=True, stop=True, skip_group_check=True)
            for g in range(2):
                mm = eng.matmul(bank[7][0:NCMP, g * DH:(g + 1) * DH], chid[:, g, 1, 0:NCMP], w2v,
                                start=True, stop=True, skip_group_check=True)
            mm.then_inc(c_out, 1)

        def act_compress(eng):
            eng.wait_ge(c_hid, 1)
            for g in range(2):
                eng.activation(chid[:, g, :, 0:NCMP],
                               bank[g][:, 0:64].rearrange("p (k n) -> p k n", k=2)[:, :, 0:NCMP],
                               ACT.Gelu_apprx_tanh).then_inc(c_act, 1)

        def dve_compress(eng):
            eng.wait_ge(c_out, 1)
            eng.tensor_copy(kcmp[:, 0:NCMP], bank[6][:, 0:NCMP]).then_inc(c_done, 1)
            eng.tensor_copy(vcmp[0:NCMP, :], bank[7][0:NCMP, 0:128]).then_inc(c_done, 1)

        def pe_hgrn_keys(eng):
            eng.wait_ge(f_act, 8)
            for h in range(HG):
                for b in range(NT):
                    mm = eng.transpose(bank[2 + h][:, b * P:(b + 1) * P], kN[:, b, h * P:(h + 1) * P], ident)
                mm.then_inc(k_turn, 1)
            eng.wait_ge(f_dve, 11)
            for b in range(3):
                eng.matmul(bank[[6, 7, 0][b]][:, :], mats[:, SUF, :], LF[:, b, :],
                           start=True, stop=True).then_inc(suf_ready, 1)

        def act_hgrn_keys(eng):
            for h in range(HG):
                eng.wait_ge(k_turn, h + 1)
                if h == 0:
                    eng.wait_ge(f_dve, 10)
                eng.activation(kT[:, h, :], bank[2 + h][:, :], ACT.Copy).then_inc(k_back, 1)
            for b in range(3):
                eng.wait_ge(suf_ready, b + 1)
                eng.activation(KDE[:, b, :], bank[[6, 7, 0][b]][:, :], ACT.Exp).then_inc(suf_exp, 1)

        def dve_hgrn_keys(eng):
            for b in range(3):
                eng.wait_ge(suf_exp, b + 1)
                eng.tensor_tensor(KDE[:, b, :], KDE[:, b, :], kN[:, b, :], ALU.mult).then_inc(kd_ready, 1)

        HU = HG * NT

        def pe_hgrn(eng):
            eng.wait_ge(suf_exp, 3)
            eng.wait_ge(kd_ready, 3)
            eng.wait_ge(vp_free, 8)

            def decays(u):
                h, b = divmod(u, NT)
                if u:
                    eng.wait_ge(dec_exp, 2 * u)
                for half in range(2):
                    mm = eng.matmul(bank[half][:, :], LF[:, b, h * P:(h + 1) * P],
                                    span[:, half * 512:half * 512 + 512], start=True, stop=True)
                mm.then_inc(dec_ready, 1)

            def scores(u):
                h, b = divmod(u, NT)
                eng.wait_ge(q_dec, u + 1)
                eng.wait_ge(k_dec, u + 1)
                if u:
                    eng.wait_ge(a_mask, 2 * u)
                for l in range(LEVELS):
                    eng.matmul(bank[2 + l // 4][:, (l % 4) * P:(l % 4 + 1) * P], KL[:, u % 2, l, :],
                               QR[:, u % 2, l, :], start=True, stop=True, skip_group_check=True)
                eng.matmul(bank[3][:, 3 * P:4 * P], kT[:, h, b * P:(b + 1) * P],
                           projT[:, HQ + h, b * P:(b + 1) * P], start=True, stop=True,
                           skip_group_check=True).then_inc(a_ready, 1)

            def output(u):
                h, b = divmod(u, NT)
                eng.wait_ge(a_sum, u + 1)
                if b == 0 and h >= 2:
                    eng.wait_ge(hout, h - 1)
                o = bank[4 + h % 2][:, b * P:(b + 1) * P]
                mm = eng.matmul(o, HV[:, b, h * P:(h + 1) * P], scs[:, u % 2, :], start=True,
                                stop=(b == 0), skip_group_check=True)
                if b:
                    eng.wait_ge(st_ready, 3 * h + b)
                    mm = eng.matmul(o, ST[:, (b - 1) % 2, :], QR[:, u % 2, 7, :], start=False, stop=True,
                                    skip_group_check=True)
                mm.then_inc(ho_ready, 1)
                if b < NT - 1:
                    if 3 * h + b >= 1:
                        eng.wait_ge(st_ready, 3 * h + b)
                    eng.matmul(bank[7][:, 0:P], KDE[:, b, h * P:(h + 1) * P], HV[:, b, h * P:(h + 1) * P],
                               start=True, stop=True).then_inc(u_ready, 1)

            decays(0)
            for u in range(HU + 1):
                if u < HU:
                    if u + 1 < HU:
                        decays(u + 1)
                    scores(u)
                if u >= 1:
                    output(u - 1)
                    if (u - 1) % NT == NT - 1:
                        h = (u - 1) // NT
                        eng.wait_ge(hsq, h + 1)
                        eng.matmul(bank[6][:, :], onesD, sq[:, h % 2, :], start=True, stop=True).then_inc(hsum, 1)

        def act_hgrn(eng):
            for u in range(HU + 2):
                if u < HU:
                    eng.wait_ge(dec_ready, u + 1)
                    if u >= 2:
                        eng.wait_ge(q_dec, u - 1)
                        eng.wait_ge(k_dec, u - 1)
                        eng.wait_ge(st_ready, (u - 1) // NT * 3 + min((u - 1) % NT, 3))
                    for half in range(2):
                        eng.activation(E[:, u % 2, half * 512:half * 512 + 512], bank[half][:, :],
                                       ACT.Exp).then_inc(dec_exp, 1)
                if u >= 2 and (u - 2) % NT == NT - 1:
                    h = (u - 2) // NT
                    eng.wait_ge(ho_ready, 4 * (h + 1))
                    eng.activation(sq[:, h % 2, :], bank[4 + h % 2][:, :], ACT.Square).then_inc(hsq, 1)
                    eng.wait_ge(hsum, h + 1)
                    eng.activation(lnv, bank[6][:, :], ACT.Ln, bias=EPS_RMS, scale=D / P).then_inc(hrs, 1)
                    eng.wait_ge(hrs, 2 * h + 1)
                    if h:
                        eng.wait_ge(hout, h)
                    eng.activation(rs, lnv, ACT.Exp, scale=-0.5).then_inc(hrs, 1)

        def dve_hgrn(eng):
            eng.wait_ge(k_back, 4)

            def queries(u):
                h, b = divmod(u, NT)
                eng.wait_ge(dec_exp, 2 * u + 2)
                if u >= 2:
                    eng.wait_ge(ho_ready, u - 1)
                eng.tensor_tensor(QR[:, u % 2, :, :], E[:, u % 2, :].rearrange("p (l s) -> p l s", l=8),
                                  projT[:, HQ + h, b * P:(b + 1) * P].unsqueeze(1).broadcast_to([P, 8, P]),
                                  ALU.mult).then_inc(q_dec, 1)

            queries(0)
            for u in range(HU):
                h, b = divmod(u, NT)
                eng.wait_ge(a_ready, u + 1)
                if u:
                    eng.wait_ge(a_sum, u)
                for half in range(2):
                    eng.tensor_tensor(AM[:, half * 512:half * 512 + 512], bank[2 + half][:, :],
                                      lmask[:, half * 512:half * 512 + 512], ALU.mult).then_inc(a_mask, 1)
                if u + 1 < HU:
                    queries(u + 1)
                eng.wait_ge(a_mask, 2 * u + 2)
                if u >= 2:
                    eng.wait_ge(ho_ready, u - 1)
                eng.tensor_reduce(scs[:, u % 2, :], AM.rearrange("p (l s) -> p s l", l=8), AX_X,
                                  ALU.add).then_inc(a_sum, 1)
                if b < NT - 1:
                    eng.wait_ge(u_ready, 3 * h + b + 1)
                    if b == 0:
                        if h:
                            eng.wait_ge(ho_ready, 4 * h)
                        eng.tensor_copy(ST[:, 0, :], bank[7][:, 0:P]).then_inc(st_ready, 1)
                    else:
                        if b == 2:
                            eng.wait_ge(ho_ready, 4 * h + 2)
                        eng.wait_ge(st_ready, 3 * h + b)
                        eng.scalar_tensor_tensor(ST[:, b % 2, :], ST[:, (b - 1) % 2, :],
                                                 E[:, u % 2, 1023:1024], bank[7][:, 0:P],
                                                 ALU.mult, ALU.add).then_inc(st_ready, 1)
                if b == NT - 1:
                    eng.wait_ge(hrs, 2 * h + 2)
                    if h >= 2:
                        eng.wait_ge(hmix, 3 * (h - 2) + 1)
                    eng.scalar_tensor_tensor(tmp[:, h % 2, :], bank[4 + h % 2][:, :], gwcol, rs,
                                             ALU.mult, ALU.mult).then_inc(hout, 1)

        def pool_hgrn(eng):
            def keys(u):
                h, b = divmod(u, NT)
                eng.wait_ge(dec_exp, 2 * u + 2)
                if u >= 2:
                    eng.wait_ge(a_ready, u - 1)
                eng.tensor_tensor(KL[:, u % 2, :, :], E[:, u % 2, 0:LEVELS * P].rearrange("p (l s) -> p l s", l=LEVELS),
                                  kT[:, h, b * P:(b + 1) * P].unsqueeze(1).broadcast_to([P, LEVELS, P]),
                                  ALU.mult).then_inc(k_dec, 1)

            def mix(h):
                eng.wait_ge(hout, h + 1)
                eng.wait_ge(silu_g, 4)
                full = projT[:, HGT + h, :]
                eng.tensor_tensor(full, tmp[:, h % 2, :], full, ALU.mult).then_inc(hmix, 1)
                eng.wait_ge(hmix, 3 * h + 1)
                eng.tensor_copy(hH[:, h, :], full).then_inc(hmix, 1)
                eng.wait_ge(hmix, 3 * h + 2)
                eng.tensor_tensor(hL[:, h, :], full, hH[:, h, :], ALU.subtract).then_inc(hmix, 1)

            eng.wait_ge(k_back, 4)
            for u in range(HU):
                keys(u)
                if u >= NT and u % NT == 1:
                    mix(u // NT - 1)
            mix(HG - 1)

        sc.at = both_at
        p3 = sc.take(2 * 3 * S).rearrange("p (r w s) -> p r w s", r=2, w=3)
        probS = sc.take(4096)
        probC = sc.take(1024).rearrange("p (r s) -> p r s", r=2)
        st3 = sc.take(32)
        pT = [probS.rearrange("p (w j s) -> p w j s", w=2, j=NT), yflat.rearrange("p (w j s) -> p w j s", w=2, j=NT)]
        NU = NSA * NT

        def cw(i):
            return 8 * i + 7

        def pe_nsa(eng):
            eng.wait_ge(hout, 4)
            eng.wait_ge(c_done, 2)

            def scores(u):
                h, i = divmod(u, NT)
                g, hp = divmod(h, 4)
                lo = g * DH
                q = projT[lo:lo + DH, NQ + hp, i * P:(i + 1) * P]
                for w, (keys, n) in enumerate(((kcmp[lo:lo + DH, 0:cw(i)], cw(i)),
                                               (projT[lo:lo + DH, KSL, 0:(i + 1) * P], (i + 1) * P),
                                               (projT[lo:lo + DH, KWI, 0:(i + 1) * P], (i + 1) * P))):
                    if u:
                        eng.wait_ge(p_max, 3 * u + w - 2)
                    eng.matmul(bank[w][:, 0:n], q, keys, start=True, stop=True).then_inc(s_ready, 1)

            def turn(u):
                h, i = divmod(u, NT)
                for w in range(3):
                    eng.wait_ge(p_norm, 3 * u + w + 1)
                    if u:
                        eng.wait_ge(p_back, 3 * u + w - 2)
                    if w == 0:
                        mm = eng.transpose(bank[6][0:cw(i), 0:P], p3[:, u % 2, 0, 0:cw(i)], ident)
                    else:
                        for j in range(i + 1):
                            mm = eng.transpose(bank[2 + w][:, j * P:(j + 1) * P],
                                               p3[:, u % 2, w, j * P:(j + 1) * P], ident)
                    mm.then_inc(p_turn, 1)

            def pv(h):
                g, pair, lo = h // 4, h // 2, (h % 2) * DH
                eng.wait_ge(p_back, 12 * (h + 1))
                if h % 2 == 0 and pair >= 2:
                    eng.wait_ge(o_taken, pair - 1)
                o = bank[5 + 2 * (pair % 2)]
                for w in range(2):
                    for j in range(NT):
                        eng.matmul(o[lo:lo + DH, j * P:S], vg[:, j, w * P + g * DH:w * P + (g + 1) * DH],
                                   pT[h % 2][:, w, j, j * P:S], start=(w == 0 and j == 0), stop=False,
                                   skip_group_check=True)
                for i in range(NT):
                    mm = eng.matmul(o[lo:lo + DH, i * P:(i + 1) * P], vcmp[0:cw(i), g * DH:(g + 1) * DH],
                                    probC[0:cw(i), h % 2, i * P:(i + 1) * P], start=False, stop=(i == NT - 1),
                                    skip_group_check=True)
                mm.then_inc(o_ready, 1)

            scores(0)
            for u in range(NU + 1):
                if u + 1 < NU:
                    scores(u + 1)
                if u < NU:
                    turn(u)
                if u >= 1 and (u - 1) % NT == NT - 1:
                    pv((u - 1) // NT)

        def dve_gates(eng):
            eng.wait_ge(gate_ready, 1)
            g2d = gate.rearrange("p b n -> p (b n)")
            eng.tensor_scalar(g2d, g2d, 1.0, None, ALU.add).then_inc(p_rec, 1)
            eng.wait_ge(p_rec, 1)
            eng.reciprocal(g2d, g2d).then_inc(p_rec, 1)
            eng.wait_ge(p_rec, 2)
            eng.tensor_scalar(gate[:, 0, 0:8], gate[:, 0, 0:8], valid, None, ALU.mult).then_inc(p_rec, 1)
            eng.wait_ge(p_rec, 3)

        def dve_nsa(eng):
            rec = [3]
            eng.wait_ge(tab_in, 16)
            for u in range(NU + 3):
                if u >= 3 and (u - 3) % (2 * NT) == 2 * NT - 1:
                    pair = (u - 3) // (2 * NT)
                    eng.wait_ge(o_hi, pair + 1)
                    eng.tensor_tensor(hL[:, HG + pair, :], bank[5 + 2 * (pair % 2)][:, :], hH[:, HG + pair, :],
                                      ALU.subtract).then_inc(o_taken, 1)
                if u < NU:
                    h, i = divmod(u, NT)
                    n = (i + 1) * P
                    c0 = S - P - i * P + CMP_END
                    for w in range(3):
                        m = cw(i) if w == 0 else n
                        bias = tab2[:, h, c0:c0 + 16 * (m - 1) + 1:16] if w == 0 else tab2[:, h, S - n:S]
                        eng.wait_ge(s_ready, 3 * u + w + 1)
                        if u >= 2:
                            eng.wait_ge(p_turn, 3 * (u - 2) + w + 1)
                        a = (u % 2) * 3 + w
                        eng.tensor_tensor_reduce(p3[:, u % 2, w, 0:m], bank[w][:, 0:m], bias, 1.0, 3.0e38,
                                                 ALU.add, ALU.min, st3[:, a:a + 1]).then_inc(p_max, 1)
                if 1 <= u <= NU:
                    v = u - 1
                    h, i = divmod(v, NT)
                    a = (v % 2) * 3
                    eng.wait_ge(p_exp, 3 * v + 3)
                    eng.reciprocal(st3[:, 16 + a:19 + a], st3[:, 8 + a:11 + a]).then_inc(p_rec, 1)
                    eng.wait_ge(p_rec, rec[0] + 1)
                    eng.tensor_tensor(st3[:, 24 + a:27 + a], st3[:, 16 + a:19 + a],
                                      gate[:, i, h:h + 17:8], ALU.mult).then_inc(p_rec, 1)
                    eng.wait_ge(p_rec, rec[0] + 2)
                    rec[0] += 2
                    for w in range(3):
                        m = cw(i) if w == 0 else (i + 1) * P
                        x = p3[:, v % 2, w, 0:m]
                        eng.tensor_scalar(x, x, st3[:, 24 + a + w:25 + a + w], None, ALU.mult).then_inc(p_norm, 1)

        def act_nsa(eng):
            def back(u):
                h, i = divmod(u, NT)
                if i == 0 and h >= 2:
                    eng.wait_ge(o_ready, h - 1)
                for w in range(3):
                    eng.wait_ge(p_turn, 3 * u + w + 1)
                    if w == 0:
                        eng.activation(probC[0:cw(i), h % 2, i * P:(i + 1) * P], bank[6][0:cw(i), 0:P],
                                       ACT.Copy).then_inc(p_back, 1)
                    else:
                        eng.activation(pT[h % 2][:, w - 1, 0:i + 1, i * P:(i + 1) * P],
                                       bank[2 + w][:, 0:(i + 1) * P].rearrange("p (j s) -> p j s", j=i + 1),
                                       ACT.Copy).then_inc(p_back, 1)

            for u in range(NU + 2):
                if u < NU:
                    i = u % NT
                    for w in range(3):
                        m = cw(i) if w == 0 else (i + 1) * P
                        a = (u % 2) * 3 + w
                        eng.wait_ge(p_max, 3 * u + w + 1)
                        eng.activation(p3[:, u % 2, w, 0:m], p3[:, u % 2, w, 0:m], ACT.Exp, scale=-1.0,
                                       bias=st3[:, a:a + 1], accum_out=st3[:, 8 + a:9 + a]).then_inc(p_exp, 1)
                if 1 <= u <= NU:
                    back(u - 1)
                if u >= 2 and (u - 2) % (2 * NT) == 2 * NT - 1:
                    pair = (u - 2) // (2 * NT)
                    eng.wait_ge(o_ready, 2 * pair + 2)
                    eng.activation(hH[:, HG + pair, :], bank[5 + 2 * (pair % 2)][:, :], ACT.Copy).then_inc(o_hi, 1)

        def dve_sum(eng, q, n1, per_tile, m, i=0, per=0):
            eng.wait_ge(slots_done, i * (per * per_tile) + (n1 + per_tile * (m + 1)))
            if per == 0:
                x, y = xT[:, m, :], yT[:, m, :]
            else:
                x, y = (v[:, bass.ds(i * per + m, 1), :].rearrange("p a s -> p (a s)") for v in (xT, yT))
            eng.scalar_tensor_tensor(y, x, ALPHA, bank[4 + m % 2][:, :], ALU.mult, ALU.add).then_inc(y_done, 1)

        def dve_ln(eng, q, g, b):
            eng.wait_ge(y_summed, 8 * q + 8)
            for m in range(KD):
                eng.tensor_tensor(yT[:, m, :], yT[:, m, :], bank[6][:, :], ALU.subtract).then_inc(c_ready, 1)
            eng.wait_ge(rs_ready, q + 1)
            for m in range(KD):
                if 8 * q + m >= 2:
                    eng.wait_ge(x_ready, 8 * q + m - 1)
                eng.scalar_tensor_tensor(tmp[:, m % 2, :], yT[:, m, :], g[:, m:m + 1], rs,
                                         ALU.mult, ALU.mult).then_inc(t_ready, 1)

        def pool_ln(eng, q, b):
            for m in range(KD):
                eng.wait_ge(t_ready, 8 * q + m + 1)
                eng.tensor_scalar(xT[:, m, :], tmp[:, m % 2, :], b[:, m:m + 1], None, ALU.add).then_inc(x_ready, 1)

        def act_ln(eng, q):
            for m in range(KD):
                eng.wait_ge(c_ready, 8 * q + m + 1)
                eng.wait_ge(sq_used, 8 * q + m + 1)
                eng.activation(sq[:, m % 2, :], yT[:, m, :], ACT.Square).then_inc(sq_ready, 1)
            act_root(eng, q, EPS_LN, 7)

        with nc.Block() as block:
            @block.sync
            def _(sp):
                sp.sem_clear(io)
        with nc.Block() as block:
            a0 = 64
            onehot = mix[0:33, a0:a0 + 640]
            rb = mix[0:33, a0 + 640:a0 + 648]
            rows8 = mix[0:8, a0 + 648:a0 + 1288]
            flip = mix[:, a0 + 1288:a0 + 1288 + P]
            turned = mix[:, a0 + 1500:a0 + 1500 + NSA * S].rearrange("p (h s) -> p h s", h=NSA)

            @block.sync
            def _(sp):
                sp.dma_start(onehot, t["onehot"]).then_inc(io, 16)
                sp.dma_start(rb[0:32, :], t["rel_bias"]).then_inc(io, 16)
                sp.dma_start(rb[32:33, :], t["one8"]).then_inc(io, 16)
                sp.dma_start(flip, t["flip"]).then_inc(io, 16)
                sp.wait_ge(c_done, 2)
                sp.dma_start(t["spread"], rows8).then_inc(w_in1, 16)
                sp.wait_ge(w_in1, 16)
                sp.dma_start(turned, bass.AP(tensor=t["spread"].tensor, offset=0,
                                             ap=[[1, P], [640, NSA], [1, S]])).then_inc(par_in, 16)
                sp.wait_ge(par_in, 16)
                sp.wait_ge(c_done, 2 + NSA)
                sp.dma_start(t["bias"], tab2).then_inc(par_in, 16)
                sp.wait_ge(par_in, 32)

            @block.tensor
            def _(pe):
                pe.wait_ge(io, 64)
                for n, c in enumerate((0, 320)):
                    pe.matmul(bank[n][0:8, 0:320], rb, onehot[:, c:c + 320], start=True, stop=True).then_inc(c_out, 1)
                pe.wait_ge(par_in, 16)
                for h in range(NSA):
                    if h == 0:
                        pe.wait_ge(c_done, 2)
                    if h >= 2:
                        pe.wait_ge(c_done, 2 + h - 1)
                    pe.matmul(bank[h % 2][:, :], flip, turned[:, h, :], start=True, stop=True).then_inc(c_out, 1)

            @block.vector
            def _(dve):
                for n, c in enumerate((0, 320)):
                    dve.wait_ge(c_out, n + 1)
                    dve.tensor_copy(rows8[:, c:c + 320], bank[n][0:8, 0:320]).then_inc(c_done, 1)
                for h in range(NSA):
                    dve.wait_ge(c_out, 2 + h + 1)
                    dve.tensor_copy(tab2[:, h, :], bank[h % 2][:, :]).then_inc(c_done, 1)

        with nc.Block() as block:
            @block.sync
            def _(sp):
                for s in nsem.values():
                    sp.sem_clear(s)

        n_in2, n_vg = 0, 24
        n_out2 = n_vg + len(VG_ROWS)
        n_ffn2 = n_out2 + KD
        total_slots[0] = n_ffn2 + FFN_SLOTS
        widths += [WIDE] * n_vg + [c * VG for c in VG_ROWS]

        with nc.Fori(0, DEPTH) as layer:
            with nc.Block() as block:
                @block.sync
                def _(sp):
                    stream(sp, layer, t["w8_2"], 0, 2, n_in2, WIDE)
                    sp.dma_start(par, of_layer(layer, "par2")).then_inc(par_in, 16)
                    sp.dma_start(small[:, 0:32], of_layer(layer, "ln2")).then_inc(par_in, 16)
                    sp.dma_start(flags, of_layer(layer, "flags")).then_inc(par_in, 16)
                    sp.dma_start(T2[:, 2:4, :], of_layer(layer, "lbp")).then_inc(par_in, 16)
                    sp.dma_start(mix[:, forget_at + 4096:forget_at + 6144], t["table2"]).then_inc(par_in, 16)
                    sp.dma_start(valid, t["valid"]).then_inc(par_in, 16)
                    stream(sp, layer, t["w8_2"], 2, 22, n_in2 + 2, WIDE)
                    sp.dma_start(w1k, of_layer(layer, "w1k")).then_inc(w_in1, 16)
                    sp.dma_start(w1v, of_layer(layer, "w1v")).then_inc(w_in1, 16)
                    for k, c in enumerate(VG_ROWS):
                        load(sp, n_vg + k, t["vg_2"][bass.ds(layer, 1), k, :, 0:c * VG].rearrange("a p n -> (a p) n"), c * VG)
                    stream(sp, layer, t["w8_2"], 24, 2, n_out2, WIDE)
                    sp.wait_ge(ho_ready, HU)
                    sp.dma_start(tab2, t["bias"]).then_inc(tab_in, 16)
                    stream(sp, layer, t["w8_2"], 26, KD - 2 + A, n_out2 + 2, WIDE)
                    stream_down(sp, layer, t["down_2"], 0, n_ffn2 + A)

                @block.tensor
                def _(pe):
                    pe_proj_T(pe, n_in2, 16, 0)
                    pe_proj_N(pe, n_in2 + 16, 0)
                    pe_proj_N(pe, n_in2 + 20, 1)
                    pe_proj_N(pe, n_vg, 2, VG, VG_ROWS)
                    pe_compress(pe)
                    pe.wait_ge(vp_free, 12)
                    pe.wait_ge(c_done, 2)
                    pe.wait_ge(par_in, 96)
                    pe_hgrn_keys(pe)
                    pe_hgrn(pe)
                    pe_nsa(pe)
                    pe.wait_ge(o_taken, 4)
                    pe.wait_ge(hmix, 12)
                    pe_out(pe, n_out2, ln_free(0), ln_add(0))
                    for m in range(KD):
                        sum_square(pe, 0, m, on=7)
                    pe_ffn(pe, 0, n_ffn2, 8, ln_free(1), ln_add(1))
                    for m in range(KD):
                        sum_square(pe, 1, m, on=7)

                @block.scalar
                def _(act):
                    act.preload_act_table_set(EXP_LN)
                    act_round(act, 0, of_x, None)
                    hi(act, 0)
                    hi(act, 1)
                    act_proj_T(act, n_in2, [1.0] * 8 + [-DH ** -0.5] * 4 + [1.0] * 4)
                    act_proj_N(act, n_in2 + 16, 8 + len(VG_ROWS))
                    act.wait_ge(vp_free, 12)
                    act.activation(gate, vg[:, :, 256:280], ACT.Exp, scale=-1.0).then_inc(gate_ready, 1)
                    act_compress(act)
                    act.preload_act_table_set(EXP_LN)
                    act_forget(act)
                    for h in range(HG):
                        act.activation(projT[:, HGT + h, :], projT[:, HGT + h, :], ACT.Silu).then_inc(silu_g, 1)
                    act.preload_act_table_set(EXP_LN)
                    act_hgrn_keys(act)
                    act_hgrn(act)
                    act_nsa(act)
                    for m in range(KD):
                        hi(act, n_out2 + m + 2)
                    act_ln(act, 0)
                    act_round(act, 8, of_x, (x_ready, 0))
                    act_silu(act, 0, n_ffn2)
                    act_down(act, n_ffn2 + A, lambda m, i, per: None)
                    act_ln(act, 1)

                @block.vector
                def _(dve):
                    dve.sem_inc(g_free, 2)
                    dve.sem_inc(sq_used, 2)
                    dve.sem_inc(y_done, 2)
                    dve.wait_ge(par_in, 96)
                    dve_windows(dve)
                    dve_proj_N(dve, n_in2 + 16, LF)
                    dve_proj_N(dve, n_in2 + 20, HV)
                    dve_proj_N(dve, n_vg, vg, VG, len(VG_ROWS))
                    dve_compress(dve)
                    dve_forget(dve)
                    dve_gates(dve)
                    dve_hgrn_keys(dve)
                    dve_hgrn(dve)
                    dve_nsa(dve)
                    for m in range(KD):
                        dve_sum(dve, 0, n_out2, 1, m)
                    dve_ln(dve, 0, g1, b1)
                    dve_ffn(dve, 0, n_ffn2)
                    with dve.Fori(0, KD // 2) as i:
                        for m in range(2):
                            dve_sum(dve, 1, n_ffn2 + A, 3, m, i, 2)
                    dve_ln(dve, 1, g2, b2)

                @block.gpsimd
                def _(pool):
                    pool_rest(pool, 0, of_x)
                    los(pool, 0, n_out2 + 2)
                    pool_hgrn(pool)
                    los(pool, n_out2 + 2, n_ffn2 + 2)
                    pool_ln(pool, 0, b1)
                    pool_rest(pool, 8, of_x)
                    pool_ffn(pool, n_ffn2)
                    pool_ln(pool, 1, b2)

            with nc.Block() as block:
                @block.sync
                def _(sp):
                    for s in nsem.values():
                        sp.sem_clear(s)

        with nc.Block() as block:
            @block.sync
            def _(sp):
                sp.dma_start(t["out"], xT[:, :, :]).then_inc(io, 16)
                sp.wait_ge(io, 16)


def alibi(n):
    return 2.0 ** (-8.0 * np.arange(1, n + 1, dtype=np.float32) / np.float32(n))


def constants():
    p = np.arange(P)[:, None]
    c = np.arange(S)[None, :]
    dist = p + (S - P) - c
    count = (dist <= 128).astype(np.int64) + (dist % 4 == 0) + (dist % 16 == 0)
    mult = np.where((dist >= 0) & (count > 0), count, 1)
    dil = [np.where((dist >= 0) & (count > 0), sl * dist - np.log(mult), BIG) for sl in alibi(DIL)]
    dif = [np.where(dist >= 0, sl * dist, BIG) for sl in alibi(DIFF)]
    table1 = np.stack(dil + dif, 1).reshape(P, -1).astype(np.float32)
    j, k = np.arange(P)[:, None], np.arange(P)[None, :]
    mats = np.zeros((7, P, P), np.float32)
    mats[0] = -1.0
    mats[1] = 1.0 / D
    mats[2] = (j // DH == k // DH) / DH
    mats[3] = -1.0 * (j >= k)
    mats[4] = np.eye(P)
    mats[5] = j > k
    mats[6] = np.where(j >= k, -BIG, 0.0)
    return table1, np.ascontiguousarray(mats.transpose(1, 0, 2))


def columns(w):
    k, n = w.shape
    return w.reshape(k // P, P, n // P, P).transpose(2, 1, 0, 3).reshape(n // P, P, k)


def rows(w, width, per):
    k, n = w.shape
    return w.reshape(k // P // per, per, P, width).transpose(0, 2, 1, 3).reshape(-1, P, per * width)


def parts(v, counts, w):
    out = np.zeros((len(counts), P, WIDE), v.dtype)
    k = 0
    for i, c in enumerate(counts):
        out[i, :, 0:c * w] = v[k:k + c].transpose(1, 0, 2).reshape(P, c * w)
        k += c
    return out


def down(w):
    return np.concatenate([parts(w[:, m * P:(m + 1) * P].reshape(KF, P, P), DOWN, P) for m in range(KD)])


def gate_up(g, u):
    return np.stack([columns(g), columns(u)], 1).reshape(2 * KF, P, WIDE)


def by_partition(v):
    return v.reshape(-1, KD, P).transpose(2, 0, 1).reshape(P, -1)


def laid_out(x, norm_gains, w_ffn_gate, w_ffn_up, w_ffn_down, w_in, w_out, diff_lambda, diff_subln_gain, **second):
    a = {}
    a["xT"] = x[0].T.reshape(KD, P, S).transpose(1, 0, 2)
    a["table1"], a["mats"] = constants()
    w8, w11 = [], []
    for l in range(DEPTH):
        c = np.cumsum([0, 384, 384, 384, 256, 256, 256, 384, 384, 384])
        part = [w_in[l][:, c[i]:c[i + 1]] for i in range(9)]
        qk = np.concatenate([part[i] for i in (0, 1, 3, 4, 6, 7)], 1)
        v = np.concatenate([part[i] for i in (2, 5, 8)], 1)
        w8 += [gate_up(w_ffn_gate[l, 0], w_ffn_up[l, 0]), columns(qk), rows(v[:, :512], 512, 2),
               rows(v[:, 512:], 512, 2), columns(w_out[l]), gate_up(w_ffn_gate[l, 1], w_ffn_up[l, 1])]
        w11 += [down(w_ffn_down[l, 0]), down(w_ffn_down[l, 1])]
    a["w8_1"] = np.concatenate(w8).reshape(DEPTH, -1, P, WIDE)
    a["down_1"] = np.concatenate(w11).reshape(DEPTH, -1, P, WIDE)
    a["gains1"] = np.stack([by_partition(norm_gains[l]) for l in range(DEPTH)])
    init = [0.8 - 0.6 * math.exp(-0.3 * l) for l in range(DEPTH)]
    lam = diff_lambda[:, [0, 2, 1, 3], :].reshape(DEPTH, 1, 128)
    tail = np.array(init, np.float32).reshape(DEPTH, 1, 1)
    a["lam"] = np.broadcast_to(np.concatenate([lam, tail], 2), (DEPTH, P, 129))
    gain = np.concatenate([diff_subln_gain] * 2, 1)[:, :, None]
    keep = np.broadcast_to(np.array([1.0 - i for i in init], np.float32).reshape(DEPTH, 1, 1), (DEPTH, P, 1))
    a["subg"] = np.concatenate([gain, keep], 2)
    laid_out_2(a, **second)
    return {k: np.ascontiguousarray(v) for k, v in a.items()}


def bucket(n):
    exact = 16
    nf = np.maximum(n, 1).astype(np.float32)
    large = exact + (np.log(nf / np.float32(exact)) / np.float32(math.log(128 / exact)) * np.float32(16)).astype(np.int32)
    return np.where(n < exact, np.maximum(n, 0), np.minimum(large, 31))


def constants_2():
    x = np.arange(640)
    dist = S - 1 - x
    onehot = np.zeros((33, 640), np.float32)
    seen = dist >= 0
    onehot[bucket(dist)[seen], x[seen]] = -1.0
    onehot[32, ~seen] = BIG
    s, u = np.arange(P)[:, None], np.arange(P)[None, :]
    span, mask = np.zeros((P, 8, P), np.float32), np.zeros((P, 8, P), np.float32)
    for l in range(LEVELS):
        half = (P // 2) >> l
        mid = u // (2 * half) * (2 * half) + half
        right = u >= mid
        span[:, l] = np.where(right, (s >= mid) & (s <= u), (s > u) & (s < mid))
        mask[:, l] = right & (s // (2 * half) == u // (2 * half)) & (s < mid)
    span[:, 7] = s <= u
    mask[:, 7] = s == u
    return onehot, np.concatenate([span.reshape(P, -1), mask.reshape(P, -1)], 1)


def laid_out_2(a, w_in_2, hg_lb_param_2, hg_norm_w_2, cmp_pos_k_2, cmp_w1_k_2, cmp_w2_k_2, cmp_pos_v_2,
               cmp_w1_v_2, cmp_w2_v_2, rel_bias_2, w_out_2, ln1_g_2, ln1_b_2, w_ffn_gate_2,
               w_ffn_up_2, w_ffn_down_2, ln2_g_2, ln2_b_2):
    a["onehot"], a["table2"] = constants_2()
    a["rel_bias"] = rel_bias_2
    a["flip"] = np.eye(P, dtype=np.float32)[::-1]
    a["one8"] = np.ones((1, NSA), np.float32)
    a["valid"] = (np.arange(P) >= CMP_END).astype(np.float32)[:, None]
    w8, w11, vg, w1, par = [], [], [], {"k": [], "v": []}, []
    ln = []
    order = [h * DH + g * 4 * DH + d for h in range(4) for g in range(2) for d in range(DH)]
    for l in range(DEPTH):
        c = np.cumsum([0, 512, 512, 512, 512, 512] + [128] * 6 + [24])
        hq, hf, hi, hg, nq, kc, vc, ks, vs, kw, vw, gt = (w_in_2[l][:, c[i]:c[i + 1]] for i in range(12))
        turned = np.concatenate([hq, hg, nq[:, order], kc, vc, ks, kw], 1)
        w8 += [columns(turned), rows(hf, 512, 2), rows(hi, 512, 2), columns(w_out_2[l]),
               gate_up(w_ffn_gate_2[l], w_ffn_up_2[l])]
        vg.append(parts(np.concatenate([vs, vw, gt], 1).reshape(KD, P, VG), VG_ROWS, VG))
        w11.append(down(w_ffn_down_2[l]))
        for kind, w in (("k", cmp_w1_k_2), ("v", cmp_w1_v_2)):
            v = w[l].reshape(32, DH, P).transpose(1, 0, 2).reshape(DH, -1)
            w1[kind].append(np.concatenate([v, v], 0))
        pos = [np.concatenate([p[l].T] * 2, 0) for p in (cmp_pos_k_2, cmp_pos_v_2)]
        par.append(np.concatenate(pos + [cmp_w2_k_2[l], cmp_w2_v_2[l], hg_norm_w_2[l][:, None]], 1))
        ln.append(np.concatenate([by_partition(v[l]) for v in (ln1_g_2, ln1_b_2, ln2_g_2, ln2_b_2)], 1))
    a["w8_2"] = np.concatenate(w8).reshape(DEPTH, -1, P, WIDE)
    a["down_2"] = np.concatenate(w11).reshape(DEPTH, -1, P, WIDE)
    a["vg_2"] = np.stack(vg)
    a["w1k"], a["w1v"] = np.stack(w1["k"]), np.stack(w1["v"])
    a["par2"], a["ln2"] = np.stack(par), np.stack(ln)
    a["flags"] = np.broadcast_to(np.array([[[0, 0, -BIG, 0]], [[1, -1, 0, 0]]], np.float32), (DEPTH, P, 4))
    a["lbp"] = np.broadcast_to(hg_lb_param_2.reshape(1, 1, DEPTH * 512), (DEPTH, P, DEPTH * 512))


def kernel(**inputs):
    import concourse.bacc as bacc
    from concourse.bass_utils import run_bass_kernel_spmd

    arrays = laid_out(**{k: np.asarray(v) for k, v in inputs.items()})
    nc = bacc.Bacc("TRN2", target_bir_lowering=False, num_devices=1)
    t = {k: nc.dram_tensor("in_" + k, v.shape, mybir.dt.from_np(v.dtype), kind="ExternalInput").ap()
         for k, v in arrays.items()}
    t["spread"] = nc.dram_tensor("spread", (NSA, 640), F32).ap()
    t["bias"] = nc.dram_tensor("bias", (P, NSA, S), F32).ap()
    t["out"] = nc.dram_tensor("out", (P, KD, S), F32, kind="ExternalOutput").ap()
    build(nc, t)
    r = run_bass_kernel_spmd(nc, [{"in_" + k: v for k, v in arrays.items()}], core_ids=[0])
    out = r.results[0]["out"]
    return np.ascontiguousarray(out.transpose(1, 0, 2).reshape(D, S).T)[None]
```

```python
from contextlib import ExitStack
import math

import numpy as np

import concourse.bass as bass
from concourse import mybir

F32 = mybir.dt.float32
F32R = mybir.dt.float32r
BF16 = mybir.dt.bfloat16
ALU = mybir.AluOpType
ACT = mybir.ActivationFunctionType
AX_X = mybir.AxisListType.X

P = 128
S = 512
NT = S // P
D = 1024
KD = D // P
FF = 2816
KF = FF // P
DEPTH = 2
NSLOT = 2
WIDE = KD * P
DOWN = (8, 7, 7)
assert sum(DOWN) == KF
BIG = 1e30
EPS_RMS = 1e-6
EXP_LN = "natural_log_exp_and_others"
EPS_LN = 1e-5
ALPHA = (2.0 * DEPTH) ** 0.25

DIL, DIFF, SB = 6, 4, 6
DH = 64
QA, KA, QB, KB, QC, KC = 0, 3, 6, 8, 10, 13
HG = 4
NSA = 8
LEVELS = 7
CMP_END = 31
NCMP = 31
VG = 280
VG_ROWS = (2, 2, 2, 2)


class Layout:

    def __init__(self, tensor, width):
        self.tensor, self.width, self.at = tensor, width, 0

    def take(self, n):
        a = self.at
        self.at += n
        assert self.at <= self.width, (self.at, self.width)
        return self.tensor[:, a:self.at]


def triangle(a):
    return [0, 512, 896, 1152][a]


def build(nc, t):
    ctx = ExitStack()
    with ctx:
        bank = [ctx.enter_context(nc.psum_tensor(f"bank{i}", [P, 512], F32)) for i in range(8)]
        base = -(-nc.sbuf_base // 64) * 64

        def at(name, floats, shape, dt=F32):
            n = int(np.prod(shape[1:])) * (2 if dt == BF16 else 4)
            assert base + 4 * floats + n <= nc.sbuf_usable_end, name
            return nc.alloc_sbuf_tensor_at(name, shape, dt, offset=base + 4 * floats)

        xT = at("xT", 0, [P, KD, S])
        yT = at("yT", 4096, [P, KD, S])
        hH = at("hH", 8192, [P, KD, S], F32R)
        hL = at("hL", 12288, [P, KD, S], F32R)
        ring = at("ring", 16384, [P, NSLOT, WIDE])
        wH = at("wH", 18432, [P, NSLOT, WIDE], F32R)
        wL = at("wL", 20480, [P, NSLOT, WIDE], F32R)
        work = at("work", 22528, [P, 3072])
        small = at("small", 25600, [P, 512])
        mats = at("mats", 26112, [P, 7, P])
        matsb = at("matsb", 27008, [P, 2, P], BF16)
        M = 27136
        guH = at("guH", M, [P, KF, S], F32R)
        guL = at("guL", M + KF * S, [P, KF, S], F32R)
        spareH = at("spareH", M + (2 * KF - 4) * S, [P, WIDE], F32R)
        spareL = at("spareL", M + (2 * KF - 2) * S, [P, WIDE], F32R)
        gfull = at("gfull", M + 2 * KF * S, [P, 2, S])
        MW = ((nc.sbuf_usable_end - base) // 4 - M - S) // 16 * 16
        spH = at("spH", M + 16 * S, [P, 2, 1280], F32R)
        spL = at("spL", M + 16 * S + 2560, [P, 2, 1280], F32R)
        negR = at("negR", M + MW - 2 * P, [P, 2, P], F32R)
        acc = at("acc", M + MW, [P, S])[:, :]
        mix = at("mix", M, [P, MW])
        projT = mix[:, 0:16 * S].rearrange("p (c s) -> p c s", c=16)

        nsem = {}

        def sem(name):
            nsem[name] = ctx.enter_context(nc.semaphore(name))
            return nsem[name]

        slot_in = [sem(f"slot_in{i}") for i in range(NSLOT)]
        w_hi = sem("w_hi")
        w_lo = sem("w_lo")
        slots_done = sem("slots_done")
        xsq_ready = sem("xsq_ready")
        xsq_summed = sem("xsq_summed")
        acc_steps = sem("acc_steps")
        stat_ready = sem("stat_ready")
        g_scaled = sem("g_scaled")
        h_hi = sem("h_hi")
        gsteps = sem("gsteps")
        o_hi = sem("o_hi")
        tab_in = sem("tab_in")
        g_free = sem("g_free")
        silu_ready = sem("silu_ready")
        sq_ready = sem("sq_ready")
        sq_used = sem("sq_used")
        ln_ready = sem("ln_ready")
        rs_ready = sem("rs_ready")
        t_ready = sem("t_ready")
        x_ready = sem("x_ready")
        h_ready = sem("h_ready")
        par_in = sem("par_in")
        par_ready = sem("par_ready")
        seq = sem("seq")
        io = sem("io")
        x_in = [sem(f"x_in{i}") for i in range(4)]
        bias_out = ctx.enter_context(nc.semaphore("bias_out"))
        r_steps = sem("r_steps")
        tp_free = sem("tp_free")
        vp_free = sem("vp_free")
        s_ready = sem("s_ready")
        p_max = sem("p_max")
        p_exp = sem("p_exp")
        p_rec = sem("p_rec")
        p_norm = sem("p_norm")
        p_turn = sem("p_turn")
        p_back = sem("p_back")
        o_ready = sem("o_ready")
        o_taken = sem("o_taken")
        z_ready = sem("z_ready")
        z_abs = sem("z_abs")
        z_exp = sem("z_exp")
        z_ln = sem("z_ln")
        z_sp = sem("z_sp")
        z_cum = sem("z_cum")
        z_parts = sem("z_parts")
        z_w = sem("z_w")
        z_pv = sem("z_pv")
        d_sq = sem("d_sq")
        d_sum = sem("d_sum")
        d_rs = sem("d_rs")
        d_out = sem("d_out")
        y_done = sem("y_done")
        c_ready = sem("c_ready")
        w_in1 = sem("w_in1")
        win = sem("win")
        c_hid = sem("c_hid")
        c_act = sem("c_act")
        c_out = sem("c_out")
        c_done = sem("c_done")
        f_act = sem("f_act")
        f_dve = sem("f_dve")
        k_turn = sem("k_turn")
        k_back = sem("k_back")
        suf_ready = sem("suf_ready")
        suf_exp = sem("suf_exp")
        kd_ready = sem("kd_ready")
        dec_ready = sem("dec_ready")
        dec_exp = sem("dec_exp")
        q_dec = sem("q_dec")
        k_dec = sem("k_dec")
        a_ready = sem("a_ready")
        a_mask = sem("a_mask")
        a_sum = sem("a_sum")
        u_ready = sem("u_ready")
        st_ready = sem("st_ready")
        ho_ready = sem("ho_ready")
        hsq = sem("hsq")
        hsum = sem("hsum")
        hrs = sem("hrs")
        hout = sem("hout")
        hmix = sem("hmix")
        silu_g = sem("silu_g")
        gate_ready = sem("gate_ready")

        sc = Layout(work, 3072)
        sq = sc.take(2 * S).rearrange("p (b s) -> p b s", b=2)
        lnv = sc.take(S)
        rs = sc.take(S)
        tmp = sc.take(2 * S).rearrange("p (b s) -> p b s", b=2)
        gnext = small[:, 344:352]
        rlog = small[:, 340:344]
        rcol = small[:, 336:340]

        NEG1, MEAN, HEAD_MEAN, NEG_FROM, IDENT, AFTER, MASK = range(7)
        onesD, blk64, negL, ident, negones = (mats[:, i, :] for i in (MEAN, HEAD_MEAN, NEG_FROM, IDENT, NEG1))

        def slot_sem(eng, n, i=0, per=0):
            eng.wait_ge(slot_in[n % NSLOT], i * (16 * per // NSLOT) + 16 * (n // NSLOT + 1))

        def landed(eng, n, i=0, per=0):
            eng.wait_ge(w_lo, i * per + (n + 1))

        spares = set()

        def parts_of(n, per=0):
            if per == 0 and n in spares:
                return spareH[:, :], spareL[:, :]
            return wH[:, n % NSLOT, :], wL[:, n % NSLOT, :]

        def product(eng, out, n, c0, c1, hi, lo, first, last, per=0):
            a, b = (v[:, c0:c1] for v in parts_of(n, per))
            eng.matmul(out, a, hi, start=first, stop=False)
            eng.matmul(out, a, lo, start=False, stop=False)
            return eng.matmul(out, b, hi, start=False, stop=last)

        def load(eng, n, src, width, i=0, per=0):
            if per or n >= NSLOT:
                eng.wait_ge(w_lo, i * per + (n - NSLOT + 1))
            eng.dma_start(ring[:, n % NSLOT, 0:width], src).then_inc(slot_in[n % NSLOT], 16)

        def stream(eng, layer, arr, first, count, n0, width):
            def src(k):
                return arr[bass.ds(layer, 1), bass.ds(k, 1), :, 0:width].rearrange("a b p n -> (a b p) n")
            loops = count // NSLOT
            if loops:
                with eng.Fori(0, loops) as i:
                    for k in range(NSLOT):
                        load(eng, n0 + k, src(i * NSLOT + (first + k)), width, i, NSLOT)
            for k in range(loops * NSLOT, count):
                load(eng, n0 + k, src(first + k), width)

        def stream_down(eng, layer, arr, first, n0):
            with eng.Fori(0, KD // 2) as i:
                for k in range(6):
                    w = DOWN[k % 3] * P
                    load(eng, n0 + k, arr[bass.ds(layer, 1), bass.ds(i * 6 + (first + k), 1), :, 0:w]
                         .rearrange("a b p n -> (a b p) n"), w, i, 6)

        def hi(eng, n, width=WIDE, i=0, per=0):
            if n >= total_slots[0]:
                return
            slot_sem(eng, n, i, per)
            if per or (n >= NSLOT and n not in spares):
                eng.wait_ge(slots_done, i * per + (n - NSLOT + 1))
            eng.activation(parts_of(n, per)[0][:, 0:width], ring[:, n % NSLOT, 0:width], ACT.Copy).then_inc(w_hi, 1)

        def lo(eng, n, width=WIDE, i=0, per=0):
            if n >= total_slots[0]:
                return
            eng.wait_ge(w_hi, i * per + (n + 1))
            h, l = parts_of(n, per)
            eng.tensor_tensor(l[:, 0:width], ring[:, n % NSLOT, 0:width], h[:, 0:width],
                              ALU.subtract).then_inc(w_lo, 1)

        total_slots = [3]
        widths = []

        def width(n):
            return widths[n] if n < len(widths) else WIDE

        def los(eng, a, b):
            for n in range(a, b):
                lo(eng, n, width(n))

        def add_squares(eng, r, m, i=0, per=0):
            eng.wait_ge(sq_ready, i * per + (8 * r + m + 1))
            if m == 0:
                eng.tensor_copy(acc, sq[:, 0, :]).then_inc(sq_used, 1)
                return
            if m == KD - 1:
                eng.wait_ge(stat_ready, 2 * r + 2)
                eng.sem_inc(sq_used, 1)
                return
            eng.wait_ge(sq_used, i * per + (8 * r + m + 2))
            eng.tensor_tensor(acc, acc, sq[:, m % 2, :], ALU.add).then_inc(sq_used, 1)

        def sum_x_squares(eng, p):
            eng.wait_ge(xsq_ready, 8 * p + 8)
            eng.tensor_reduce(acc, yT[:, :, :].rearrange("p c s -> p s c"), AX_X, ALU.add).then_inc(xsq_summed, 1)

        def pe_stat_out(eng, r):
            eng.wait_ge(sq_used, 8 * r + 7 + 2)
            eng.matmul(bank[6][:, :], onesD, acc, start=True, stop=False, skip_group_check=True)
            eng.wait_ge(sq_ready, 8 * r + 8)
            eng.matmul(bank[6][:, :], onesD, sq[:, 1, :], start=False, stop=True,
                       skip_group_check=True).then_inc(stat_ready, 1)

        def pe_stat_in(eng, p, columns=False):
            eng.wait_ge(xsq_summed, p + 1)
            if columns:
                for tile in range(NT):
                    eng.matmul(bank[7][:, tile:tile + 1], acc[:, tile * P:(tile + 1) * P],
                               onesD[:, 0:1], start=True, stop=True, skip_group_check=True)
            eng.matmul(bank[6][:, :], onesD, acc, start=True, stop=True).then_inc(stat_ready, 1)

        def act_root(eng, q, eps, on=6):
            if on == 6:
                eng.wait_ge(stat_ready, q + 1)
            else:
                eng.wait_ge(sq_used, 8 * q + 8 + 2)
            eng.activation(lnv, bank[on][:, :], ACT.Ln, bias=eps).then_inc(ln_ready, 1)
            eng.wait_ge(ln_ready, q + 1)
            eng.activation(rs, lnv, ACT.Exp, scale=-0.5).then_inc(rs_ready, 1)

        def act_split(eng, xr, gains, squares):
            for m in range(KD):
                if xr is None:
                    eng.wait_ge(x_in[m // 2], 16 if m // 2 else 32)
                else:
                    eng.wait_ge(x_ready, xr + m + 1)
                if gains is None:
                    eng.activation(hH[:, m, :], xT[:, m, :], ACT.Copy).then_inc(h_hi, 1)
                else:
                    eng.activation(hH[:, m, :], xT[:, m, :], ACT.Copy, scale=gains[:, m:m + 1]).then_inc(h_hi, 1)
                if squares:
                    eng.activation(yT[:, m, :], xT[:, m, :], ACT.Square).then_inc(xsq_ready, 1)

        def rest(eng, h0, m, gains):
            eng.wait_ge(h_hi, h0 + m + 1)
            if gains is None:
                eng.tensor_tensor(hL[:, m, :], xT[:, m, :], hH[:, m, :], ALU.subtract).then_inc(h_ready, 1)
            else:
                eng.scalar_tensor_tensor(hL[:, m, :], xT[:, m, :], gains[:, m:m + 1], hH[:, m, :],
                                         ALU.mult, ALU.subtract).then_inc(h_ready, 1)

        def normed(eng, n, m, g, b):
            if n + m >= 2:
                eng.wait_ge(x_ready, n + m - 1)
            eng.scalar_tensor_tensor(tmp[:, m % 2, :], yT[:, m, :], g[:, m:m + 1], rs,
                                     ALU.mult, ALU.mult).then_inc(t_ready, 1)
            if m == 0:
                eng.wait_ge(t_ready, n + 1)
                if b is None:
                    eng.tensor_tensor(xT[:, 0, :], xT[:, 0, :], tmp[:, 0, :], ALU.add).then_inc(x_ready, 1)
                else:
                    eng.tensor_scalar(xT[:, 0, :], tmp[:, 0, :], b[:, 0:1], None, ALU.add).then_inc(x_ready, 1)

        def dve_post(eng, q, n, g, h0=None, gains=None, b=None):
            eng.wait_ge(rs_ready, q + 1)
            for m in range(KD + 2):
                if m < KD:
                    normed(eng, n, m, g, b)
                if m >= 2 and h0 is not None:
                    rest(eng, h0, m - 2, gains)

        def pool_post(eng, n):
            for m in range(1, KD):
                eng.wait_ge(t_ready, n + m + 1)
                eng.tensor_tensor(xT[:, m, :], xT[:, m, :], tmp[:, m % 2, :], ALU.add).then_inc(x_ready, 1)

        def pair_of(eng, n, h0, banks=(0, 2)):
            landed(eng, n + 1)
            for kc in range(KD):
                eng.wait_ge(h_ready, h0 + kc + 1)
                for u, out in enumerate(bank[b][:, :] for b in banks):
                    mm = product(eng, out, n + u, kc * P, (kc + 1) * P, hH[:, kc, :], hL[:, kc, :],
                                 kc == 0, kc == KD - 1)
                    if kc == KD - 1:
                        mm.then_inc(slots_done, 1)

        def pe_ffn(eng, c, n0, h0, free, stat=None):
            def slot(i, k, u, per=0):
                n = n0 + 2 * k + u
                landed(eng, n, i, 4)
                for kc in range(KD):
                    mm = product(eng, bank[k + 2 * u][:, :], n, kc * P, (kc + 1) * P,
                                 hH[:, kc, :], hL[:, kc, :], kc == 0, kc == KD - 1, per)
                mm.then_inc(slots_done, 1)

            if n0:
                eng.wait_ge(g_free, KF * c + 1)
                pair_of(eng, n0, h0)
            eng.wait_ge(g_free, KF * c + 2)
            slot(0, 1, 0)
            if stat is not None:
                pe_stat_in(eng, stat)
            slot(0, 1, 1)
            with eng.Fori(1, KF // 2) as i:
                for k in range(2):
                    eng.wait_ge(g_free, i * 2 + (KF * c + k + 1))
                    for u in range(2):
                        slot(i, k, u, 4)
            n1 = n0 + 2 * KF

            def down(m, i=0, per=0, first=False):
                free(eng, m, i, per)
                kc = 0
                for s, tiles_ in enumerate(DOWN):
                    n = n1 + 3 * m + s
                    landed(eng, n, i, 3 * per)
                    for b in range(tiles_):
                        if first and kc in (0, KF - 2, KF - 1):
                            eng.wait_ge(g_free, KF * (c + 1) + 2 - (2, 1, 0)[(0, KF - 2, KF - 1).index(kc)])
                        mm = product(eng, bank[4 + m % 2][:, :], n, b * P, (b + 1) * P,
                                     guH[:, kc, :], guL[:, kc, :], kc == 0, kc == KF - 1)
                        kc += 1
                    mm.then_inc(slots_done, 1)

            down(0, first=True)
            down(1)
            with eng.Fori(0, 3) as i:
                down(2, i, 2)
                down(3, i, 2)

        def rms_free(q):
            def wait(eng, m, i=0, per=0):
                if 8 * q + m >= 2:
                    eng.wait_ge(sq_ready, i * per + (8 * q + m - 1))
                    eng.wait_ge(y_done, i * per + (8 * q + m + 1))
            return wait

        def ln_free(q):
            def wait(eng, m, i=0, per=0):
                eng.wait_ge(y_done, i * per + (8 * q + m + 1))
            return wait

        def act_y(eng, r, n1, per_tile, m, i=0, per=0):
            eng.wait_ge(slots_done, i * (per * per_tile) + (n1 + per_tile * (m + 1)))
            eng.wait_ge(sq_used, i * per + (8 * r + m + 1))
            eng.activation(sq[:, m % 2, :], bank[4 + m % 2][:, :], ACT.Square).then_inc(sq_ready, 1)

        def dve_y(eng, r, m, i=0, per=0):
            add_squares(eng, r, m, i, per)
            dst = yT[:, m, :] if per == 0 else yT[:, bass.ds(i * per + m, 1), :].rearrange("p a s -> p (a s)")
            eng.tensor_copy(dst, bank[4 + m % 2][:, :]).then_inc(y_done, 1)

        def dve_ys(eng, r):
            dve_y(eng, r, 0)
            with eng.Fori(0, 3) as i:
                for m in (1, 2):
                    dve_y(eng, r, m, i, 2)
            dve_y(eng, r, KD - 1)

        def act_silu(eng, c, n0, stat=None):
            def silu(k, i=0):
                if stat is None:
                    eng.wait_ge(g_free, i * 2 + (KF * c + k + 1))
                    eng.wait_ge(slots_done, i * 4 + (n0 + 2 * k + 1))
                    src = bank[k][:, :]
                else:
                    eng.wait_ge(g_scaled, i * 2 + (KF * c + k + 1))
                    src = tmp[:, k, :]
                eng.activation(tmp[:, k, :], src, ACT.Silu).then_inc(silu_ready, 1)

            if n0:
                hi(eng, n0 + 2)
            hi(eng, n0 + 3)
            if stat is not None:
                act_root(eng, stat, EPS_RMS)
            eng.preload_act_table(ACT.Silu)
            for k in range(2):
                silu(k)
                hi(eng, n0 + 4 + k)
            with eng.Fori(1, KF // 2) as i:
                for k in range(2):
                    silu(k, i)
                    hi(eng, n0 + 2 * k + 2, WIDE, i, 4)
                    hi(eng, n0 + 2 * k + 3, WIDE, i, 4)
            eng.preload_act_table_set(EXP_LN)

        def pool_silu(eng, n0):
            for k in range(0 if n0 else 1, 4):
                lo(eng, n0 + 2 + k)
            with eng.Fori(1, KF // 2) as i:
                for k in range(4):
                    lo(eng, n0 + 2 + k, WIDE, i, 4)

        def act_down(eng, n1, take):
            def pair(i, per):
                for m in range(2):
                    for s in range(3):
                        hi(eng, n1 + 3 * m + s + 2, WIDE, i, 3 * per)
                    take(m, i, per)
            with eng.Fori(0, KD // 2 - 1) as i:
                pair(i, 2)
            for m in (KD - 2, KD - 1):
                for s in range(3):
                    hi(eng, n1 + 3 * m + s + 2, WIDE)
                take(m, 0, 0)

        def pool_down(eng, n1):
            with eng.Fori(0, KD // 2 - 1) as i:
                for s in range(6):
                    lo(eng, n1 + s + 2, WIDE, i, 6)
            for s in range(6):
                lo(eng, n1 + 3 * (KD - 2) + s + 2, WIDE)

        def act_ffn(eng, c, r, n0, q):
            act_silu(eng, c, n0, q)
            act_down(eng, n0 + 2 * KF, lambda m, i, per: act_y(eng, r, n0 + 2 * KF, 3, m, i, per))
            act_root(eng, q + 1, EPS_RMS)

        def pool_ffn(eng, n0):
            pool_silu(eng, n0)
            pool_down(eng, n0 + 2 * KF)

        def dve_ffn(eng, c, n0, scaled):
            steps = 3 if scaled else 2
            with eng.Fori(0, KF // 2) as i:
                for k in range(2):
                    g = steps * (KF * c + k)
                    full, up = gfull[:, k, :], bank[2 + k][:, :]
                    at_h, at_l = (v[:, bass.ds(i * 2 + k, 1), :].rearrange("p a s -> p (a s)") for v in (guH, guL))
                    if scaled:
                        eng.wait_ge(slots_done, i * 4 + (n0 + 2 * k + 1))
                        eng.tensor_tensor(tmp[:, k, :], bank[k][:, :], rs, ALU.mult).then_inc(g_scaled, 1)
                    eng.wait_ge(slots_done, i * 4 + (n0 + 2 * k + 2))
                    if scaled:
                        eng.tensor_tensor(full, up, rs, ALU.mult).then_inc(gsteps, 1)
                        g += 1
                        eng.wait_ge(gsteps, i * (2 * steps) + g)
                        up = full
                    eng.wait_ge(silu_ready, i * 2 + (KF * c + k + 1))
                    eng.tensor_tensor(full, tmp[:, k, :], up, ALU.mult).then_inc(gsteps, 1)
                    eng.wait_ge(gsteps, i * (2 * steps) + (g + 1))
                    eng.tensor_copy(at_h, full).then_inc(gsteps, 1)
                    eng.wait_ge(gsteps, i * (2 * steps) + (g + 2))
                    eng.tensor_tensor(at_l, full, at_h, ALU.subtract).then_inc(g_free, 1)

        gcol = small[:, 0:48]
        ghalf = small[:, 48:96]

        N_IN = 24
        T_BANKS = (0, 2)
        V_BANKS = ((3, 4, 5, 6), (7, 3, 4, 5))

        def pe_proj_T(eng, n0, a, z, banks, h0=None, stat=None):
            j = a
            if h0 is not None:
                pair_of(eng, n0, h0, banks[0:2])
                j = a + 2
            for j in range(j, z):
                if j >= len(banks):
                    eng.wait_ge(tp_free, j - len(banks) + 1)
                n = n0 + j - a
                landed(eng, n)
                for kc in range(KD):
                    mm = product(eng, bank[banks[j % len(banks)]][:, :], n, kc * P, (kc + 1) * P,
                                 hH[:, kc, :], hL[:, kc, :], kc == 0, kc == KD - 1)
                mm.then_inc(slots_done, 1)
                if stat is not None and j == 2:
                    pe_stat_in(eng, stat, columns=True)

        def dve_proj_T(eng, n0, scales):
            for j, f in enumerate(scales):
                eng.wait_ge(slots_done, n0 + j + 1)
                eng.scalar_tensor_tensor(projT[:, j, :], bank[j % 3][:, :], f, rs,
                                         ALU.mult, ALU.mult).then_inc(tp_free, 1)

        def act_proj_T(eng, n0, a, z, place, scale, forget):
            for j in range(a, z):
                n = n0 + j - a
                eng.wait_ge(slots_done, n + 1)
                p = place(j)
                eng.activation(projT[:, p, :], bank[T_BANKS[j % 2]][:, :], ACT.Copy, scale=scale(p)).then_inc(tp_free, 1)
                if n:
                    hi(eng, n + 2, width(n + 2))
                if forget:
                    act_forget(eng, j - a)

        def act_hi(eng, n0, slots):
            for n in range(n0, n0 + slots):
                hi(eng, n, width(n))

        def pe_proj_N(eng, n0, banks, w=512, per=(2, 2, 2, 2), taken=None):
            kc = 0
            for s, count in enumerate(per):
                n = n0 + s
                landed(eng, n)
                for k in range(count):
                    a, b = (v[:, k * w:(k + 1) * w] for v in parts_of(n))
                    for tile in range(NT):
                        out = bank[banks[tile]][:, 0:w]
                        if taken and kc == 0:
                            eng.wait_ge(vp_free, taken[tile])
                        x, y = (v[:, kc, tile * P:(tile + 1) * P] for v in (hH, hL))
                        eng.matmul(out, x, a, start=(kc == 0), stop=False)
                        eng.matmul(out, x, b, start=False, stop=False)
                        mm = eng.matmul(out, y, a, start=False, stop=(kc == KD - 1))
                    kc += 1
                mm.then_inc(slots_done, 1)

        def dve_proj_N(eng, n0, banks, dst, w=512, slots=4, scale=None):
            eng.wait_ge(slots_done, n0 + slots)
            for b in range(NT):
                if scale is None:
                    eng.tensor_copy(dst[:, b, :], bank[banks[b]][:, 0:w]).then_inc(vp_free, 1)
                else:
                    eng.tensor_scalar(dst[:, b, :], bank[banks[b]][:, 0:w], scale[:, b:b + 1], None,
                                      ALU.mult).then_inc(vp_free, 1)

        V1 = yT[:, :, :].rearrange("p c s -> p (c s)").rearrange("p (b n) -> p b n", b=NT)
        sc = Layout(mix, MW)
        sc.take(16 * S)
        tab1 = sc.take(10 * S).rearrange("p (h s) -> p h s", h=10)
        PR = 8
        prob = [sc.take(S) for _ in range(PR // 2)]
        probT = sc.take(4 * S * 2).rearrange("p (b j s) -> p b j s", b=2, j=NT)
        stat = sc.take(64)
        absz = sc.take(1280)
        softp = sc.take(2560)
        prob += [softp[:, i * S:(i + 1) * S] for i in range(PR - PR // 2)]
        diag = absz[:, 0:PR * P].rearrange("p (r n) -> p r n", r=PR)
        softp = softp.rearrange("p (r n) -> p r n", r=2)
        wts = probT.rearrange("p b j s -> p b (j s)")
        dsq = sc.take(S)
        dfull = sc.take(2 * S).rearrange("p (n s) -> p n s", n=2)
        negcol = small[:, 97:98]
        subg = small[:, 98:99]
        lamtmp = small[:, 100:140]
        lam_in = small[:, 140:272]
        lamprod = small[:, 272:336].rearrange("p (a n) -> p a n", a=2)

        units = [(h, i) for h in range(DIL + DIFF) for i in range(NT)]
        maps = []
        for u, (h, i) in enumerate(units):
            maps += [(u, 0)] + ([(u, 1)] if h >= DIL else [])

        def operands(h, w):
            if h < DIL:
                lo = (h % 2) * DH
                return QA + h // 2, KA + h // 2, lo, lo + DH
            g = h - DIL
            lo = (g % 2) * DH + w * 32
            return QB + g // 2, KB + g // 2, lo, lo + 32

        def pe_soft(eng):
            eng.wait_ge(tp_free, 16)

            def scores(k):
                u, w = maps[k]
                h, i = units[u]
                q, kk, lo, hi = operands(h, w)
                if k >= 3:
                    eng.wait_ge(p_max, k - 2)
                eng.matmul(bank[k % 3][:, 0:(i + 1) * P], projT[lo:hi, q, i * P:(i + 1) * P],
                           projT[lo:hi, kk, 0:(i + 1) * P], start=True, stop=True).then_inc(s_ready, 1)

            def turn(u):
                h, i = units[u]
                ks = [k for k, (v, _) in enumerate(maps) if v == u]
                eng.wait_ge(p_norm, ks[-1] + 1)
                if u == 0:
                    eng.wait_ge(vp_free, 8)
                if u >= 2:
                    eng.wait_ge(p_back, u - 1)
                for j in range(i + 1):
                    for k in ks:
                        mm = eng.matmul(bank[3 + u % 2][:, j * P:(j + 1) * P], prob[k % PR][:, j * P:(j + 1) * P],
                                        diag[:, k % PR, :], start=(k == ks[0]), stop=(k == ks[-1]),
                                        skip_group_check=True)
                mm.then_inc(p_turn, 1)

            def pv(h):
                pair = h // 2
                eng.wait_ge(p_back, NT * (h + 1))
                if h % 2 == 0 and pair >= 2:
                    eng.wait_ge(o_taken, pair - 1)
                lo = (h % 2) * DH
                for j in range(NT):
                    mm = eng.matmul(bank[5 + 2 * (pair % 2)][lo:lo + DH, j * P:S],
                                    V1[:, j, h * DH:(h + 1) * DH], probT[:, h % 2, j, j * P:S],
                                    start=(j == 0), stop=(j == NT - 1), skip_group_check=True)
                mm.then_inc(o_ready, 1)

            k = 0
            LAG = 3
            for u in range(len(units) + LAG + 1):
                if u < len(units):
                    while k < len(maps) and maps[k][0] == u:
                        scores(k)
                        k += 1
                if 0 <= u - LAG < len(units):
                    turn(u - LAG)
                v = u - LAG - 1
                if v >= 0 and v % NT == NT - 1:
                    pv(v // NT)
                    if v // NT == DIL + 1 or v // NT == DIL + 3:
                        pair = v // NT // 2
                        eng.wait_ge(d_sq, pair - 2)
                        eng.matmul(bank[6][:, :], blk64, dsq, start=True, stop=True).then_inc(d_sum, 1)

        def dve_soft(eng):
            def post(u):
                h, i = units[u]
                for k, (v, which) in enumerate(maps):
                    if v != u:
                        continue
                    c = k % PR
                    eng.wait_ge(p_exp, k + 1)
                    eng.reciprocal(stat[:, 32 + c:33 + c], stat[:, 16 + c:17 + c]).then_inc(p_rec, 1)
                    eng.wait_ge(p_rec, k + 1)
                    eng.tensor_scalar(diag[:, c, :], ident, stat[:, 32 + c:33 + c], negcol if which else None,
                                      ALU.mult, *([ALU.mult] if which else [])).then_inc(p_norm, 1)

            def freed(k):
                if k >= PR:
                    v = maps[k - PR][0]
                    eng.wait_ge(p_turn, v + 1)

            k = 0

            def take(pair):
                b = bank[5 + 2 * (pair % 2)][:, :]
                if pair < DIL // 2:
                    eng.wait_ge(o_hi, pair + 1)
                    eng.tensor_tensor(hL[:, pair, :], b, hH[:, pair, :], ALU.subtract).then_inc(o_taken, 1)
                else:
                    n = pair - DIL // 2
                    eng.wait_ge(d_rs, 2 * n + 2)
                    eng.scalar_tensor_tensor(dfull[:, n, :], b, subg, rs, ALU.mult, ALU.mult).then_inc(o_taken, 1)

            for u in range(len(units) + 5):
                if u >= 5 and (u - 5) % (2 * NT) == 2 * NT - 1:
                    take((u - 5) // (2 * NT))
                if u < len(units):
                    while k < len(maps) and maps[k][0] == u:
                        h, i = units[u]
                        w = (i + 1) * P
                        eng.wait_ge(s_ready, k + 1)
                        freed(k)
                        eng.tensor_tensor_reduce(prob[k % PR][:, 0:w], bank[k % 3][:, 0:w],
                                                 tab1[:, h, S - w:S], 1.0, 3.0e38, ALU.add, ALU.min,
                                                 stat[:, k % PR:k % PR + 1]).then_inc(p_max, 1)
                        k += 1
                if 1 <= u <= len(units):
                    post(u - 1)

        def act_soft(eng):
            def back(u):
                h, i = units[u]
                eng.wait_ge(p_turn, u + 1)
                if h >= 2 and i == 0:
                    eng.wait_ge(o_ready, h - 1)
                eng.activation(probT[:, h % 2, 0:i + 1, i * P:(i + 1) * P],
                               bank[3 + u % 2][:, 0:(i + 1) * P].rearrange("p (j s) -> p j s", j=i + 1),
                               ACT.Copy).then_inc(p_back, 1)

            def take(pair):
                eng.wait_ge(o_ready, 2 * pair + 2)
                b = bank[5 + 2 * (pair % 2)][:, :]
                if pair < DIL // 2:
                    eng.activation(hH[:, pair, :], b, ACT.Copy).then_inc(o_hi, 1)
                    return
                n = pair - DIL // 2
                eng.activation(dsq, b, ACT.Square).then_inc(d_sq, 1)
                eng.wait_ge(d_sum, n + 1)
                if n:
                    eng.wait_ge(o_taken, DIL // 2 + n)
                eng.activation(lnv, bank[6][:, :], ACT.Ln, bias=EPS_RMS).then_inc(d_rs, 1)
                eng.wait_ge(d_rs, 2 * n + 1)
                eng.activation(rs, lnv, ACT.Exp, scale=-0.5).then_inc(d_rs, 1)

            k = 0
            for u in range(len(units) + 4):
                if u < len(units):
                    while k < len(maps) and maps[k][0] == u:
                        h, i = units[u]
                        w = (i + 1) * P
                        eng.wait_ge(p_max, k + 1)
                        eng.activation(prob[k % PR][:, 0:w], prob[k % PR][:, 0:w], ACT.Exp, scale=-1.0,
                                       bias=stat[:, k % PR:k % PR + 1],
                                       accum_out=stat[:, 16 + k % PR:17 + k % PR]).then_inc(p_exp, 1)
                        k += 1
                if 0 <= u - 3 < len(units):
                    back(u - 3)
                if u >= 4 and (u - 4) % (2 * NT) == 2 * NT - 1:
                    take((u - 4) // (2 * NT))

        def pool_diff(eng):
            for n in range(2):
                m = DIL // 2 + n
                eng.wait_ge(o_taken, m + 1)
                eng.tensor_copy(hH[:, m, :], dfull[:, n, :]).then_inc(d_out, 1)
                eng.wait_ge(d_out, 2 * n + 1)
                eng.tensor_tensor(hL[:, m, :], dfull[:, n, :], hH[:, m, :], ALU.subtract).then_inc(d_out, 1)

        def zcols(a, c0, c1):
            return (c0 - 384, c1 - 384) if a == 3 else (c0, c1)

        Z_ORDER = (0, 1, 3, 2)

        def zb(h, a):
            return bank[3 * (h % 2) + [0, 1, 2, 1][a]]

        def pe_stick(eng):
            def z(h):
                q, kk, lo = QC + h // 2, KC + h // 2, (h % 2) * DH
                if h >= 2:
                    eng.wait_ge(z_w, 4 * (h - 1))
                for a in (0, 1, 3, 2):
                    c0, c1 = zcols(a, a * P, S)
                    eng.matmul(zb(h, a)[:, c0:c1], projT[lo:lo + DH, kk, a * P:(a + 1) * P],
                               projT[lo:lo + DH, q, a * P:S], start=(a != 3), stop=False,
                               skip_group_check=True)
                    mm = eng.matmul(zb(h, a)[:, c0:c0 + P], matsb[:, 0, :], matsb[:, 1, :],
                                    start=False, stop=True, skip_group_check=True)
                mm.then_inc(z_ready, 1)

            def cum(h):
                for n, b in enumerate(Z_ORDER):
                    eng.wait_ge(z_parts, 8 * h + 2 * n + 2)
                    for a in range(b + 1):
                        c0, c1 = zcols(a, b * P, S)
                        for part in (spH, spL):
                            mm = eng.matmul(zb(h, a)[:, c0:c1], negR[:, 0 if a == b else 1, :],
                                            part[:, h % 2, triangle(b):triangle(b) + (NT - b) * P],
                                            start=False, stop=True, skip_group_check=True)
                mm.then_inc(z_cum, 1)

            def pv(h):
                eng.wait_ge(z_w, 4 * (h + 1))
                pair, lo = h // 2, (h % 2) * DH
                if h % 2 == 0 and pair >= 1:
                    eng.wait_ge(o_taken, 5 + pair)
                for a in range(NT):
                    mm = eng.matmul(bank[7][lo:lo + DH, a * P:S], V1[:, a, 640 + h * DH:640 + (h + 1) * DH],
                                    wts[:, h % 2, triangle(a):triangle(a) + (NT - a) * P],
                                    start=(a == 0), stop=(a == NT - 1), skip_group_check=True)
                mm.then_inc(z_pv, 1)

            eng.wait_ge(p_max, len(maps))
            z(0)
            eng.wait_ge(p_back, len(units))
            eng.wait_ge(o_taken, 5)
            z(1)
            for h in range(SB):
                cum(h)
                if h >= 1:
                    pv(h - 1)
                if h + 2 < SB:
                    z(h + 2)
            pv(SB - 1)

        def dve_stick(eng):
            def take(pair):
                eng.wait_ge(o_hi, DIL // 2 + pair + 1)
                eng.tensor_tensor(hL[:, 5 + pair, :], bank[7][:, :], hH[:, 5 + pair, :],
                                  ALU.subtract).then_inc(o_taken, 1)

            def softplus(h, a):
                c0, c1 = zcols(a, a * P, S)
                sp = softp[:, h % 2, triangle(a):triangle(a) + c1 - c0]
                eng.scalar_tensor_tensor(sp, zb(h, a)[:, c0:c1], 0.0, sp, ALU.max, ALU.add).then_inc(z_sp, 1)

            for h in range(SB):
                eng.wait_ge(z_ready, h + 1)
                eng.wait_ge(z_ln, h + 1)
                if h >= 2:
                    eng.wait_ge(z_cum, h - 1)
                softplus(h, Z_ORDER[0])
                for n, b in enumerate(Z_ORDER):
                    if n + 1 < NT:
                        softplus(h, Z_ORDER[n + 1])
                    sp, high, low = (v[:, h % 2, triangle(b):triangle(b) + (NT - b) * P] for v in (softp, spH, spL))
                    eng.wait_ge(z_sp, 4 * h + n + 1)
                    eng.tensor_copy(high, sp).then_inc(z_parts, 1)
                    eng.wait_ge(z_parts, 8 * h + 2 * n + 1)
                    eng.tensor_tensor(low, sp, high, ALU.subtract).then_inc(z_parts, 1)
                if h >= 2 and h % 2 == 0:
                    take(h // 2 - 1)
            take(2)

        def act_stick(eng):
            def first(h):
                eng.wait_ge(z_ready, h + 1)
                if h:
                    eng.wait_ge(z_ln, h)
                for a in range(NT):
                    c0, c1 = zcols(a, a * P, S)
                    t0 = triangle(a)
                    eng.activation(absz[:, t0:t0 + c1 - c0], zb(h, a)[:, c0:c1], ACT.Abs).then_inc(z_abs, 1)
                eng.wait_ge(z_abs, 4 * (h + 1))
                eng.activation(absz, absz, ACT.Exp, scale=-1.0).then_inc(z_exp, 1)
                eng.wait_ge(z_exp, h + 1)
                if h >= 2:
                    eng.wait_ge(z_parts, 8 * (h - 1))
                eng.activation(softp[:, h % 2, :], absz, ACT.Ln, bias=1.0).then_inc(z_ln, 1)

            def weights(h):
                eng.wait_ge(z_cum, h + 1)
                if h >= 2:
                    eng.wait_ge(z_pv, h - 1)
                for a in range(NT):
                    c0, c1 = zcols(a, a * P, S)
                    t0 = triangle(a)
                    eng.activation(wts[:, h % 2, t0:t0 + c1 - c0], zb(h, a)[:, c0:c1], ACT.Exp).then_inc(z_w, 1)

            def take(pair):
                eng.wait_ge(z_pv, 2 * pair + 2)
                eng.activation(hH[:, 5 + pair, :], bank[7][:, :], ACT.Copy).then_inc(o_hi, 1)

            first(0)
            for h in range(SB):
                if h + 1 < SB:
                    first(h + 1)
                weights(h)
                if h >= 2 and h % 2 == 0:
                    take(h // 2 - 1)
            take(2)

        def pe_out(eng, n0, free, made):
            def col(m):
                free(eng, m)
                landed(eng, n0 + m)
                for kc in range(KD):
                    if m == 0 and made[kc]:
                        eng.wait_ge(*made[kc])
                    mm = product(eng, bank[4 + m % 2][:, :], n0 + m, kc * P, (kc + 1) * P,
                                 hH[:, kc, :], hL[:, kc, :], kc == 0, kc == KD - 1)
                mm.then_inc(slots_done, 1)
            for m in range(KD):
                col(m)

        found = {"slot_in0": 32, "slot_in1": 32, "w_hi": 3, "w_lo": 3, "slots_done": 2, "h_hi": KD, "h_ready": KD,
                 "xsq_ready": KD, "g_free": 2, "sq_used": 2, "y_done": 2}

        def start_layer(block):
            names = list(nsem)

            def clear(eng, quarter):
                for name in names[quarter::4]:
                    eng.sem_clear(nsem[name])
                for name in names[quarter::4]:
                    if name in found:
                        eng.sem_inc(nsem[name], found[name])

            @block.sync
            def _(sp):
                clear(sp, 0)

            @block.scalar
            def _(act):
                clear(act, 1)

            @block.vector
            def _(dve):
                clear(dve, 2)

            @block.gpsimd
            def _(pool):
                clear(pool, 3)

        onehot, rb, rows8, flip = mix[0:33, 0:640], mix[0:33, 640:648], mix[0:8, 648:1288], mix[:, 1288:1288 + P]
        turned, biases = (mix[:, a:a + NSA * S].rearrange("p (h s) -> p h s", h=NSA) for a in (1536, 16384))

        spares.add(2)
        with nc.Block() as block:
            @block.sync
            def _(sp):
                sp.dma_start(onehot, t["onehot"]).then_inc(tab_in, 16)
                sp.dma_start(rb[0:32, :], t["rel_bias"]).then_inc(tab_in, 16)
                sp.dma_start(rb[32:33, :], t["one8"]).then_inc(tab_in, 16)
                sp.dma_start(flip, t["flip"]).then_inc(tab_in, 16)
                sp.dma_start(gnext, t["gfirst"]).then_inc(x_in[0], 16)
                for m in range(4):
                    sp.dma_start(xT[:, 2 * m:2 * m + 2, :], t["xT"][:, 2 * m:2 * m + 2, :]).then_inc(x_in[m], 16)
                    if m < 2:
                        load(sp, m, t["first"][m, :, :], WIDE)
                sp.wait_ge(c_done, 2)
                sp.dma_start(t["spread"], rows8).then_inc(w_in1, 16)
                for n in range(2, 4):
                    load(sp, n, t["first"][n, :, :], WIDE)
                sp.dma_start(mats[:, :, :], t["mats"]).then_inc(par_in, 16)
                sp.wait_ge(w_in1, 16)
                sp.dma_start(turned, bass.AP(tensor=t["spread"].tensor, offset=0,
                                             ap=[[1, P], [640, NSA], [1, S]])).then_inc(w_in1, 16)
                sp.wait_ge(c_done, 2 + NSA)
                sp.dma_start(t["bias"], biases).then_inc(bias_out, 16)
                slot_sem(sp, 3)

            @block.tensor
            def _(pe):
                pe.wait_ge(tab_in, 64)
                for n, c in enumerate((0, 320)):
                    pe.matmul(bank[4 + n][0:8, 0:320], rb, onehot[:, c:c + 320], start=True, stop=True).then_inc(c_out, 1)
                pair_of(pe, 0, 0)
                pe.wait_ge(w_in1, 32)
                for h in range(NSA):
                    pe.matmul(bank[6 + h % 2][:, :], flip, turned[:, h, :], start=True, stop=True).then_inc(c_out, 1)
                    if h < NSA - 1:
                        pe.wait_ge(c_done, 2 + h)

            @block.scalar
            def _(act):
                act.preload_act_table_set(EXP_LN)
                hi(act, 0)
                hi(act, 1)
                act_split(act, None, gnext, True)
                hi(act, 2)

            @block.vector
            def _(dve):
                for n, c in enumerate((0, 320)):
                    dve.wait_ge(c_out, n + 1)
                    dve.tensor_copy(rows8[:, c:c + 320], bank[4 + n][0:8, 0:320]).then_inc(c_done, 1)
                for m in range(KD):
                    rest(dve, 0, m, gnext)
                for h in range(NSA):
                    dve.wait_ge(c_out, 2 + h + 1)
                    dve.tensor_copy(biases[:, h, :], bank[6 + h % 2][:, :]).then_inc(c_done, 1)
                dve.wait_ge(par_in, 16)
                dve.tensor_copy(matsb[:, 0, :], ident)
                dve.tensor_copy(matsb[:, 1, :], mats[:, MASK, :])
                dve.tensor_copy(negR[:, 0, :], negL)
                dve.tensor_copy(negR[:, 1, :], negones)

            @block.gpsimd
            def _(pool):
                los(pool, 0, 3)

        with nc.Block() as block:
            start_layer(block)

        FFN_SLOTS = 2 * KF + 3 * KD
        A, B = 2 * KF, 3 * KD
        n_ffn0, n_in = 0, FFN_SLOTS
        n_out = n_in + N_IN
        n_ffn1 = n_out + KD
        n_next = n_ffn1 + FFN_SLOTS
        total_slots[0] = n_next + 3
        spares.update((2, n_in + 2, n_ffn1 + 2, n_next + 2))

        def of_layer(layer, name):
            return t[name][bass.ds(layer, 1), :, :].rearrange("a p n -> (a p) n")

        with nc.Fori(0, DEPTH) as layer:
            with nc.Block() as block:
                @block.sync
                def _(sp):
                    sp.dma_start(small[:, 0:48], of_layer(layer, "gains1")).then_inc(par_in, 16)
                    sp.dma_start(small[:, 98:100], of_layer(layer, "subg")).then_inc(par_in, 16)
                    sp.dma_start(lam_in[:, 0:129], of_layer(layer, "lam")).then_inc(par_in, 16)
                    sp.dma_start(gnext, of_layer(layer, "gnext")).then_inc(par_in, 16)
                    stream(sp, layer, t["w8_1"], 4, A - 4, n_ffn0 + 4, WIDE)
                    stream_down(sp, layer, t["down_1"], 0, n_ffn0 + A)
                    stream(sp, layer, t["w8_1"], A, 4, n_in, WIDE)
                    sp.wait_ge(slots_done, n_in)
                    sp.dma_start(tab1, t["table1"]).then_inc(tab_in, 16)
                    stream(sp, layer, t["w8_1"], A + 4, N_IN + KD - 4, n_in + 4, WIDE)
                    stream(sp, layer, t["w8_1"], A + N_IN + KD, A, n_ffn1, WIDE)
                    stream_down(sp, layer, t["down_1"], B, n_ffn1 + A)
                    stream(sp, layer, t["next_1"], 0, 4, n_next, WIDE)
                    slot_sem(sp, n_next + 3)

                @block.tensor
                def _(pe):
                    pe_ffn(pe, 0, n_ffn0, 0, rms_free(0), stat=0)
                    pe_stat_out(pe, 0)
                    pe_proj_T(pe, n_in, 0, 16, (0, 1, 2), h0=8, stat=1)
                    pe.wait_ge(r_steps, 1)
                    pe_proj_N(pe, n_in + 16, V_BANKS[0])
                    pe_proj_N(pe, n_in + 20, V_BANKS[1], taken=(1, 1, 2, 3))
                    pe_soft(pe)
                    pe_stick(pe)
                    pe_out(pe, n_out, rms_free(1), [(o_taken, 3), None, None, (d_out, 2), (d_out, 4)]
                           + [(o_taken, 6 + pair) for pair in range(3)])
                    pe_stat_out(pe, 1)
                    pe_ffn(pe, 1, n_ffn1, 16, rms_free(2), stat=2)
                    pe_stat_out(pe, 2)
                    pair_of(pe, n_next, 24)

                @block.scalar
                def _(act):
                    act_ffn(act, 0, 0, n_ffn0, 0)
                    act.wait_ge(par_in, 64)
                    act_split(act, 0, gcol[:, 16:24], True)
                    act_hi(act, n_in + 2, 2)
                    act_root(act, 2, EPS_RMS)
                    act.activation(rlog, bank[7][:, 0:NT], ACT.Ln, bias=EPS_RMS).then_inc(r_steps, 1)
                    act.wait_ge(r_steps, 1)
                    act.activation(rcol, rlog, ACT.Exp, scale=-0.5).then_inc(r_steps, 1)
                    act_hi(act, n_in + 4, 22)
                    act.wait_ge(seq, 4)
                    act.activation(lamtmp[:, 2:4], lamtmp[:, 0:2], ACT.Exp).then_inc(par_ready, 1)
                    act_soft(act)
                    act_stick(act)
                    for m in range(KD):
                        act_y(act, 1, n_out, 1, m)
                        hi(act, n_out + m + 2)
                    act_root(act, 3, EPS_RMS)
                    act_split(act, 8, gcol[:, 32:40], True)
                    act_ffn(act, 1, 2, n_ffn1, 4)
                    act_split(act, 16, gnext, True)
                    hi(act, n_next + 2)

                @block.vector
                def _(dve):
                    sum_x_squares(dve, 0)
                    dve.wait_ge(par_in, 64)
                    dve.tensor_scalar(ghalf, gcol, 0.5, None, ALU.mult).then_inc(seq, 1)
                    dve.tensor_tensor(lamprod, lam_in[:, 0:64].rearrange("p (a n) -> p a n", a=2),
                                      lam_in[:, 64:128].rearrange("p (a n) -> p a n", a=2), ALU.mult).then_inc(seq, 1)
                    dve.wait_ge(seq, 2)
                    dve.tensor_reduce(lamtmp[:, 0:2], lamprod, AX_X, ALU.add).then_inc(seq, 1)
                    dve.tensor_scalar(subg, subg, small[:, 99:100], None, ALU.mult).then_inc(seq, 1)
                    dve.wait_ge(seq, 4)
                    dve.wait_ge(rs_ready, 1)
                    dve.wait_ge(bias_out, 16)
                    dve_ffn(dve, 0, n_ffn0, True)
                    dve_ys(dve, 0)
                    dve_post(dve, 1, 0, ghalf[:, 8:16], 8, gcol[:, 16:24])
                    sum_x_squares(dve, 1)
                    dve.wait_ge(rs_ready, 3)
                    dve_proj_T(dve, n_in, [-DH ** -0.5] * 3 + [1.0] * 3 + [-32 ** -0.5] * 2 + [1.0] * 2
                               + [DH ** -0.5] * 3 + [1.0] * 3)
                    dve.wait_ge(r_steps, 2)
                    dve_proj_N(dve, n_in + 16, V_BANKS[0], V1[:, :, 0:512], scale=rcol)
                    dve_proj_N(dve, n_in + 20, V_BANKS[1], V1[:, :, 512:1024], scale=rcol)
                    dve.wait_ge(par_ready, 1)
                    dve.tensor_tensor(lamtmp[:, 4:5], lamtmp[:, 3:4], lamtmp[:, 2:3], ALU.subtract).then_inc(seq, 1)
                    dve.wait_ge(seq, 5)
                    dve.tensor_scalar(negcol, lamtmp[:, 4:5], lam_in[:, 128:129], None, ALU.subtract).then_inc(seq, 1)
                    dve.wait_ge(seq, 6)
                    dve.wait_ge(tab_in, 16)
                    dve_soft(dve)
                    dve_stick(dve)
                    for m in range(KD):
                        dve_y(dve, 1, m)
                    dve_post(dve, 3, 8, gcol[:, 24:32], 16, gcol[:, 32:40])
                    sum_x_squares(dve, 2)
                    dve.wait_ge(rs_ready, 5)
                    dve_ffn(dve, 1, n_ffn1, True)
                    dve_ys(dve, 2)
                    dve_post(dve, 5, 16, ghalf[:, 40:48], 24, gnext)

                @block.gpsimd
                def _(pool):
                    pool_ffn(pool, n_ffn0)
                    pool_post(pool, 0)
                    los(pool, n_in + 2, n_out + 2)
                    pool_diff(pool)
                    los(pool, n_out + 2, n_ffn1 + 2)
                    pool_post(pool, 8)
                    pool_ffn(pool, n_ffn1)
                    pool_post(pool, 16)
                    lo(pool, n_next + 2)

            with nc.Block() as block:
                start_layer(block)

        HQ, HGT, NQ, KCM, VCM, KSL, KWI = 0, 4, 8, 12, 13, 14, 15
        yflat = yT[:, :, :].rearrange("p c s -> p (c s)")
        sc = Layout(mix, MW)
        sc.take(16 * S)
        forget_at = sc.at
        LF = sc.take(2048).rearrange("p (b n) -> p b n", b=NT)
        HV = sc.take(2048).rearrange("p (b n) -> p b n", b=NT)
        tab2 = mix[:, forget_at:forget_at + NSA * S].rearrange("p (h s) -> p h s", h=NSA)
        span = sc.take(1024)
        lmask = sc.take(1024)
        par = sc.take(64 + 128 + 1)
        posk, posv, w2k, w2v = par[:, 0:32], par[:, 32:64], par[:, 64:128], par[:, 128:192]
        gwcol = par[:, 192:193]
        g1, b1, g2, b2 = (small[:, 8 * n:8 * n + 8] for n in range(4))
        flags = sc.take(4)
        vg = sc.take(NT * VG).rearrange("p (b n) -> p b n", b=NT)
        gate = sc.take(NT * 24).rearrange("p (b n) -> p b n", b=NT)
        chid = sc.take(128).rearrange("p (k n) -> p k n", k=2)
        kcmp = sc.take(32)
        vcmp = sc.take(128)
        valid = sc.take(1)
        both_at = sc.at
        winK = sc.take(32 * NCMP).rearrange("p (i n) -> p i n", i=16)
        winV = sc.take(32 * NCMP).rearrange("p (i n) -> p i n", i=16)
        w1k = yflat[:, 0:2048].rearrange("p (i n) -> p i n", i=16)
        w1v = yflat[:, 2048:4096].rearrange("p (i n) -> p i n", i=16)

        sc.at = both_at
        kN = sc.take(2048).rearrange("p (b n) -> p b n", b=NT)
        kT = sc.take(2048).rearrange("p (h s) -> p h s", h=HG)
        t_at = sc.at
        QR = sc.take(2 * LEVELS * P).rearrange("p (r l s) -> p r l s", r=2, l=LEVELS)
        KL = sc.take(1792).rearrange("p (r l s) -> p r l s", r=2, l=LEVELS)
        AM = sc.take(1024)
        scs = sc.take(256).rearrange("p (r s) -> p r s", r=2)
        ST = sc.take(512).rearrange("p (r s) -> p r s", r=4)
        T1 = mix[:, t_at:t_at + 2048].rearrange("p (b n) -> p b n", b=NT)
        T2 = mix[:, t_at + 2048:t_at + 4096].rearrange("p (b n) -> p b n", b=NT)
        logA, logB = kT[:, 0, :], kT[:, 1, :]
        lbp0, lbp1 = T2[:, 2, :], T2[:, 3, :]
        E = yflat[:, 0:2048].rearrange("p (r n) -> p r n", r=2)
        QI = yflat[:, 3584:4096].rearrange("p (r s) -> p r s", r=4)
        KDE = yflat[:, 2048:3584].rearrange("p (b n) -> p b n", b=3)

        def wide(v):
            return v.unsqueeze(1).broadcast_to([P, NT, 512])

        def step(ins, count):
            ins.then_inc(count, 1)

        def dve_forget(eng):
            eng.wait_ge(par_in, 96)
            step(eng.tensor_tensor(T1[:, 0, :], lbp1, lbp0, ALU.subtract), f_dve)
            eng.wait_ge(f_act, 3)
            step(eng.scalar_tensor_tensor(T1[:, 1, :], T1[:, 0, :], 0.0, T1[:, 1, :], ALU.max, ALU.add), f_dve)
            eng.wait_ge(f_dve, 2)
            step(eng.tensor_scalar(logB, T1[:, 1, :], flags[:, 1:2], None, ALU.mult), f_dve)
            step(eng.tensor_tensor(T1[:, 2, :], T1[:, 0, :], T1[:, 1, :], ALU.subtract), f_dve)
            eng.wait_ge(f_dve, 4)
            step(eng.tensor_scalar(logA, T1[:, 2, :], flags[:, 0:1], flags[:, 2:3], ALU.mult, ALU.add), f_dve)
            eng.wait_ge(f_dve, 5)
            eng.wait_ge(f_act, 6)
            step(eng.scalar_tensor_tensor(T2, LF, 0.0, T1, ALU.min, ALU.subtract), f_dve)
            eng.wait_ge(f_dve, 6)
            step(eng.tensor_tensor(T2, T2, wide(logB), ALU.add), f_dve)
            eng.wait_ge(f_dve, 7)
            step(eng.tensor_tensor(kN, T2, LF, ALU.subtract), f_dve)
            step(eng.tensor_tensor(T1, wide(logA), T2, ALU.subtract), f_dve)
            eng.wait_ge(f_dve, 9)
            step(eng.tensor_tensor(LF, wide(logA), T2, ALU.max), f_dve)
            eng.wait_ge(f_act, 10)
            eng.wait_ge(f_dve, 10)
            step(eng.tensor_tensor(LF, LF, T1, ALU.add), f_dve)

        def act_forget(eng, n):
            if n in (1, 2, 4, 5, 9):
                eng.wait_ge(f_act, n)
            if n == 0:
                eng.wait_ge(f_dve, 1)
                step(eng.activation(T1[:, 1, :], T1[:, 0, :], ACT.Abs), f_act)
            elif n == 1:
                step(eng.activation(T1[:, 1, :], T1[:, 1, :], ACT.Exp, scale=-1.0), f_act)
            elif n == 2:
                step(eng.activation(T1[:, 1, :], T1[:, 1, :], ACT.Ln, bias=1.0), f_act)
            elif n == 3:
                eng.wait_ge(f_dve, 5)
                eng.wait_ge(vp_free, 4)
                step(eng.activation(T1, LF, ACT.Abs), f_act)
            elif n == 4:
                step(eng.activation(T1, T1, ACT.Exp, scale=-1.0), f_act)
            elif n == 5:
                step(eng.activation(T1, T1, ACT.Ln, bias=1.0), f_act)
            elif n == 6:
                eng.wait_ge(f_dve, 9)
                step(eng.activation(T1, T1, ACT.Abs), f_act)
            elif n == 7:
                step(eng.activation(kN, kN, ACT.Exp), f_act)
            elif n == 8:
                eng.wait_ge(f_act, 7)
                step(eng.activation(T1, T1, ACT.Exp, scale=-1.0), f_act)
            elif n == 9:
                step(eng.activation(T1, T1, ACT.Ln, bias=1.0), f_act)

        def dve_windows(eng):
            eng.wait_ge(tp_free, 2)
            for dst, j, pos_ in ((winK, KCM, posk), (winV, VCM, posv)):
                for g in range(2):
                    lo = g * DH
                    src = projT[lo:lo + DH, j, :].rearrange("p (n i) -> p i n", i=16)
                    for odd in range(2):
                        out = dst[odd * DH:(odd + 1) * DH, :, g * NCMP:(g + 1) * NCMP]
                        for half in range(2):
                            at_pos = pos_[lo:lo + DH, 16 * half + odd:16 * half + odd + 15:2]
                            eng.tensor_tensor(out[:, 8 * half:8 * half + 8, :],
                                              src[:, odd:odd + 15:2, half:half + NCMP],
                                              at_pos.unsqueeze(2).broadcast_to([DH, 8, NCMP]),
                                              ALU.add).then_inc(win, 1)

        def pe_compress(eng):
            eng.wait_ge(w_in1, 32)
            eng.wait_ge(win, 16)
            eng.wait_ge(tp_free, 4)
            for kind, (w1, src) in enumerate(((w1k, winK), (w1v, winV))):
                for i in range(16):
                    mm = eng.matmul(bank[0][:, kind * 64:kind * 64 + 2 * NCMP], w1[:, i, :], src[:, i, :],
                                    start=(i == 0), stop=(i == 15), skip_group_check=True)
            mm.then_inc(c_hid, 1)
            eng.wait_ge(c_act, 1)
            for g in range(2):
                eng.matmul(bank[6][g * DH:(g + 1) * DH, 0:NCMP], w2k, chid[:, 0, g * NCMP:(g + 1) * NCMP],
                           start=True, stop=True, skip_group_check=True)
            for g in range(2):
                mm = eng.matmul(bank[7][0:NCMP, g * DH:(g + 1) * DH], chid[:, 1, g * NCMP:(g + 1) * NCMP], w2v,
                                start=True, stop=True, skip_group_check=True)
            mm.then_inc(c_out, 1)

        def act_compress(eng):
            eng.wait_ge(c_hid, 1)
            eng.activation(chid[:, :, 0:2 * NCMP],
                           bank[0][:, 0:128].rearrange("p (k n) -> p k n", k=2)[:, :, 0:2 * NCMP],
                           ACT.Gelu_apprx_tanh).then_inc(c_act, 1)

        def dve_compress(eng):
            eng.wait_ge(c_out, 1)
            eng.tensor_copy(kcmp[:, 0:NCMP], bank[6][:, 0:NCMP]).then_inc(c_done, 1)
            eng.tensor_copy(vcmp[0:NCMP, :], bank[7][0:NCMP, 0:128]).then_inc(c_done, 1)

        def pe_hgrn_keys(eng):
            eng.wait_ge(f_act, 8)
            for h in range(HG):
                for b in range(NT):
                    mm = eng.transpose(bank[2 + h][:, b * P:(b + 1) * P], kN[:, b, h * P:(h + 1) * P], ident)
                mm.then_inc(k_turn, 1)
            eng.wait_ge(f_dve, 11)
            for b in range(3):
                eng.matmul(bank[[6, 7, 0][b]][:, :], mats[:, AFTER, :], LF[:, b, :],
                           start=True, stop=True).then_inc(suf_ready, 1)

        def act_hgrn_keys(eng):
            for h in range(HG):
                eng.wait_ge(k_turn, h + 1)
                if h == 0:
                    eng.wait_ge(f_dve, 10)
                eng.activation(kT[:, h, :], bank[2 + h][:, :], ACT.Copy).then_inc(k_back, 1)
            for b in range(3):
                eng.wait_ge(suf_ready, b + 1)
                eng.activation(KDE[:, b, :], bank[[6, 7, 0][b]][:, :], ACT.Exp).then_inc(suf_exp, 1)

        def dve_hgrn_keys(eng):
            for b in range(3):
                eng.wait_ge(suf_exp, b + 1)
                eng.tensor_tensor(KDE[:, b, :], KDE[:, b, :], kN[:, b, :], ALU.mult).then_inc(kd_ready, 1)

        HU = HG * NT

        def pe_hgrn(eng):
            eng.wait_ge(suf_exp, 3)
            eng.wait_ge(kd_ready, 3)
            eng.wait_ge(vp_free, 8)

            def decays(u):
                h, b = divmod(u, NT)
                if u:
                    eng.wait_ge(dec_exp, 2 * u)
                for half in range(2):
                    mm = eng.matmul(bank[half][:, :], LF[:, b, h * P:(h + 1) * P],
                                    span[:, half * 512:half * 512 + 512], start=True, stop=True)
                mm.then_inc(dec_ready, 1)

            def scores(u):
                h, b = divmod(u, NT)
                eng.wait_ge(q_dec, 2 * u + 2)
                eng.wait_ge(k_dec, u + 1)
                if u:
                    eng.wait_ge(a_mask, 2 * u)
                for l in range(LEVELS):
                    eng.matmul(bank[2 + l // 4][:, (l % 4) * P:(l % 4 + 1) * P], KL[:, u % 2, l, :],
                               QR[:, u % 2, l, :], start=True, stop=True, skip_group_check=True)
                eng.matmul(bank[3][:, 3 * P:4 * P], kT[:, h, b * P:(b + 1) * P],
                           projT[:, HQ + h, b * P:(b + 1) * P], start=True, stop=True,
                           skip_group_check=True).then_inc(a_ready, 1)

            def update(u):
                h, b = divmod(u, NT)
                if b == NT - 1:
                    return
                n = 3 * h + b
                if n:
                    eng.wait_ge(st_ready, n)
                eng.matmul(bank[7][:, 0:P], KDE[:, b, h * P:(h + 1) * P], HV[:, b, h * P:(h + 1) * P],
                           start=True, stop=True).then_inc(u_ready, 1)

            def output(u):
                h, b = divmod(u, NT)
                eng.wait_ge(a_sum, u + 1)
                if b == 0 and h >= 2:
                    eng.wait_ge(hout, h - 1)
                o = bank[4 + h % 2][:, b * P:(b + 1) * P]
                mm = eng.matmul(o, HV[:, b, h * P:(h + 1) * P], scs[:, u % 2, :], start=True,
                                stop=(b == 0), skip_group_check=True)
                if b:
                    n = 3 * h + b - 1
                    eng.wait_ge(st_ready, n + 1)
                    mm = eng.matmul(o, ST[:, n % 4, :], QI[:, u % 4, :], start=False, stop=True,
                                    skip_group_check=True)
                mm.then_inc(ho_ready, 1)

            decays(0)
            for u in range(HU + 2):
                if u < HU:
                    if u + 1 < HU:
                        decays(u + 1)
                    scores(u)
                    update(u)
                if 1 <= u <= HU:
                    output(u - 1)
                if u >= 2 and (u - 2) % NT == NT - 1:
                    h = (u - 2) // NT
                    eng.wait_ge(hsq, h + 1)
                    eng.matmul(bank[6][:, :], onesD, sq[:, h % 2, :], start=True, stop=True).then_inc(hsum, 1)

        def act_hgrn(eng):
            for u in range(HU + 4):
                if u < HU:
                    eng.wait_ge(dec_ready, u + 1)
                    if u >= 2:
                        eng.wait_ge(q_dec, 2 * u - 2)
                        eng.wait_ge(k_dec, u - 1)
                        eng.wait_ge(st_ready, (u - 1) // NT * 3 + min((u - 1) % NT, 3))
                    for half in range(2):
                        eng.activation(E[:, u % 2, half * 512:half * 512 + 512], bank[half][:, :],
                                       ACT.Exp).then_inc(dec_exp, 1)
                if u >= 2 and (u - 2) % NT == NT - 1 and u - 2 < HU:
                    h = (u - 2) // NT
                    eng.wait_ge(ho_ready, 4 * (h + 1))
                    eng.activation(sq[:, h % 2, :], bank[4 + h % 2][:, :], ACT.Square).then_inc(hsq, 1)
                if u >= 4 and (u - 4) % NT == NT - 1:
                    h = (u - 4) // NT
                    eng.wait_ge(hsum, h + 1)
                    eng.activation(lnv, bank[6][:, :], ACT.Ln, bias=EPS_RMS, scale=D / P).then_inc(hrs, 1)
                    eng.wait_ge(hrs, 2 * h + 1)
                    if h:
                        eng.wait_ge(hout, h)
                    eng.activation(rs, lnv, ACT.Exp, scale=-0.5).then_inc(hrs, 1)

        def dve_hgrn(eng):
            eng.wait_ge(k_back, 4)

            def queries(u):
                h, b = divmod(u, NT)
                q = projT[:, HQ + h, b * P:(b + 1) * P]
                eng.wait_ge(dec_exp, 2 * u + 2)
                if u >= 2:
                    eng.wait_ge(a_ready, u - 1)
                if u >= 4:
                    eng.wait_ge(ho_ready, u - 3)
                eng.tensor_tensor(QR[:, u % 2, :, :], E[:, u % 2, 0:LEVELS * P].rearrange("p (l s) -> p l s", l=LEVELS),
                                  q.unsqueeze(1).broadcast_to([P, LEVELS, P]), ALU.mult).then_inc(q_dec, 1)
                eng.tensor_tensor(QI[:, u % 4, :], E[:, u % 2, LEVELS * P:8 * P], q, ALU.mult).then_inc(q_dec, 1)

            queries(0)
            for u in range(HU + 3):
                if u < HU:
                    h, b = divmod(u, NT)
                    if u + 1 < HU:
                        queries(u + 1)
                    eng.wait_ge(a_ready, u + 1)
                    if u:
                        eng.wait_ge(a_sum, u)
                    for half in range(2):
                        eng.tensor_tensor(AM[:, half * 512:half * 512 + 512], bank[2 + half][:, :],
                                          lmask[:, half * 512:half * 512 + 512], ALU.mult).then_inc(a_mask, 1)
                    if b < NT - 1:
                        n = 3 * h + b
                        eng.wait_ge(u_ready, n + 1)
                        if n >= 4:
                            eng.wait_ge(ho_ready, (n - 4) // 3 * NT + (n - 4) % 3 + 2)
                        if b == 0:
                            eng.tensor_copy(ST[:, n % 4, :], bank[7][:, 0:P]).then_inc(st_ready, 1)
                        else:
                            eng.wait_ge(st_ready, n)
                            eng.scalar_tensor_tensor(ST[:, n % 4, :], ST[:, (n - 1) % 4, :],
                                                     E[:, u % 2, 1023:1024], bank[7][:, 0:P],
                                                     ALU.mult, ALU.add).then_inc(st_ready, 1)
                    eng.wait_ge(a_mask, 2 * u + 2)
                    if u >= 2:
                        eng.wait_ge(ho_ready, u - 1)
                    eng.tensor_reduce(scs[:, u % 2, :], AM.rearrange("p (l s) -> p s l", l=8), AX_X,
                                      ALU.add).then_inc(a_sum, 1)
                if u >= 3 and (u - 3) % NT == NT - 1:
                    h = (u - 3) // NT
                    eng.wait_ge(hrs, 2 * h + 2)
                    if h >= 2:
                        eng.wait_ge(hmix, 3 * (h - 2) + 1)
                    eng.scalar_tensor_tensor(tmp[:, h % 2, :], bank[4 + h % 2][:, :], gwcol, rs,
                                             ALU.mult, ALU.mult).then_inc(hout, 1)

        def pool_hgrn(eng):
            def keys(u):
                h, b = divmod(u, NT)
                eng.wait_ge(dec_exp, 2 * u + 2)
                if u >= 2:
                    eng.wait_ge(a_ready, u - 1)
                eng.tensor_tensor(KL[:, u % 2, :, :], E[:, u % 2, 0:LEVELS * P].rearrange("p (l s) -> p l s", l=LEVELS),
                                  kT[:, h, b * P:(b + 1) * P].unsqueeze(1).broadcast_to([P, LEVELS, P]),
                                  ALU.mult).then_inc(k_dec, 1)

            def gated(h, part):
                full = projT[:, HGT + h, :]
                if part == 0:
                    eng.wait_ge(hout, h + 1)
                    eng.wait_ge(silu_g, 4)
                    eng.tensor_tensor(full, tmp[:, h % 2, :], full, ALU.mult).then_inc(hmix, 1)
                elif part == 1:
                    eng.wait_ge(hmix, 3 * h + 1)
                    eng.tensor_copy(hH[:, h, :], full).then_inc(hmix, 1)
                else:
                    eng.wait_ge(hmix, 3 * h + 2)
                    eng.tensor_tensor(hL[:, h, :], full, hH[:, h, :], ALU.subtract).then_inc(hmix, 1)

            eng.wait_ge(k_back, 4)
            for u in range(HU):
                keys(u)
                if u >= 7 and (u - 7) % NT < 3:
                    gated((u - 7) // NT, (u - 7) % NT)
            for u in range(HU, HU + 7):
                if (u - 7) % NT < 3:
                    gated((u - 7) // NT, (u - 7) % NT)

        sc.at = both_at
        p3 = [sc.take(3 * S).rearrange("p (w s) -> p w s", w=3) for _ in range(2)]
        p3.append(mix[:, 0:3 * S].rearrange("p (w s) -> p w s", w=3))
        diag = mix[:, 3 * S:3 * S + 6 * P].rearrange("p (r w s) -> p r w s", r=2, w=3)
        probS = sc.take(4096)
        probC = sc.take(1024).rearrange("p (r s) -> p r s", r=2)
        st3 = sc.take(64)
        pT = [probS.rearrange("p (w j s) -> p w j s", w=2, j=NT), yflat.rearrange("p (w j s) -> p w j s", w=2, j=NT)]
        NU = NSA * NT

        def cw(i):
            return 8 * i + 7

        def pe_nsa(eng):
            eng.wait_ge(hout, 4)
            eng.wait_ge(c_done, 2)

            def scores(u):
                h, i = divmod(u, NT)
                g, hp = divmod(h, 4)
                lo = g * DH
                q = projT[lo:lo + DH, NQ + hp, i * P:(i + 1) * P]
                for w, (keys, n) in enumerate(((kcmp[lo:lo + DH, 0:cw(i)], cw(i)),
                                               (projT[lo:lo + DH, KSL, 0:(i + 1) * P], (i + 1) * P),
                                               (projT[lo:lo + DH, KWI, 0:(i + 1) * P], (i + 1) * P))):
                    if u:
                        eng.wait_ge(p_max, 3 * u + w - 2)
                    eng.matmul(bank[w][:, 0:n], q, keys, start=True, stop=True).then_inc(s_ready, 1)

            def turn(u):
                h, i = divmod(u, NT)
                for w in range(3):
                    eng.wait_ge(p_norm, 3 * u + w + 1)
                    if u:
                        eng.wait_ge(p_back, 3 * u + w - 2)
                    if w == 0:
                        mm = eng.matmul(bank[6][0:cw(i), 0:P], p3[u % 3][:, 0, 0:cw(i)], diag[:, u % 2, 0, :],
                                        start=True, stop=True)
                    else:
                        for j in range(i + 1):
                            mm = eng.matmul(bank[2 + w][:, j * P:(j + 1) * P],
                                            p3[u % 3][:, w, j * P:(j + 1) * P], diag[:, u % 2, w, :],
                                            start=True, stop=True, skip_group_check=True)
                    mm.then_inc(p_turn, 1)

            def pv(h):
                g, pair, lo = h // 4, h // 2, (h % 2) * DH
                eng.wait_ge(p_back, 12 * (h + 1))
                if h % 2 == 0 and pair >= 2:
                    eng.wait_ge(o_taken, pair - 1)
                o = bank[5 + 2 * (pair % 2)]
                for w in range(2):
                    for j in range(NT):
                        eng.matmul(o[lo:lo + DH, j * P:S], vg[:, j, w * P + g * DH:w * P + (g + 1) * DH],
                                   pT[h % 2][:, w, j, j * P:S], start=(w == 0 and j == 0), stop=False,
                                   skip_group_check=True)
                for i in range(NT):
                    mm = eng.matmul(o[lo:lo + DH, i * P:(i + 1) * P], vcmp[0:cw(i), g * DH:(g + 1) * DH],
                                    probC[0:cw(i), h % 2, i * P:(i + 1) * P], start=False, stop=(i == NT - 1),
                                    skip_group_check=True)
                mm.then_inc(o_ready, 1)

            scores(0)
            scores(1)
            for u in range(NU + 1):
                if u + 2 < NU:
                    scores(u + 2)
                if u < NU:
                    turn(u)
                if u >= 1 and (u - 1) % NT == NT - 1:
                    pv((u - 1) // NT)

        def dve_gates(eng):
            eng.wait_ge(gate_ready, 1)
            g2d = gate.rearrange("p b n -> p (b n)")
            eng.tensor_scalar(g2d, g2d, 1.0, None, ALU.add).then_inc(p_rec, 1)
            eng.wait_ge(p_rec, 1)
            eng.reciprocal(g2d, g2d).then_inc(p_rec, 1)
            eng.wait_ge(p_rec, 2)
            eng.tensor_scalar(gate[:, 0, 0:8], gate[:, 0, 0:8], valid, None, ALU.mult).then_inc(p_rec, 1)
            eng.wait_ge(p_rec, 3)

        def dve_nsa(eng):
            rec = [3]
            eng.wait_ge(tab_in, 16)
            for u in range(NU + 3):
                if u >= 3 and (u - 3) % (2 * NT) == 2 * NT - 1:
                    pair = (u - 3) // (2 * NT)
                    eng.wait_ge(o_hi, pair + 1)
                    eng.tensor_tensor(hL[:, HG + pair, :], bank[5 + 2 * (pair % 2)][:, :], hH[:, HG + pair, :],
                                      ALU.subtract).then_inc(o_taken, 1)
                if u < NU:
                    h, i = divmod(u, NT)
                    n = (i + 1) * P
                    c0 = S - P - i * P + CMP_END
                    for w in range(3):
                        m = cw(i) if w == 0 else n
                        bias = tab2[:, h, c0:c0 + 16 * (m - 1) + 1:16] if w == 0 else tab2[:, h, S - n:S]
                        eng.wait_ge(s_ready, 3 * u + w + 1)
                        if u >= 3:
                            eng.wait_ge(p_turn, 3 * (u - 3) + w + 1)
                        a = (u % 3) * 3 + w
                        eng.tensor_tensor_reduce(p3[u % 3][:, w, 0:m], bank[w][:, 0:m], bias, 1.0, 3.0e38,
                                                 ALU.add, ALU.min, st3[:, a:a + 1]).then_inc(p_max, 1)
                if 1 <= u <= NU:
                    v = u - 1
                    h, i = divmod(v, NT)
                    a = (v % 3) * 3
                    eng.wait_ge(p_exp, 3 * v + 3)
                    eng.reciprocal(st3[:, 32 + a:35 + a], st3[:, 16 + a:19 + a]).then_inc(p_rec, 1)
                    eng.wait_ge(p_rec, rec[0] + 1)
                    eng.tensor_tensor(st3[:, 48 + a:51 + a], st3[:, 32 + a:35 + a],
                                      gate[:, i, h:h + 17:8], ALU.mult).then_inc(p_rec, 1)
                    eng.wait_ge(p_rec, rec[0] + 2)
                    rec[0] += 2
                    if v >= 2:
                        eng.wait_ge(p_turn, 3 * (v - 1))
                    for w in range(3):
                        eng.tensor_scalar(diag[:, v % 2, w, :], ident, st3[:, 48 + a + w:49 + a + w], None,
                                          ALU.mult).then_inc(p_norm, 1)

        def act_nsa(eng):
            def back(u):
                h, i = divmod(u, NT)
                if i == 0 and h >= 2:
                    eng.wait_ge(o_ready, h - 1)
                for w in range(3):
                    eng.wait_ge(p_turn, 3 * u + w + 1)
                    if w == 0:
                        eng.activation(probC[0:cw(i), h % 2, i * P:(i + 1) * P], bank[6][0:cw(i), 0:P],
                                       ACT.Copy).then_inc(p_back, 1)
                    else:
                        eng.activation(pT[h % 2][:, w - 1, 0:i + 1, i * P:(i + 1) * P],
                                       bank[2 + w][:, 0:(i + 1) * P].rearrange("p (j s) -> p j s", j=i + 1),
                                       ACT.Copy).then_inc(p_back, 1)

            for u in range(NU + 2):
                if u < NU:
                    i = u % NT
                    for w in range(3):
                        m = cw(i) if w == 0 else (i + 1) * P
                        a = (u % 3) * 3 + w
                        eng.wait_ge(p_max, 3 * u + w + 1)
                        eng.activation(p3[u % 3][:, w, 0:m], p3[u % 3][:, w, 0:m], ACT.Exp, scale=-1.0,
                                       bias=st3[:, a:a + 1], accum_out=st3[:, 16 + a:17 + a]).then_inc(p_exp, 1)
                if 1 <= u <= NU:
                    back(u - 1)
                if u >= 2 and (u - 2) % (2 * NT) == 2 * NT - 1:
                    pair = (u - 2) // (2 * NT)
                    eng.wait_ge(o_ready, 2 * pair + 2)
                    eng.activation(hH[:, HG + pair, :], bank[5 + 2 * (pair % 2)][:, :], ACT.Copy).then_inc(o_hi, 1)

        def dve_sum(eng, q, n1, per_tile, m, i=0, per=0):
            eng.wait_ge(slots_done, i * (per * per_tile) + (n1 + per_tile * (m + 1)))
            if per == 0:
                x, y = xT[:, m, :], yT[:, m, :]
            else:
                x, y = (v[:, bass.ds(i * per + m, 1), :].rearrange("p a s -> p (a s)") for v in (xT, yT))
            eng.scalar_tensor_tensor(y, x, ALPHA, bank[4 + m % 2][:, :], ALU.mult, ALU.add).then_inc(y_done, 1)

        def add_output(eng, q, m, i=0, per=0):
            eng.wait_ge(y_done, i * per + (8 * q + m + 3))
            if m == 0:
                eng.tensor_copy(acc, yT[:, 0, :]).then_inc(acc_steps, 1)
                return
            y = yT[:, m, :] if per == 0 else yT[:, bass.ds(i * per + m, 1), :].rearrange("p a s -> p (a s)")
            eng.wait_ge(acc_steps, i * per + (8 * q + m))
            eng.tensor_tensor(acc, acc, y, ALU.add).then_inc(acc_steps, 1)

        def pe_layer_norm(eng, q):
            eng.wait_ge(acc_steps, 8 * q + 8)
            eng.matmul(bank[6][:, :], onesD, acc, start=True, stop=True).then_inc(stat_ready, 1)
            for m in range(KD):
                eng.wait_ge(sq_ready, 8 * q + m + 1)
                eng.matmul(bank[7][:, :], onesD, sq[:, m % 2, :], start=(m == 0), stop=(m == KD - 1),
                           skip_group_check=True).then_inc(sq_used, 1)

        def dve_ln(eng, q, g, b, h0):
            eng.wait_ge(stat_ready, q + 1)
            for m in range(KD):
                eng.tensor_tensor(yT[:, m, :], yT[:, m, :], bank[6][:, :], ALU.subtract).then_inc(c_ready, 1)
            dve_post(eng, q, 8 * q, g, h0, b=b)

        def pool_ln(eng, q, b):
            for m in range(1, KD):
                eng.wait_ge(t_ready, 8 * q + m + 1)
                eng.tensor_scalar(xT[:, m, :], tmp[:, m % 2, :], b[:, m:m + 1], None, ALU.add).then_inc(x_ready, 1)

        def act_ln(eng, q):
            for m in range(KD):
                eng.wait_ge(c_ready, 8 * q + m + 1)
                eng.wait_ge(sq_used, 8 * q + m + 1)
                eng.activation(sq[:, m % 2, :], yT[:, m, :], ACT.Square).then_inc(sq_ready, 1)
            act_root(eng, q, EPS_LN, 7)

        n_in2, n_vg = 0, 24
        n_out2 = n_vg + len(VG_ROWS)
        n_ffn2 = n_out2 + KD
        n_next2 = n_ffn2 + FFN_SLOTS
        total_slots[0] = n_next2 + 3
        spares.clear()
        spares.update((2, n_ffn2 + 2, n_next2 + 2))
        widths += [WIDE] * n_vg + [c * VG for c in VG_ROWS]

        with nc.Fori(0, DEPTH) as layer:
            with nc.Block() as block:
                @block.sync
                def _(sp):
                    sp.dma_start(par, of_layer(layer, "par2")).then_inc(par_in, 16)
                    sp.dma_start(small[:, 0:32], of_layer(layer, "ln2")).then_inc(par_in, 16)
                    sp.dma_start(flags, of_layer(layer, "flags")).then_inc(par_in, 16)
                    sp.dma_start(T2[:, 2:4, :], of_layer(layer, "lbp")).then_inc(par_in, 16)
                    sp.dma_start(mix[:, forget_at + 4096:forget_at + 6144], t["table2"]).then_inc(par_in, 16)
                    sp.dma_start(valid, t["valid"]).then_inc(par_in, 16)
                    sp.dma_start(w1k, of_layer(layer, "w1k")).then_inc(w_in1, 16)
                    stream(sp, layer, t["w8_2"], 4, 1, n_in2 + 4, WIDE)
                    sp.dma_start(w1v, of_layer(layer, "w1v")).then_inc(w_in1, 16)
                    stream(sp, layer, t["w8_2"], 5, 19, n_in2 + 5, WIDE)
                    for k, c in enumerate(VG_ROWS):
                        load(sp, n_vg + k, t["vg_2"][bass.ds(layer, 1), k, :, 0:c * VG].rearrange("a p n -> (a p) n"), c * VG)
                    stream(sp, layer, t["w8_2"], 24, 2, n_out2, WIDE)
                    sp.wait_ge(ho_ready, HU)
                    sp.wait_ge(bias_out, 16)
                    sp.dma_start(tab2, t["bias"]).then_inc(tab_in, 16)
                    stream(sp, layer, t["w8_2"], 26, KD - 2 + A, n_out2 + 2, WIDE)
                    stream_down(sp, layer, t["down_2"], 0, n_ffn2 + A)
                    stream(sp, layer, t["next_2"], 0, 4, n_next2, WIDE)
                    slot_sem(sp, n_next2 + 3)

                @block.tensor
                def _(pe):
                    pe_proj_T(pe, n_in2 + 2, 2, 4, T_BANKS)
                    pe_proj_N(pe, n_in2 + 4, (1, 3, 4, 5))
                    pe_compress(pe)
                    pe_proj_T(pe, n_in2 + 8, 4, 16, T_BANKS)
                    pe.wait_ge(vp_free, 4)
                    pe_proj_N(pe, n_in2 + 20, (1, 3, 4, 5))
                    pe.wait_ge(tp_free, 16)
                    pe.wait_ge(c_done, 2)
                    pe_proj_N(pe, n_vg, (6, 7, 0, 2), VG, VG_ROWS)
                    pe.wait_ge(vp_free, 12)
                    pe.wait_ge(c_done, 2)
                    pe.wait_ge(par_in, 96)
                    pe_hgrn_keys(pe)
                    pe_hgrn(pe)
                    pe_nsa(pe)
                    pe_out(pe, n_out2, ln_free(0), [(hmix, 12), None, None, None]
                           + [(o_taken, 1 + pair) for pair in range(4)])
                    pe_layer_norm(pe, 0)
                    pe_ffn(pe, 0, n_ffn2, 8, ln_free(1))
                    pe_layer_norm(pe, 1)
                    pair_of(pe, n_next2, 16)

                @block.scalar
                def _(act):
                    act.preload_act_table_set(EXP_LN)
                    def place(j):
                        return KCM + j if j < 4 else j - 4
                    def scale(p):
                        return -DH ** -0.5 if NQ <= p < NQ + 4 else 1.0
                    act_proj_T(act, n_in2, 0, 4, place, scale, False)
                    act_hi(act, n_in2 + 6, 4)
                    act_compress(act)
                    act.preload_act_table_set(EXP_LN)
                    act_proj_T(act, n_in2 + 8, 4, 16, place, scale, True)
                    for h in range(HG):
                        act.activation(projT[:, HGT + h, :], projT[:, HGT + h, :], ACT.Silu).then_inc(silu_g, 1)
                    act.preload_act_table_set(EXP_LN)
                    act_hi(act, n_in2 + 22, 4 + len(VG_ROWS))
                    act.wait_ge(vp_free, 12)
                    act.activation(gate, vg[:, :, 256:280], ACT.Exp, scale=-1.0).then_inc(gate_ready, 1)
                    act_hgrn_keys(act)
                    act_hgrn(act)
                    act_nsa(act)
                    for m in range(KD):
                        hi(act, n_out2 + m + 2)
                    act_ln(act, 0)
                    act_split(act, 0, None, False)
                    act_silu(act, 0, n_ffn2)
                    act_down(act, n_ffn2 + A, lambda m, i, per: None)
                    act_ln(act, 1)
                    act_split(act, 8, None, False)
                    hi(act, n_next2 + 2)

                @block.vector
                def _(dve):
                    dve.wait_ge(par_in, 96)
                    dve_windows(dve)
                    dve_proj_N(dve, n_in2 + 4, (1, 3, 4, 5), LF)
                    dve_compress(dve)
                    dve_forget(dve)
                    dve_proj_N(dve, n_in2 + 20, (1, 3, 4, 5), HV)
                    dve_proj_N(dve, n_vg, (6, 7, 0, 2), vg, VG, len(VG_ROWS))
                    dve_gates(dve)
                    dve_hgrn_keys(dve)
                    dve_hgrn(dve)
                    dve_nsa(dve)
                    for m in range(KD):
                        dve_sum(dve, 0, n_out2, 1, m)
                        add_output(dve, 0, m)
                    dve_ln(dve, 0, g1, b1, 8)
                    dve_ffn(dve, 0, n_ffn2, False)
                    dve_sum(dve, 1, n_ffn2 + A, 3, 0)
                    add_output(dve, 1, 0)
                    with dve.Fori(0, 3) as i:
                        for m in (1, 2):
                            dve_sum(dve, 1, n_ffn2 + A, 3, m, i, 2)
                            add_output(dve, 1, m, i, 2)
                    dve_sum(dve, 1, n_ffn2 + A, 3, KD - 1)
                    add_output(dve, 1, KD - 1)
                    dve_ln(dve, 1, g2, b2, 16)

                @block.gpsimd
                def _(pool):
                    los(pool, 3, n_out2 + 2)
                    pool_hgrn(pool)
                    los(pool, n_out2 + 2, n_ffn2 + 2)
                    pool_ln(pool, 0, b1)
                    pool_ffn(pool, n_ffn2)
                    pool_ln(pool, 1, b2)
                    lo(pool, n_next2 + 2)

            with nc.Block() as block:
                start_layer(block)

        with nc.Block() as block:
            @block.sync
            def _(sp):
                sp.dma_start(t["out"], xT[:, :, :]).then_inc(io, 16)
                sp.wait_ge(io, 16)


def alibi(n):
    return 2.0 ** (-8.0 * np.arange(1, n + 1, dtype=np.float32) / np.float32(n))


def constants():
    p = np.arange(P)[:, None]
    c = np.arange(S)[None, :]
    dist = p + (S - P) - c
    count = (dist <= 128).astype(np.int64) + (dist % 4 == 0) + (dist % 16 == 0)
    mult = np.where((dist >= 0) & (count > 0), count, 1)
    dil = [np.where((dist >= 0) & (count > 0), sl * dist - np.log(mult), BIG) for sl in alibi(DIL)]
    dif = [np.where(dist >= 0, sl * dist, BIG) for sl in alibi(DIFF)]
    table1 = np.stack(dil + dif, 1).reshape(P, -1).astype(np.float32)
    j, k = np.arange(P)[:, None], np.arange(P)[None, :]
    mats = np.zeros((7, P, P), np.float32)
    mats[0] = -1.0
    mats[1] = 1.0 / D
    mats[2] = (j // DH == k // DH) / DH
    mats[3] = -1.0 * (j >= k)
    mats[4] = np.eye(P)
    mats[5] = j > k
    mats[6] = np.where(j >= k, -BIG, 0.0)
    return table1, np.ascontiguousarray(mats.transpose(1, 0, 2))


def columns(w):
    k, n = w.shape
    return w.reshape(k // P, P, n // P, P).transpose(2, 1, 0, 3).reshape(n // P, P, k)


def rows(w, width, per):
    k, n = w.shape
    return w.reshape(k // P // per, per, P, width).transpose(0, 2, 1, 3).reshape(-1, P, per * width)


def parts(v, counts, w):
    out = np.zeros((len(counts), P, WIDE), v.dtype)
    k = 0
    for i, c in enumerate(counts):
        out[i, :, 0:c * w] = v[k:k + c].transpose(1, 0, 2).reshape(P, c * w)
        k += c
    return out


def down(w):
    return np.concatenate([parts(w[:, m * P:(m + 1) * P].reshape(KF, P, P), DOWN, P) for m in range(KD)])


def gate_up(g, u):
    return np.stack([columns(g), columns(u)], 1).reshape(2 * KF, P, WIDE)


def by_partition(v):
    return v.reshape(-1, KD, P).transpose(2, 0, 1).reshape(P, -1)


def laid_out(x, norm_gains, w_ffn_gate, w_ffn_up, w_ffn_down, w_in, w_out, diff_lambda, diff_subln_gain, **second):
    a = {}
    a["xT"] = x[0].T.reshape(KD, P, S).transpose(1, 0, 2)
    a["table1"], a["mats"] = constants()
    w8, w11 = [], []
    for l in range(DEPTH):
        c = np.cumsum([0, 384, 384, 384, 256, 256, 256, 384, 384, 384])
        part = [w_in[l][:, c[i]:c[i + 1]] for i in range(9)]
        qk = np.concatenate([part[i] for i in (0, 1, 3, 4, 6, 7)], 1)
        v = np.concatenate([part[i] for i in (2, 5, 8)], 1)
        w8 += [gate_up(w_ffn_gate[l, 0], w_ffn_up[l, 0]), columns(qk), rows(v[:, :512], 512, 2),
               rows(v[:, 512:], 512, 2), columns(w_out[l]), gate_up(w_ffn_gate[l, 1], w_ffn_up[l, 1])]
        w11 += [down(w_ffn_down[l, 0]), down(w_ffn_down[l, 1])]
    a["w8_1"] = np.concatenate(w8).reshape(DEPTH, -1, P, WIDE)
    a["down_1"] = np.concatenate(w11).reshape(DEPTH, -1, P, WIDE)
    a["gfirst"] = by_partition(norm_gains[0, 0])
    a["gnext"] = np.stack([by_partition(norm_gains[l, 0]) for l in range(1, DEPTH)] + [np.ones((P, KD), np.float32)])
    a["gains1"] = np.stack([by_partition(norm_gains[l]) for l in range(DEPTH)])
    init = [0.8 - 0.6 * math.exp(-0.3 * l) for l in range(DEPTH)]
    lam = diff_lambda[:, [0, 2, 1, 3], :].reshape(DEPTH, 1, 128)
    tail = np.array(init, np.float32).reshape(DEPTH, 1, 1)
    a["lam"] = np.broadcast_to(np.concatenate([lam, tail], 2), (DEPTH, P, 129))
    gain = np.concatenate([diff_subln_gain] * 2, 1)[:, :, None]
    keep = np.broadcast_to(np.array([1.0 - i for i in init], np.float32).reshape(DEPTH, 1, 1), (DEPTH, P, 1))
    a["subg"] = np.concatenate([gain, keep], 2)
    laid_out_2(a, **second)
    a["first"] = a["w8_1"][0, 0:4]
    a["next_1"] = np.stack([a["w8_1"][l, 0:4] for l in range(1, DEPTH)] + [a["w8_2"][0, 0:4]])
    a["next_2"] = np.stack([a["w8_2"][l, 0:4] for l in range(1, DEPTH)] + [a["w8_2"][0, 0:4]])
    return {k: np.ascontiguousarray(v) for k, v in a.items()}


def bucket(n):
    exact = 16
    nf = np.maximum(n, 1).astype(np.float32)
    large = exact + (np.log(nf / np.float32(exact)) / np.float32(math.log(128 / exact)) * np.float32(16)).astype(np.int32)
    return np.where(n < exact, np.maximum(n, 0), np.minimum(large, 31))


def constants_2():
    x = np.arange(640)
    dist = S - 1 - x
    onehot = np.zeros((33, 640), np.float32)
    seen = dist >= 0
    onehot[bucket(dist)[seen], x[seen]] = -1.0
    onehot[32, ~seen] = BIG
    s, u = np.arange(P)[:, None], np.arange(P)[None, :]
    span, mask = np.zeros((P, 8, P), np.float32), np.zeros((P, 8, P), np.float32)
    for l in range(LEVELS):
        half = (P // 2) >> l
        mid = u // (2 * half) * (2 * half) + half
        right = u >= mid
        span[:, l] = np.where(right, (s >= mid) & (s <= u), (s > u) & (s < mid))
        mask[:, l] = right & (s // (2 * half) == u // (2 * half)) & (s < mid)
    span[:, 7] = s <= u
    mask[:, 7] = s == u
    return onehot, np.concatenate([span.reshape(P, -1), mask.reshape(P, -1)], 1)


def laid_out_2(a, w_in_2, hg_lb_param_2, hg_norm_w_2, cmp_pos_k_2, cmp_w1_k_2, cmp_w2_k_2, cmp_pos_v_2,
               cmp_w1_v_2, cmp_w2_v_2, rel_bias_2, w_out_2, ln1_g_2, ln1_b_2, w_ffn_gate_2,
               w_ffn_up_2, w_ffn_down_2, ln2_g_2, ln2_b_2):
    a["onehot"], a["table2"] = constants_2()
    a["rel_bias"] = rel_bias_2
    a["flip"] = np.eye(P, dtype=np.float32)[::-1]
    a["one8"] = np.ones((1, NSA), np.float32)
    a["valid"] = (np.arange(P) >= CMP_END).astype(np.float32)[:, None]
    w8, w11, vg, w1, par = [], [], [], {"k": [], "v": []}, []
    ln = []
    order = [h * DH + g * 4 * DH + d for h in range(4) for g in range(2) for d in range(DH)]
    for l in range(DEPTH):
        c = np.cumsum([0, 512, 512, 512, 512, 512] + [128] * 6 + [24])
        hq, hf, hi, hg, nq, kc, vc, ks, vs, kw, vw, gt = (w_in_2[l][:, c[i]:c[i + 1]] for i in range(12))
        turned = np.concatenate([hq, hg, nq[:, order]], 1)
        w8 += [columns(np.concatenate([kc, vc, ks, kw], 1)), rows(hf, 512, 2), columns(turned),
               rows(hi, 512, 2), columns(w_out_2[l]),
               gate_up(w_ffn_gate_2[l], w_ffn_up_2[l])]
        vg.append(parts(np.concatenate([vs, vw, gt], 1).reshape(KD, P, VG), VG_ROWS, VG))
        w11.append(down(w_ffn_down_2[l]))
        for kind, w in (("k", cmp_w1_k_2), ("v", cmp_w1_v_2)):
            w1[kind].append(w[l].reshape(16, 2, DH, P).transpose(1, 2, 0, 3).reshape(P, -1))
        pos = [np.concatenate([p[l].T] * 2, 0) for p in (cmp_pos_k_2, cmp_pos_v_2)]
        par.append(np.concatenate(pos + [cmp_w2_k_2[l], cmp_w2_v_2[l], hg_norm_w_2[l][:, None]], 1))
        ln.append(np.concatenate([by_partition(v[l]) for v in (ln1_g_2, ln1_b_2, ln2_g_2, ln2_b_2)], 1))
    a["w8_2"] = np.concatenate(w8).reshape(DEPTH, -1, P, WIDE)
    a["down_2"] = np.concatenate(w11).reshape(DEPTH, -1, P, WIDE)
    a["vg_2"] = np.stack(vg)
    a["w1k"], a["w1v"] = np.stack(w1["k"]), np.stack(w1["v"])
    a["par2"], a["ln2"] = np.stack(par), np.stack(ln)
    a["flags"] = np.broadcast_to(np.array([[[0, 0, -BIG, 0]], [[1, -1, 0, 0]]], np.float32), (DEPTH, P, 4))
    a["lbp"] = np.broadcast_to(hg_lb_param_2.reshape(1, 1, DEPTH * 512), (DEPTH, P, DEPTH * 512))


def kernel(**inputs):
    import concourse.bacc as bacc
    from concourse.bass_utils import run_bass_kernel_spmd

    arrays = laid_out(**{k: np.asarray(v) for k, v in inputs.items()})
    nc = bacc.Bacc("TRN2", target_bir_lowering=False, num_devices=1)
    t = {k: nc.dram_tensor("in_" + k, v.shape, mybir.dt.from_np(v.dtype), kind="ExternalInput").ap()
         for k, v in arrays.items()}
    t["spread"] = nc.dram_tensor("spread", (NSA, 640), F32).ap()
    t["bias"] = nc.dram_tensor("bias", (P, NSA, S), F32).ap()
    t["out"] = nc.dram_tensor("out", (P, KD, S), F32, kind="ExternalOutput").ap()
    build(nc, t)
    r = run_bass_kernel_spmd(nc, [{"in_" + k: v for k, v in arrays.items()}], core_ids=[0])
    out = r.results[0]["out"]
    return np.ascontiguousarray(out.transpose(1, 0, 2).reshape(D, S).T)[None]
```
